# Optimizing a Trainium2 kernel written in Bass

```python
import math, functools
import jax, jax.numpy as jnp
from jax import lax
import numpy as np

D_MODEL = 1024
BATCH = 1
SEQ = 512
DEPTH = 1
DEC_BATCH = 8
DEC_SEQ = 8
PAST_LEN = 256
PAGE_SIZE = 128

D_A = 512
CONV_W = 31
N_HEADS = 8
N_KV = 2
GROUP = N_HEADS // N_KV
HEAD_DIM = 64
D_ATT = N_HEADS * HEAD_DIM
N_IDX_HEADS = 4
D_IDX = 64
TOPK_MAX = 256
N_BUCKETS = 32
MAX_DIST = 128
Q_BLOCK = 128
D_C = 512
N_CGROUPS = 8
CHUNK = 128
N_EXPERTS = 16
N_GROUPS = 4
EXPERTS_PER_GROUP = N_EXPERTS // N_GROUPS
TOP_K_EXPERTS = 2
D_EXPERT = 512
ALPHA = (2 * DEPTH) ** 0.25
BETA = (8 * DEPTH) ** -0.25
LN_EPS = 1e-5

SPLIT_SIZES = [2 * D_A, D_ATT, N_KV * HEAD_DIM, N_KV * HEAD_DIM, N_IDX_HEADS * D_IDX, D_IDX, N_IDX_HEADS, 2 * D_C, 3 * D_MODEL]
SPLIT_OFFSETS = [int(o) for o in np.cumsum(SPLIT_SIZES)[:-1]]
D_IN = int(sum(SPLIT_SIZES))

kernel_name = "hybrid_conv_dsa_gmlp_moe_step"

def layer_norm(x, g, b):
    xf = x.astype(jnp.float32)
    mu = jnp.mean(xf, axis=-1, keepdims=True)
    var = jnp.mean(jnp.square(xf - mu), axis=-1, keepdims=True)
    return ((xf - mu) * lax.rsqrt(var + LN_EPS)).astype(x.dtype) * g + b

def t5_bucket(rel):
    n = jnp.maximum(-rel, 0)
    max_exact = N_BUCKETS // 2
    nf = jnp.maximum(n, 1).astype(jnp.float32)
    large = max_exact + (jnp.log(nf / max_exact) / math.log(MAX_DIST / max_exact) * (N_BUCKETS - max_exact)).astype(jnp.int32)
    large = jnp.minimum(large, N_BUCKETS - 1)
    return jnp.where(n < max_exact, n, large)

def conformer_conv(a_glu, conv_buf, conv_k, conv_b, ln_g, ln_b):
    a, a_gate = jnp.split(a_glu, 2, axis=-1)
    a = a * jax.nn.sigmoid(a_gate)
    ext = jnp.concatenate([conv_buf.astype(a.dtype), a], axis=1)
    y = lax.conv_general_dilated(ext, conv_k[:, None, :].astype(a.dtype), window_strides=(1,), padding='VALID',
                                 dimension_numbers=('NWC', 'WIO', 'NWC'), feature_group_count=D_A) + conv_b
    y = jax.nn.silu(layer_norm(y, ln_g, ln_b))
    return y, ext[:, -(CONV_W - 1):]

def select_and_attend(qb, qib, wib, qpos, ki_all, kpos, gather_kv, rel_table, topk):
    B, Q = qb.shape[:2]
    qib = qib.reshape(B, Q, N_IDX_HEADS, D_IDX)
    dots = jnp.einsum('bqhd,bsd->bqhs', qib, ki_all).astype(jnp.float32)
    score = jnp.einsum('bqh,bqhs->bqs', wib.astype(jnp.float32), jax.nn.relu(dots))
    admissible = kpos[None, None, :] <= qpos[None, :, None]
    score = jnp.where(admissible, score, -jnp.inf)
    _, idx = lax.top_k(score, topk)
    valid = idx <= qpos[None, :, None]
    ks, vs = gather_kv(idx)
    qg = qb.reshape(B, Q, N_KV, GROUP, HEAD_DIM)
    logits = jnp.einsum('bqngd,bqknd->bqngk', qg, ks).astype(jnp.float32) * (HEAD_DIM ** -0.5)
    bias = rel_table[t5_bucket(idx - qpos[None, :, None])]
    bias = bias.reshape(B, Q, topk, N_KV, GROUP).transpose(0, 1, 3, 4, 2).astype(jnp.float32)
    logits = jnp.where(valid[:, :, None, None, :], logits + bias, -jnp.inf)
    p = jax.nn.softmax(logits, axis=-1).astype(vs.dtype)
    o = jnp.einsum('bqngk,bqknd->bqngd', p, vs)
    return o.reshape(B, Q, D_ATT)

def dsa_prompt(q, k, v, qi, ki, wi, rel_table):
    B, T = q.shape[:2]
    topk = min(TOPK_MAX, T // 4)
    kpos = jnp.arange(T)

    def gather_kv(idx):
        take = jax.vmap(lambda rows, i: rows[i])
        return take(k, idx), take(v, idx)

    def block(start):
        qb = lax.dynamic_slice_in_dim(q, start, Q_BLOCK, axis=1)
        qib = lax.dynamic_slice_in_dim(qi, start, Q_BLOCK, axis=1)
        wib = lax.dynamic_slice_in_dim(wi, start, Q_BLOCK, axis=1)
        qpos = start + jnp.arange(Q_BLOCK)
        return select_and_attend(qb, qib, wib, qpos, ki, kpos, gather_kv, rel_table, topk)

    out = lax.map(block, jnp.arange(T // Q_BLOCK) * Q_BLOCK)
    return jnp.moveaxis(out, 0, 1).reshape(B, T, D_ATT)

def dsa_sample(q, k, v, qi, ki, wi, cache_k_l, cache_v_l, cache_ki_l, page_table, rel_table):
    B, T = q.shape[:2]
    P = page_table.shape[1] * PAGE_SIZE
    L = P + T
    topk = min(TOPK_MAX, L // 4)
    ki_past = cache_ki_l[page_table].reshape(B, P, D_IDX)
    ki_all = jnp.concatenate([ki_past.astype(ki.dtype), ki], axis=1)
    kpos = jnp.arange(L)
    qpos = P + jnp.arange(T)
    take = jax.vmap(lambda rows, i: rows[i])

    def gather_kv(idx):
        in_past = (idx < P)[..., None, None]
        pidx = jnp.minimum(idx, P - 1)
        phys = take(page_table, pidx // PAGE_SIZE)
        off = pidx % PAGE_SIZE
        nidx = jnp.clip(idx - P, 0, T - 1)
        ks = jnp.where(in_past, cache_k_l[phys, off].astype(k.dtype), take(k, nidx))
        vs = jnp.where(in_past, cache_v_l[phys, off].astype(v.dtype), take(v, nidx))
        return ks, vs

    return select_and_attend(q, qi, wi, qpos, ki_all, kpos, gather_kv, rel_table, topk)

def chunk_sgu(uv, ln_g, ln_b, w_s, b_s, rows):
    B, T = uv.shape[:2]
    u, vv = jnp.split(uv, 2, axis=-1)
    vv = layer_norm(vv, ln_g, ln_b)
    mask = jnp.tril(jnp.ones((rows, rows), dtype=bool))
    ws = jnp.where(mask, w_s[:, :rows, :rows], 0).astype(vv.dtype)
    vc = vv.reshape(B, T // rows, rows, N_CGROUPS, D_C // N_CGROUPS)
    mixed = jnp.einsum('gts,bcsgd->bctgd', ws, vc) + b_s[:, :rows].T[None, None, :, :, None]
    return u * mixed.reshape(B, T, D_C), vv

def moe(h, w_router, router_bias, w_e_gate, w_e_up, w_e_down):
    B, T, D = h.shape
    scores = jax.nn.sigmoid(jnp.einsum('btd,de->bte', h, w_router).astype(jnp.float32))
    sel = scores + router_bias.astype(jnp.float32)
    grp_score = lax.top_k(sel.reshape(B, T, N_GROUPS, EXPERTS_PER_GROUP), 2)[0].sum(-1)
    best = jnp.argmax(grp_score, axis=-1)
    in_group = (jnp.arange(N_EXPERTS)[None, None, :] // EXPERTS_PER_GROUP) == best[..., None]
    _, top_idx = lax.top_k(jnp.where(in_group, sel, -jnp.inf), TOP_K_EXPERTS)
    top_w = jnp.take_along_axis(scores, top_idx, axis=-1)
    top_w = top_w / jnp.sum(top_w, axis=-1, keepdims=True)
    gate = jnp.sum(jax.nn.one_hot(top_idx, N_EXPERTS, dtype=jnp.float32) * top_w[..., None], axis=-2).astype(h.dtype)
    y = jnp.zeros_like(h)
    for e in range(N_EXPERTS):
        he = jax.nn.silu(h @ w_e_gate[e]) * (h @ w_e_up[e])
        y = y + gate[..., e:e + 1] * (he @ w_e_down[e])
    return y

def trunk_layer(x, c, conv_buf, attend, chunk_rows, w_ada, b_ada, w_in, b_in, conv_k, conv_b, lnA_g, lnA_b,
                lnC_g, lnC_b, w_s, b_s, w_pa, w_pb, w_pc, w_o, ln1_g, ln1_b, ln2_g, ln2_b,
                w_router, router_bias, w_e_gate, w_e_up, w_e_down):
    B, T = x.shape[:2]
    mod = jnp.einsum('bd,de->be', jax.nn.silu(c), w_ada) + b_ada
    sh1, sc1, g1, sh2, sc2, g2 = [m[:, None, :] for m in jnp.split(mod, 6, axis=-1)]
    h = x * (1 + sc1) + sh1
    z = jnp.einsum('btd,de->bte', h, w_in) + b_in
    a_glu, q, k, v, qi, ki, wi, uv, gate_logits = jnp.split(z, SPLIT_OFFSETS, axis=-1)
    y_a, conv_state = conformer_conv(a_glu, conv_buf, conv_k, conv_b, lnA_g, lnA_b)
    k = k.reshape(B, T, N_KV, HEAD_DIM)
    v = v.reshape(B, T, N_KV, HEAD_DIM)
    y_b = attend(q, k, v, qi, ki, wi)
    y_c, v_chunk = chunk_sgu(uv, lnC_g, lnC_b, w_s, b_s, chunk_rows)
    g_a, g_b, g_c = jnp.split(jax.nn.sigmoid(gate_logits), 3, axis=-1)
    merged = g_a * (y_a @ w_pa) + g_b * (y_b @ w_pb) + g_c * (y_c @ w_pc)
    x = layer_norm(ALPHA * x + (1 + g1) * (merged @ w_o), ln1_g, ln1_b)
    h2 = x * (1 + sc2) + sh2
    x = layer_norm(ALPHA * x + (1 + g2) * moe(h2, w_router, router_bias, w_e_gate, w_e_up, w_e_down), ln2_g, ln2_b)
    return x, k, v, ki, conv_state, v_chunk

def setup_inputs(seed: int = 0) -> dict:
    key = jax.random.key(seed)
    ks = jax.random.split(key, 40)
    f = jnp.float32

    def nrm(k, shape, scale):
        return jax.random.normal(k, shape, f) * scale

    n_pages = PAST_LEN // PAGE_SIZE
    n_used = DEC_BATCH * n_pages
    n_pool = n_used + max(1, n_used // 4)
    page_table = jax.random.permutation(ks[0], n_pool)[:n_used].reshape(DEC_BATCH, n_pages).astype(jnp.int32)
    return {
        "x_prompt": nrm(ks[1], (BATCH, SEQ, D_MODEL), 1.0),
        "x_sample": nrm(ks[2], (DEC_BATCH, DEC_SEQ, D_MODEL), 1.0),
        "cache_k": nrm(ks[3], (DEPTH, n_pool, PAGE_SIZE, N_KV, HEAD_DIM), 1.0),
        "cache_v": nrm(ks[4], (DEPTH, n_pool, PAGE_SIZE, N_KV, HEAD_DIM), 1.0),
        "cache_kidx": nrm(ks[5], (DEPTH, n_pool, PAGE_SIZE, D_IDX), 1.0),
        "state_conv": nrm(ks[6], (DEPTH, DEC_BATCH, CONV_W - 1, D_A), 0.5),
        "page_table": page_table,
        "c_prompt": nrm(ks[7], (BATCH, D_MODEL), 1.0),
        "c_sample": nrm(ks[8], (DEC_BATCH, D_MODEL), 1.0),
        "w_ada": nrm(ks[9], (DEPTH, D_MODEL, 6 * D_MODEL), 0.1 * D_MODEL ** -0.5),
        "b_ada": nrm(ks[10], (DEPTH, 6 * D_MODEL), 0.02),
        "w_in": nrm(ks[11], (DEPTH, D_MODEL, D_IN), D_MODEL ** -0.5),
        "b_in": nrm(ks[12], (DEPTH, D_IN), 0.02),
        "conv_k": nrm(ks[13], (DEPTH, CONV_W, D_A), CONV_W ** -0.5),
        "conv_b": nrm(ks[14], (DEPTH, D_A), 0.02),
        "lnA_g": 1.0 + nrm(ks[15], (DEPTH, D_A), 0.05),
        "lnA_b": nrm(ks[16], (DEPTH, D_A), 0.02),
        "lnC_g": 1.0 + nrm(ks[17], (DEPTH, D_C), 0.05),
        "lnC_b": nrm(ks[18], (DEPTH, D_C), 0.02),
        "w_s": nrm(ks[19], (DEPTH, N_CGROUPS, CHUNK, CHUNK), CHUNK ** -0.5),
        "b_s": 1.0 + nrm(ks[20], (DEPTH, N_CGROUPS, CHUNK), 0.05),
        "w_pa": nrm(ks[21], (DEPTH, D_A, D_MODEL), BETA * D_A ** -0.5),
        "w_pb": nrm(ks[22], (DEPTH, D_ATT, D_MODEL), BETA * D_ATT ** -0.5),
        "w_pc": nrm(ks[23], (DEPTH, D_C, D_MODEL), BETA * D_C ** -0.5),
        "w_o": nrm(ks[24], (DEPTH, D_MODEL, D_MODEL), BETA * D_MODEL ** -0.5),
        "ln1_g": 1.0 + nrm(ks[25], (DEPTH, D_MODEL), 0.05),
        "ln1_b": nrm(ks[26], (DEPTH, D_MODEL), 0.02),
        "ln2_g": 1.0 + nrm(ks[27], (DEPTH, D_MODEL), 0.05),
        "ln2_b": nrm(ks[28], (DEPTH, D_MODEL), 0.02),
        "rel_table": nrm(ks[29], (N_BUCKETS, N_HEADS), 0.5),
        "w_router": nrm(ks[30], (D_MODEL, N_EXPERTS), D_MODEL ** -0.5),
        "router_bias": nrm(ks[31], (N_EXPERTS,), 0.01),
        "w_e_gate": nrm(ks[32], (DEPTH, N_EXPERTS, D_MODEL, D_EXPERT), D_MODEL ** -0.5),
        "w_e_up": nrm(ks[33], (DEPTH, N_EXPERTS, D_MODEL, D_EXPERT), D_MODEL ** -0.5),
        "w_e_down": nrm(ks[34], (DEPTH, N_EXPERTS, D_EXPERT, D_MODEL), BETA * D_EXPERT ** -0.5),
    }

def reference(x_prompt, x_sample, cache_k, cache_v, cache_kidx, state_conv, page_table, c_prompt, c_sample,
              w_ada, b_ada, w_in, b_in, conv_k, conv_b, lnA_g, lnA_b, lnC_g, lnC_b, w_s, b_s,
              w_pa, w_pb, w_pc, w_o, ln1_g, ln1_b, ln2_g, ln2_b, rel_table, w_router, router_bias,
              w_e_gate, w_e_up, w_e_down):
    yp, ys = x_prompt, x_sample
    kp, vp, kip, cp = [], [], [], []
    ks_, vs_, kis, cs, vcs = [], [], [], [], []
    attend_p = functools.partial(dsa_prompt, rel_table=rel_table)
    for l in range(DEPTH):
        lp = (w_ada[l], b_ada[l], w_in[l], b_in[l], conv_k[l], conv_b[l], lnA_g[l], lnA_b[l], lnC_g[l], lnC_b[l],
              w_s[l], b_s[l], w_pa[l], w_pb[l], w_pc[l], w_o[l], ln1_g[l], ln1_b[l], ln2_g[l], ln2_b[l],
              w_router, router_bias, w_e_gate[l], w_e_up[l], w_e_down[l])
        buf0 = jnp.zeros((yp.shape[0], CONV_W - 1, D_A), yp.dtype)
        yp, k_l, v_l, ki_l, conv_l, _ = trunk_layer(yp, c_prompt, buf0, attend_p, CHUNK, *lp)
        kp.append(k_l); vp.append(v_l); kip.append(ki_l); cp.append(conv_l)
        attend_s = functools.partial(dsa_sample, cache_k_l=cache_k[l], cache_v_l=cache_v[l], cache_ki_l=cache_kidx[l],
                                     page_table=page_table, rel_table=rel_table)
        ys, k_s, v_s, ki_s, conv_s, vc_s = trunk_layer(ys, c_sample, state_conv[l], attend_s, ys.shape[1], *lp)
        ks_.append(k_s); vs_.append(v_s); kis.append(ki_s); cs.append(conv_s); vcs.append(vc_s)
    new_k_prompt = jnp.stack(kp)
    new_v_prompt = jnp.stack(vp)
    new_kidx_prompt = jnp.stack(kip)
    new_conv_prompt = jnp.stack(cp)
    new_k_sample = jnp.stack(ks_)
    new_v_sample = jnp.stack(vs_)
    new_kidx_sample = jnp.stack(kis)
    new_conv_sample = jnp.stack(cs)
    new_vchunk_sample = jnp.stack(vcs)
    return (yp, ys, new_k_prompt, new_v_prompt, new_kidx_prompt, new_conv_prompt,
            new_k_sample, new_v_sample, new_kidx_sample, new_conv_sample, new_vchunk_sample)


_drawn_inputs = setup_inputs


def setup_inputs(seed=0):
    import zlib

    import numpy as np

    out = dict(_drawn_inputs(seed))
    spreads = {}
    factors = {'conv_b': 8.0, 'lnA_b': 8.0, 'lnC_b': 2.996, 'ln2_b': 2.742, 'lnA_g': 3.975}
    for name, (base, spread) in spreads.items():
        noise = np.random.default_rng([zlib.crc32(name.encode()), seed]).standard_normal(out[name].shape)
        drawn = base * np.exp(spread * noise) if base else spread * noise
        out[name] = __import__('jax').numpy.asarray(drawn.astype(out[name].dtype))
    for name, factor in factors.items():
        out[name] = (out[name] * factor).astype(out[name].dtype)
    return out
```

```python
import math
from contextlib import ExitStack

import numpy as np
import concourse.bass as bass
from concourse import mybir

F32 = mybir.dt.float32
I32 = mybir.dt.int32
ALU = mybir.AluOpType
ACT = mybir.ActivationFunctionType
AX = mybir.AxisListType

P = 128
D = 1024
KT = D // P
SEQ, NB, ST = 512, 8, 8
NS = NB * ST
NTOK = SEQ + NS
NT = 5
HALF = NTOK // 2
PAST, PAGE, NPOOL = 256, 128, 20
NPG = PAST // PAGE
DA, CW = 512, 31
NJ = DA // P
NKV, HD, NC = 2, 64, 4
NBUCK, MAXD = 32, 128
NCG, CHUNK = 8, 128
NE, NG, DE = 16, 4, 512
TOPK_P, TOPK_S = 128, 66
ALPHA = 2.0 ** 0.25
EPS = 1e-5
SLEN = 640
TABLE_END = 511
NEG, REPL, SELD = -1e30, -3e38, -2e38
BIG = 1e30
TS = 128
TO = 64
MORE = (NTOK - TS) // TO
NOV = 16
FAR_ROWS = NE * TS
SLOTS = FAR_ROWS + NOV * TO
FAR = 65536.0

C_A, C_AG, C_Q, C_K, C_V, C_QI, C_KI, C_WI, C_U, C_VV, C_G = 0, 512, 1024, 1536, 1664, 1792, 2048, 2112, 2116, 2628, 3140
D_IN = 6212
NW = 132

R_A, R_Q, R_K, R_QI, R_KI, R_G, R_CB, R_LG, R_LB, R_BS, NR = 0, 8, 12, 13, 15, 16, 40, 44, 48, 52, 60

K_ID, K_PEN, K_TRI, K_ONE, K_PENS, K_E8, K_BLK, K_SLOT, K_TOK, K_STEP, K_N = 0, 128, 256, 384, 512, 576, 704, 712, 728, 736, 752

K_ALL = K_N + NE * NE + MORE

SLOT = 4096
A_CON = 0
A_RING = K_N
A_MG = A_RING + 3 * SLOT
A_HT = A_MG + 8 * NTOK
A_YA = A_HT + KT * 640
A_YB = A_YA + NJ * NTOK
A_YC = A_YB + NJ * NTOK
A_W = A_YC + NJ * NTOK
A_AE = A_W + KT * NW
EXT = 30 + SEQ + NB * (30 + ST)
A_UN = A_AE + NJ * EXT
A_VN = A_UN + NT * 512
A_QK = A_VN + NT * 512
A_WS = A_QK + 8 * NTOK
A_BD = A_WS + NCG * P
A_VA = A_BD + NCG * NS
A_PAR = A_VA + NT * P
A_CK = A_PAR + 2 * NR
A_MT = A_CK + NJ * CW
A_CT = A_MT + 16 * 9
A_SC = A_CT + KT * 9
A_PEN = A_SC + 512
A_BM = A_PEN + 256 + 384 + 512 + 320
A_LP = A_BM + 1024
A_PT = A_LP + 1024
A_GT = A_PT + 1024
A_SM = A_GT + 4 * HALF + 40
A_END = A_SM + 290
A_X = A_UN
A_WSN = A_MG
A_STN = A_WSN + 1024
A_CN = A_STN + 1024
A_CKN = A_CN + 1024
A_PRN = A_CKN + 512
A_TAB = A_BM
A_OH = A_LP
A_REL = A_PRN + 128
A_MOD = A_YC
A_BB = A_YB
A_KP = A_AE
A_KTS = A_KP + 16 * P
A_QM = A_KTS + NB * PAST
A_VP = A_QM + 2 * (NB * P + P)
A_RING2 = A_HT
A_BC = A_AE
A_X1 = A_BC + 8 * D
A_XR = A_X1 + NT * D
A_R = A_XR + 2 * D
A_H2 = A_R + 2 * D
A_H2T = A_H2 + 2 * D
A_RO = A_H2T + D
assert A_VP + 16 * P <= A_QK and A_RING2 + 3 * SLOT <= A_AE and A_RO + 1247 + NE * NE + MORE <= A_SM and A_OH + SLEN <= A_PT
A_G = A_BC
A_HG = A_G + 2 * D
A_HE = A_HG + 2 * D
A_HET = A_HE + 2 * DE
A_Y = A_HET + 2 * DE
A_GA = A_MG
A_BC2 = A_XR
A_O = A_H2


def fm_groups():
    return [(n, j) for j in range(NJ) for n in ("ag", "a")], \
           [("q", c) for c in range(NC)] + [("k", 0), ("ki", 0), ("qi", 0), ("qi", 1)]


def make_plan():
    plan = [("par",), ("ck",), ("ws", 0), ("ws", 1), ("bd",), ("st", 0), ("st", 1), ("oh", 0), ("oh", 1), ("cT",)]
    for n in range(4):
        plan += [("ada", n)]
        if n:
            plan += [("mT", n - 1)]
    plan += [("mT", 3)]
    plan += [("xT", f) for f in range(KT)] + [("xTs",)]
    ga, gq = fm_groups()
    for n, j in ga:
        plan += [("fm", n, j, 0), ("fm", n, j, 1)]
    for n, j in gq:
        plan += [("fm", n, j, 0), ("fm", n, j, 1)]
    side = [("kv", t) for t in range(NT)] + [("cvp",), ("cvs",)]
    for n in range(4, 12):
        plan += [("ada", n)]
        if side:
            plan += [side.pop(0)]
    plan += side
    for t in range(NT):
        plan += [("nat", "w", t)]
    for t in range(NT):
        plan += [("nat", "v", t), ("lnA1", t)]
        if t:
            plan += [("lnA2", t - 1)]
    plan += [("nat", "u", 0), ("lnA2", 4), ("nat", "u", 1)]
    plan += [("mix", 0), ("nat", "u", 2), ("mix", 1), ("yc", 0), ("nat", "u", 3), ("mix", 2), ("yc", 1), ("nat", "u", 4)]
    plan += [("mix", 3), ("yc", 2)]
    units = [(i, c) for i in range(4) for c in range(NC)]
    sides = {n: [] for n in range(48)}
    sides[0] += [("mix", 4), ("yc", 3)]
    sides[1] += [("yc", 4), ("dots", 1, 0), ("dots", 1, 1)]
    sides[2] += [("dots", 1, 2), ("dots", 1, 3)]
    sides[4] += [("dots", 2, 0), ("dots", 2, 1)]
    sides[5] += [("dots", 2, 2), ("dots", 2, 3)]
    sides[8] += [("dots", 3, 0), ("dots", 3, 1)]
    sides[9] += [("dots", 3, 2), ("dots", 3, 3)]
    at = 12
    for n, (i, c) in enumerate(units):
        sides[at + n] += [("lg", i, c)]
        sides[at + n + 1] += [("pt", i, c)]
        sides[at + n + 2] += [("pv", i, c)]
    return plan, sides


def full_plan():
    plan, sides = make_plan()
    n = 0
    for x in "AC":
        for f in range(KT):
            for h in range(2):
                plan += [("gate", x, f, h), ("proj", x, f, h)] + sides[n]
                n += 1
    plan += [("kit", g) for g in range(4)]
    plan += [("dots", "s", h) for h in range(4)]
    plan += [("kts", g) for g in range(4)]
    for c in range(NC):
        plan += [("lg", "s", c)]
        if c:
            plan += [("pt", "s", c - 1), ("pv", "s", c - 1)]
    plan += [("pt", "s", NC - 1), ("pv", "s", NC - 1)]
    for f in range(KT):
        for h in range(2):
            plan += [("gate", "B", f, h), ("proj", "B", f, h)]
    for t in range(NT):
        plan += [("wo", t, 0), ("wo", t, 1)]
        if t:
            plan += [("h2T", t - 1, 0), ("h2T", t - 1, 1), ("rt", t - 1)]
    plan += [("h2T", 4, 0), ("h2T", 4, 1), ("rt", 4), ("cum",), ("lst",)]
    return plan


def load_plan():
    w = [("ada", n) for n in range(4)] + [("a", 0), ("a", 1), ("q",), ("k",)] + [("ada", n) for n in range(4, 12)]
    w += [("v",), ("u",)]
    for x in "ACB":
        w += [("g", x, 0), ("p", x), ("g", x, 1)]
    return w + [("wo", 0), ("wo", 1)]


class Banks:

    def __init__(self, tiles, keys, full, free):
        self.tiles, self.full_sem, self.free_sems = tiles, full, free
        self.at = {k: n for n, k in enumerate(keys)}

    def tile(self, key):
        return self.tiles[self.at[key] % len(self.tiles)]

    def old(self, key):
        return self.at[key] >= len(self.tiles)

    def room(self, key):
        n, b = self.at[key], len(self.tiles)
        return self.free_sems[n % b], n // b

    def full(self, key):
        return self.full_sem, self.at[key] + 1

    def free(self, key):
        return self.free_sems[self.at[key] % len(self.tiles)]

    def taken(self, key):
        n, b = self.at[key], len(self.tiles)
        return self.free_sems[n % b], n // b + 1


class Steps:

    def __init__(self, eng, sem):
        self.eng, self.sem, self.n = eng, sem, 0

    def done(self, ins):
        ins.then_inc(self.sem, 1)
        self.n += 1
        return self.n

    def need(self, n=None):
        self.eng.wait_ge(self.sem, self.n if n is None else n)

    def link(self, ins):
        self.done(ins)
        self.need()


def build(nc, I, O, con_d, oh_d):
    tab_d = nc.dram_tensor("tables", [8, P, SLEN], F32).ap()
    mod_d = nc.dram_tensor("mod", [9, 6 * D], F32).ap()
    h2_d = nc.dram_tensor("h2", [NTOK, D], F32).ap()
    lst_d = nc.dram_tensor("slots", [SLOTS, 1], F32).ap()
    y_d = nc.dram_tensor("expert_rows", [SLOTS, D], F32).ap()
    with ExitStack() as ctx:
        build_in(nc, ctx, I, O, con_d, oh_d, tab_d, mod_d, h2_d, lst_d, y_d)


def build_in(nc, ctx, I, O, con_d, oh_d, tab_d, mod_d, h2_d, lst_d, y_d):
    arena = ctx.enter_context(nc.sbuf_tensor("arena", [P, A_END], F32))
    ints = ctx.enter_context(nc.sbuf_tensor("ints", [P, 80], I32))
    sem = lambda name: ctx.enter_context(nc.semaphore(name))

    def V(at, *dims):
        n = int(np.prod(dims))
        v = arena[:, at:at + n]
        if len(dims) == 2:
            v = v.rearrange("p (a b) -> p a b", b=dims[1])
        elif len(dims) == 3:
            v = v.rearrange("p (a b c) -> p a b c", b=dims[1], c=dims[2])
        elif len(dims) == 4:
            v = v.rearrange("p (a b c d) -> p a b c d", b=dims[1], c=dims[2], d=dims[3])
        return v

    con = V(A_CON, K_N)
    ident = con[:, K_ID:K_ID + P]
    tri = con[:, K_TRI:K_TRI + P]
    ones = con[:, K_ONE:K_ONE + P]
    ring = [V(A_RING + s * SLOT, SLOT) for s in range(3)] + [V(A_RING2 + s * SLOT, SLOT) for s in range(3)]
    MG = V(A_MG, KT, NTOK)
    HT = V(A_HT, KT, 640)
    YT = {"A": V(A_YA, NJ, NTOK), "B": V(A_YB, NJ, NTOK), "C": V(A_YC, NJ, NTOK)}
    ACC = YT["A"]
    W1 = V(A_W, KT, NW)
    TMP = V(A_W, 512)
    AE = V(A_AE, NJ, EXT)
    AES = arena[:, A_AE:A_AE + NJ * EXT].rearrange("p (j x) -> p j x", x=EXT)
    UN, VN = V(A_UN, NT, 512), V(A_VN, NT, 512)
    QT, KTT, QIT, KIT = V(A_QK, NC, NTOK), V(A_QK + 4 * NTOK, NTOK), V(A_QK + 5 * NTOK, 2, NTOK), V(A_QK + 7 * NTOK, NTOK)
    WS, BD, VA = V(A_WS, NCG, P), V(A_BD, NCG, NB, ST), V(A_VA, NT, P)
    PAR, PARH = V(A_PAR, NR), V(A_PAR + NR, NR)
    CK, MT, CT = V(A_CK, NJ, CW), V(A_MT, 16, 9), V(A_CT, KT, 9)
    SC = V(A_SC, 512)
    PEN = {0: con[:, K_PEN:K_PEN + P], 1: V(A_PEN, 256), 2: V(A_PEN + 256, 384), 3: V(A_PEN + 640, 512), "s": V(A_PEN + 1152, 320)}
    BM, LP, PTT = V(A_BM, 2, 512), V(A_LP, 2, 512), V(A_PT, 2, 512)
    GT, PJ = V(A_GT, 2, HALF), V(A_GT + 2 * HALF, 2, HALF)
    sm = lambda o, n: arena[:, A_SM + o:A_SM + o + n]
    WI, MX8, STAT, MV, RSTD, NEGM, RSUM, RINV = sm(0, 20), sm(20, 8), sm(28, 12), sm(40, 2), sm(42, 1), sm(43, 2), sm(45, 2), sm(47, 2)
    VEPS, HALFN, BS2 = sm(49, 1), sm(50, 1), sm(51, 8)
    X = V(A_X, NT, D)
    WSN, STN, CN, CKN, PRN = V(A_WSN, NCG, P), V(A_STN, 2, 512), V(A_CN, D), V(A_CKN, 512), V(A_PRN, P)
    TAB, OH, REL = V(A_TAB, SLEN), V(A_OH, SLEN), V(A_REL, 8)
    CVS = V(A_BM + 768, NJ, NS)
    MOD, BAD = V(A_MOD, 2, 512), V(A_MOD + 1024, 2, 512)
    BB = V(A_BB, 512 + 512 + NW + 1024)
    KP, VP, KTS = V(A_KP, 16, P), V(A_VP, 16, P), V(A_KTS, NB, PAST)
    QIM = V(A_QM, 2, NB, P)
    QI2 = V(A_QM + 2 * NB * P, 2, P)
    QMN = [(V(A_QM + z * 1152, NB, P), V(A_QM + z * 1152 + 1024, P)) for z in range(2)]
    BC = {n: V(A_BC + k * D, D) for k, n in enumerate(["g1p", "g1s", "scp", "scs", "shp", "shs", "lg", "lb"])}
    X1, XR, R, H2, H2T = V(A_X1, NT, D), V(A_XR, 2, D), V(A_R, 2, D), V(A_H2, 2, D), V(A_H2T, KT, P)
    r0 = A_RO
    TH, SEL, MSK, GATE = (V(r0 + k * 80, NT, NE) for k in range(4))
    PSUMS, GS, GBUF, GRES = V(r0 + 320, 20, 6), V(r0 + 440, 20), V(r0 + 460, NT, 11), V(r0 + 515, NT, 11)
    SBUF_, SRES = V(r0 + 570, NT, 22), V(r0 + 680, NT, 22)
    RB, SUM5, SA, SB_, WGA, WGB = V(r0 + 790, 16), V(r0 + 806, 5), V(r0 + 811, 5), V(r0 + 816, 5), V(r0 + 821, 5), V(r0 + 826, 5)
    SLM, EQ = V(r0 + 831, NT, NE), V(r0 + 911, NT, NE)
    WRT = V(r0 + 991, KT, NE)
    LSTN = V(r0 + 1119, P)
    CNT, OVER, BEFORE, TEXP = sm(92, 16), sm(108, 16), sm(124, 16), sm(140, 16)
    LSTO = sm(156, TO)
    RCON = V(r0 + 1247, NE * NE + MORE)
    CMP = V(A_H2T, NOV, NE)
    ZERO = V(A_MG + 4 * D, 512)
    GMK = sm(62, 20)
    GM8 = sm(84, 8)
    I_PG, I_SA, I_SB, I_L, I_NOV, I_E, I_O = 0, 16, 21, 26, 42, 44, 60
    G, HG, HE, HET, YO = V(A_G, 2, D), V(A_HG, 2, KT, P), V(A_HE, 2, DE), V(A_HET, 2, 4, P), V(A_Y, 2, D)
    GAT, BC2, OUT = V(A_GA, 4, D), V(A_BC2, 4, D), V(A_O, 2, D)

    banks = [ctx.enter_context(nc.psum_tensor(f"bank{b}", [P, 512], F32))[:, :] for b in range(8)]
    plan = full_plan()
    kinds = {"ada": "M", "fm": "M", "nat": "M", "gate": "M", "proj": "M", "wo": "M",
             "par": "T", "ck": "T", "ws": "T", "st": "T", "cT": "T", "mT": "T", "xT": "T", "xTs": "T", "kv": "T", "cvp": "T",
             "cvs": "T", "lnA1": "T", "lnA2": "T", "yc": "T", "pt": "T", "kit": "T", "kts": "T", "h2T": "T", "lst": "T",
             "bd": "A", "oh": "A", "mix": "A", "dots": "A", "lg": "A", "pv": "A", "rt": "A", "cum": "A"}

    def keys_of(kind):
        out = []
        for s in plan:
            if kinds[s[0]] != kind:
                continue
            two = s[0] == "pt" and s[1] != "s" or s[0] == "lg" and s[1] != "s"
            out += [s + (0,), s + (1,)] if two else [s]
        return out

    mm = Banks(banks[0:3], keys_of("M"), sem("mm_full"), [sem(f"mm_free{b}") for b in range(3)])
    tt = Banks(banks[3:5], keys_of("T"), sem("t_full"), [sem(f"t_free{b}") for b in range(2)])
    at = Banks(banks[5:8], keys_of("A"), sem("at_full"), [sem(f"at_free{b}") for b in range(3)])

    loads = load_plan()
    index = {k: n for n, k in enumerate(loads)}
    slot_in = [sem(f"slot_in{s}") for s in range(3)]
    slot_out = sem("slot_out")
    parts = {("q",): 8, ("k",): 4, ("p", "B"): 2}
    arrived_at, total = {}, [0, 0, 0]
    for n, k in enumerate(loads):
        total[n % 3] += 16 * parts.get(k, 1)
        arrived_at[k] = (slot_in[n % 3], total[n % 3])
    released = [k for k in loads if k[0] in ("ada", "a", "q", "k", "v", "u")]
    for x in "ACB":
        released += [("g", x, 0), ("g", x, 1), ("p", x)]
    released += [("wo", 0), ("wo", 1)]
    rel = {k: n + 1 for n, k in enumerate(released)}
    wslot = lambda k: ring[index[k] % 3]


    def quarter_tiles(bank):
        return bank.rearrange("p (k n) -> p k n", n=P)

    def positive(x):
        return type(x) is not int or x > 0

    def each_expert(eng, one):
        for e in range(3):
            one(e, e // 2, (e - 1) // 2, e % 2)
        with eng.Fori(1, NE // 2 - 1) as i:
            one(2 * i + 1, i, i, 1)
            one(2 * i + 2, i + 1, i, 0)
        one(NE - 1, NE // 2 - 1, NE // 2 - 1, 1)

    def each_further(eng, nov, one):
        with eng.If(nov > 0):
            with eng.Fori(0, NOV // 2) as i:
                for p in range(2):
                    with eng.If(nov > 2 * i + p):
                        one(2 * i + p, i, p)

    def further_hidden(p):
        return HET[:, p, 0:2, :].rearrange("p k n -> p (k n)").rearrange("p (k n) -> p k n", n=TO)

    named = {}

    def ev(name):
        if name not in named:
            named[name] = sem(name)
        return named[name]

    pos = {k: n for n, k in enumerate(plan)}
    pairs = [(x, f, h) for x in "ACB" for f in range(KT) for h in range(2)]
    pair_no = {k: n for n, k in enumerate(pairs)}
    units = [(i, c) for i in range(4) for c in range(NC)] + [("s", c) for c in range(NC)]
    unit_no = {u: n for n, u in enumerate(units)}
    glu_no = {(j, h): 2 * j + h for j in range(NJ) for h in range(2)}
    rows_of = lambda t: P if t < 4 else NS
    block = ctx.enter_context(nc.Block())

    def diagonal(at, row, rows):
        v = arena[row:row + rows, at:at + (NB - 1) * (P + ST) + ST]
        return bass.AP(v.tensor, v.offset, [list(v.ap[0]), [P + ST, NB], [1, ST]])

    def w_in_cols(a, b):
        return I["w_in"][0][:, a:b].rearrange("(k p) n -> p k n", p=P)

    def load_weights(sp, n):
        key = loads[n]
        slot, inc = ring[n % 3], slot_in[n % 3]
        if n >= 3:
            sp.wait_ge(slot_out, rel[loads[n - 3]])
        kn = slot.rearrange("p (k n) -> p k n", k=KT)
        if key[0] == "ada":
            sp.dma_start(kn, I["w_ada"][0][:, 512 * key[1]:512 * key[1] + 512].rearrange("(k p) n -> p k n", p=P)).then_inc(inc, 16)
        elif key[0] == "a":
            sp.dma_start(kn, w_in_cols(512 * key[1], 512 * key[1] + 512)).then_inc(inc, 16)
        elif key[0] == "q":
            for c in range(NC):
                for n2 in range(NKV):
                    a = C_Q + n2 * 256 + c * HD
                    sp.dma_start(kn[:, :, c * P + n2 * HD:c * P + n2 * HD + HD], w_in_cols(a, a + HD)).then_inc(inc, 16)
        elif key[0] == "k":
            sp.dma_start(kn[:, :, 0:128], w_in_cols(C_K, C_K + 128)).then_inc(inc, 16)
            sp.dma_start(kn[:, :, 128:192], w_in_cols(C_KI, C_KI + 64)).then_inc(inc, 16)
            sp.dma_start(kn[:, :, 192:256], w_in_cols(C_KI, C_KI + 64)).then_inc(inc, 16)
            sp.dma_start(kn[:, :, 256:512], w_in_cols(C_QI, C_QI + 256)).then_inc(inc, 16)
        elif key[0] in "uv":
            a = C_U if key[0] == "u" else C_VV
            sp.dma_start(kn, w_in_cols(a, a + 512)).then_inc(inc, 16)
        elif key[0] == "g":
            a = C_G + "ABC".index(key[1]) * D + 512 * key[2]
            sp.dma_start(kn, w_in_cols(a, a + 512)).then_inc(inc, 16)
        elif key[0] == "p":
            w = I["w_p" + key[1].lower()][0]
            kf = slot.rearrange("p (k n) -> p k n", k=NJ)
            if key[1] == "B":
                for n2 in range(NKV):
                    sp.dma_start(kf[n2 * HD:n2 * HD + HD], w[n2 * 256:n2 * 256 + 256, :].rearrange("(c d) f -> d c f", d=HD)).then_inc(inc, 16)
            else:
                sp.dma_start(kf, w.rearrange("(k p) n -> p k n", p=P)).then_inc(inc, 16)
        else:
            sp.dma_start(kn, I["w_o"][0][:, 512 * key[1]:512 * key[1] + 512].rearrange("(k p) n -> p k n", p=P)).then_inc(inc, 16)

    def load_bias(sp, i, c):
        u = unit_no[(i, c)]
        if u:
            sp.wait_ge(ev("logits_up"), 2 * u if u < 16 else 32 + u - 16)
        t = tab_d.tensor
        if i != "s":
            k = P * (i + 1)
            for n in range(NKV):
                src = bass.AP(t, (4 * n + c) * P * SLEN + P - 1 + 384 - P * i, [[SLEN - 1, P], [1, k]])
                sp.dma_start(BM[:, n, 0:k], src).then_inc(ev("bias_in"), 16)
        else:
            for n in range(NKV):
                rows = BM[n * NS:n * NS + NS, 0, :]
                h0 = (4 * n + c) * P * SLEN + TABLE_END
                sp.dma_start(rows[:, 0:PAST], bass.AP(t, h0 - PAST, [[0, NB], [SLEN - 1, ST], [1, PAST]])).then_inc(ev("bias_in"), 16)
                for b in range(NB):
                    sp.dma_start(rows[:, PAST + b * ST:PAST + b * ST + ST], bass.AP(t, h0, [[0, NB], [SLEN - 1, ST], [1, ST]])).then_inc(ev("bias_in"), 16)

    bias_need = {}
    total_bias = 0
    for u_ in units:
        total_bias += 32 if u_[0] != "s" else 32 + 32 * NB
        bias_need[u_] = total_bias

    last_use = {}
    for k in plan:
        if k[0] in ("ada", "wo"):
            last_use[k[:2] if k[0] == "ada" else ("wo", k[2])] = pos[k]
        elif k[0] == "fm":
            last_use[("a", 0) if k[1] in ("a", "ag") else ("q",) if k[1] == "q" else ("k",)] = pos[k]
        elif k[0] == "nat" and k[1] in "uv":
            last_use[(k[1],)] = pos[k]
        elif k[0] == "gate":
            last_use[("g", k[1], k[2] // 4)] = pos[k]
        elif k[0] == "proj":
            last_use[("p", k[1])] = pos[k]
    last_use[("a", 1)] = last_use[("a", 0)]
    assert [last_use[k] for k in released] == sorted(last_use[k] for k in released)
    sp_order = [(last_use[loads[n - 3]] if n >= 3 else -3 + n, "ring", n) for n in range(len(loads))]
    sp_order += [(pos[("lg",) + units[n - 1]] + 0.5 if n else pos[("cvs",)] + 0.5, "bias", units[n]) for n in range(len(units))]
    sp_order += [(pos[("yc", 4)] + 0.6, "pages", 0), (pos[("kit", 3)] + 0.6, "kpages", 0)]
    sp_order.sort(key=lambda x: x[0])

    def expert_weights(sp, e, z):
        name, k = [("w_e_gate", KT), ("w_e_up", KT), ("w_e_down", NJ)][z % 3]
        w = I[name][0]
        w = w[e] if type(e) is int else w[bass.ds(e, 1)].rearrange("e k n -> (e k) n")
        sp.dma_start(ring[z].rearrange("p (k n) -> p k n", k=k), w.rearrange("(k p) n -> p k n", p=P)).then_inc(ev(f"w_in{z}"), 16)

    @block.sync
    def _(sp):
        sp.dma_start(con, con_d[:, 0:K_N]).then_inc(ev("consts"), 16)
        sp.dma_start(CN[0:1, :], I["c_prompt"]).then_inc(ev("c_in"), 16)
        sp.dma_start(CN[1:9, :], I["c_sample"]).then_inc(ev("c_in"), 16)
        sp.dma_start(ints[0:1, I_PG:I_PG + 16], I["page_table"].rearrange("b g -> (b g)").unsqueeze(0)).then_inc(ev("page_ids"), 16)
        sp.dma_start(O["new_conv_sample"][0, :, 0:CW - 1 - ST, :], I["state_conv"][0, :, ST:CW - 1, :]).then_inc(ev("state_out"), 16)
        for _, what, n in sp_order:
            if what == "ring":
                if n == 3:
                    for t in range(NT):
                        src = I["x_prompt"][0, t * P:t * P + P, :] if t < 4 else I["x_sample"].rearrange("b t f -> (b t) f")
                        sp.dma_start(X[0:rows_of(t), t, :], src).then_inc(ev("x_in"), 16)
                    sp.dma_start(W1[:, :, 0:128], w_in_cols(C_V, C_V + 128)).then_inc(ev("w132_in"), 16)
                    sp.dma_start(W1[:, :, 128:132], w_in_cols(C_WI, C_WI + 4)).then_inc(ev("w132_in"), 16)
                load_weights(sp, n)
            elif what == "bias":
                if n == units[0]:
                    sp.wait_ge(ev("table_out"), 16)
                    sp.wait_ge(*tt.full(("cvs",)))
                load_bias(sp, *n)
            elif what == "pages":
                sp.wait_ge(ev("yct_up"), NT)
                sp.wait_ge(ev("vchunk_out"), 16)
                sp.wait_ge(ev("page_ids"), 16)
                with sp.Fori(0, NB * NPG) as g:
                    page = sp.value_load(ints[0:1, bass.ds(g, 1)], min_val=0, max_val=NPOOL - 1)
                    for twice in range(2):
                        sp.dma_start(arena[:, bass.ds(g * P + (A_KP + twice * HD), HD)],
                                     I["cache_kidx"][0, bass.ds(page, 1)].rearrange("a s d -> (a s) d")).then_inc(ev("pages_in"), 16)
                    sp.dma_start(arena[:, bass.ds(g * P + A_VP, P)],
                                 I["cache_v"][0, bass.ds(page, 1)].rearrange("a s n d -> (a s) (n d)")).then_inc(ev("pages_in"), 16)
            else:
                sp.wait_ge(*tt.full(("kit", 3)))
                with sp.Fori(0, NB * NPG) as g:
                    page = sp.value_load(ints[0:1, bass.ds(g, 1)], min_val=0, max_val=NPOOL - 1)
                    sp.dma_start(arena[:, bass.ds(g * P + A_KP, P)],
                                 I["cache_k"][0, bass.ds(page, 1)].rearrange("a s n d -> (a s) (n d)")).then_inc(ev("kpages_in"), 16)
        sp.wait_ge(ev("mod_out0"), 16 * 6)
        sp.wait_ge(ev("mod_out1"), 16 * 6)
        sp.wait_ge(ev("yb_up"), 20)

        def mod_rows(cols):
            return (mod_d[0:1, cols:cols + D].partition_broadcast(P),
                    bass.AP(mod_d.tensor, 6 * D + cols, [[6 * D, NB], [0, ST], [1, D]]))
        for name, cols in (("g1", 2 * D), ("sc", 4 * D), ("sh", 3 * D)):
            whole, samples = mod_rows(cols)
            sp.dma_start(BC[name + "p"], whole).then_inc(ev("rows_in"), 16)
            sp.dma_start(BC[name + "s"][0:NS], samples).then_inc(ev("rows_in"), 16)
        sp.dma_start(BC["lg"], I["ln1_g"].partition_broadcast(P)).then_inc(ev("rows_in"), 16)
        sp.dma_start(BC["lb"], I["ln1_b"].partition_broadcast(P)).then_inc(ev("rows_in"), 16)
        sp.wait_ge(ev("merged"), 48)
        sp.dma_start(WRT, I["w_router"].rearrange("(k p) e -> p k e", p=P)).then_inc(ev("router_in"), 16)
        sp.dma_start(RCON, con_d[:, K_N:K_ALL]).then_inc(ev("router_in"), 16)
        sp.dma_start(RB, I["router_bias"][0:1, :].partition_broadcast(P)).then_inc(ev("router_in"), 16)
        for t in range(NT):
            if t >= 2:
                sp.wait_ge(ev("x_added"), t - 1)
            src = I["x_prompt"][0, t * P:t * P + P, :] if t < 4 else I["x_sample"].rearrange("b t f -> (b t) f")
            sp.dma_start(XR[0:rows_of(t), t % 2, :], src).then_inc(ev(f"xr_in{t % 2}"), 16)
            if t == 1:
                for z in range(3):
                    expert_weights(sp, 1, 3 + z)
            if t >= 1:
                sp.wait_ge(ev("h2_ready"), t)
                sp.dma_start(h2_d[(t - 1) * P:t * P, :], H2[:, (t - 1) % 2, :]).then_inc(ev(f"h2_out{(t - 1) % 2}"), 16)
        sp.wait_ge(ev("h2_ready"), NT)
        sp.dma_start(h2_d[SEQ:NTOK, :], H2[0:NS, 0, :]).then_inc(ev("h2_out0"), 16)
        sp.wait_ge(slot_out, rel[("wo", 1)])
        for z in range(3):
            expert_weights(sp, 0, z)
        with sp.Fori(1, NE // 2) as i:
            for z in range(6):
                sp.wait_ge(ev(f"w_used{z}"), i)
                expert_weights(sp, 2 * i + z // 3, z)
        sp.wait_ge(ev("x1_ready"), NT)
        sp.dma_start(BC2[:, 0, :], mod_d[0:1, 5 * D:6 * D].partition_broadcast(P)).then_inc(ev("rows2_in"), 16)
        sp.dma_start(BC2[0:NS, 1, :], bass.AP(mod_d.tensor, 6 * D + 5 * D, [[6 * D, NB], [0, ST], [1, D]])).then_inc(ev("rows2_in"), 16)
        sp.dma_start(BC2[:, 2, :], I["ln2_g"].partition_broadcast(P)).then_inc(ev("rows2_in"), 16)
        sp.dma_start(BC2[:, 3, :], I["ln2_b"].partition_broadcast(P)).then_inc(ev("rows2_in"), 16)
        sp.wait_ge(ev("further_known"), 1)
        nov = sp.value_load(ints[0:1, I_NOV:I_NOV + 1], min_val=0, max_val=NOV)

        def further_weights(s, i, p):
            e = sp.value_load(ints[0:1, bass.ds(s + I_E, 1)], min_val=0, max_val=NE - 1)
            for z in range(3):
                sp.wait_ge(ev(f"w_used{3 * p + z}"), NE // 2 + i)
                expert_weights(sp, e, 3 * p + z)
        each_further(sp, nov, further_weights)
        for t in range(NT):
            sp.wait_ge(ev("out_ready"), t + 1)
            dst = O["y_prompt"][0, t * P:t * P + P, :] if t < 4 else O["y_sample"].rearrange("b t f -> (b t) f")
            sp.dma_start(dst, OUT[0:rows_of(t), t % 2, :]).then_inc(ev(f"y_stored{t % 2}"), 16)
        sp.wait_ge(ev("y_stored0"), 16 * 3)
        sp.wait_ge(ev("y_stored1"), 16 * 2)
        sp.wait_ge(ev("kv_out0"), 32 * 3)
        sp.wait_ge(ev("kv_out1"), 32 * 2)
        sp.wait_ge(ev("cv_out"), 16 * (1 + NB))
        sp.wait_ge(ev("state_out"), 16)
        sp.wait_ge(ev("newv_out"), 16 * NT)
        sp.wait_ge(ev("vchunk_out"), 16)

    @block.gpsimd
    def _(pool):
        own = Steps(pool, ev("pool_own"))
        own.done(pool.memset(AE[:, :, 0:30], 0.0))
        own.done(pool.memset(HALFN, -0.5))
        own.link(pool.memset(GT[:, 0, 0:SLOTS // P], 0.0))
        pool.dma_start(lst_d.rearrange("(p n) a -> p (n a)", p=P), GT[:, 0, 0:SLOTS // P]).then_inc(ev("list_zeroed"), 16)
        b_in = I["b_in"]
        for a, b, c in ((0, C_U, 1024), (1024, C_V, 128), (1152, C_WI, 4)):
            pool.dma_start(BB[:, a:a + c], b_in[:, b:b + c].partition_broadcast(P)).then_inc(ev("biasb"), 16)
        pool.dma_start(BB[:, 1156:1668], I["lnC_g"].partition_broadcast(P)).then_inc(ev("biasb"), 16)
        pool.dma_start(BB[:, 1668:2180], I["lnC_b"].partition_broadcast(P)).then_inc(ev("biasb"), 16)

        def load_bada(n):
            if n >= 2:
                pool.wait_ge(ev("mod_row"), n - 1)
            pool.dma_start(BAD[0:9, n % 2, :], I["b_ada"][:, 512 * n:512 * n + 512].partition_broadcast(9)).then_inc(ev(f"bada_in{n % 2}"), 16)
        load_bada(0)
        load_bada(1)
        rstds = [0]

        def rstd(n):
            rstds[0] += 1
            pool.wait_ge(ev("var_ready"), rstds[0])
            own.link(pool.tensor_scalar(VEPS[0:n], MV[0:n, 1:2], EPS, None, ALU.add))
            pool.tensor_tensor(RSTD[0:n], VEPS[0:n], HALFN[0:n], ALU.pow).then_inc(ev("rstd_ready"), 1)

        for key in plan:
            kind = key[0]
            if kind == "ada":
                n = key[1]
                pool.wait_ge(ev("mod_raw"), n + 1)
                pool.wait_ge(ev(f"bada_in{n % 2}"), 16 * (n // 2 + 1))
                pool.tensor_tensor(MOD[0:9, n % 2, :], MOD[0:9, n % 2, :], BAD[0:9, n % 2, :], ALU.add).then_inc(ev("mod_row"), 1)
                pool.wait_ge(ev("mod_row"), n + 1)
                pool.dma_start(mod_d[:, 512 * n:512 * n + 512], MOD[0:9, n % 2, :]).then_inc(ev(f"mod_out{n % 2}"), 16)
                if n + 2 < 12:
                    load_bada(n + 2)
            elif kind == "nat":
                _, what, t = key
                if what == "w" and t == 0:
                    pool.wait_ge(ev("biasb"), 80)
                pool.wait_ge(*mm.taken(key))
                if what == "w":
                    own.done(pool.tensor_tensor(VA[:, t, :], VA[:, t, :], BB[:, 1024:1152], ALU.add))
                    pool.tensor_tensor(WI[:, 4 * t:4 * t + 4], WI[:, 4 * t:4 * t + 4], BB[:, 1152:1156], ALU.add).then_inc(ev("w_biased"), 1)
                    own.need()
                    if t < 4:
                        dst = O["new_v_prompt"][0, 0, t * P:t * P + P].rearrange("s n d -> s (n d)")
                    else:
                        dst = O["new_v_sample"][0].rearrange("b s n d -> (b s) (n d)")
                    pool.dma_start(dst, VA[0:rows_of(t), t, :]).then_inc(ev("newv_out"), 16)
                elif what == "u":
                    pool.tensor_tensor(UN[:, t, :], UN[:, t, :], BB[:, 0:512], ALU.add).then_inc(ev("u_biased"), 1)
                else:
                    pool.tensor_tensor(VN[:, t, :], VN[:, t, :], BB[:, 512:1024], ALU.add).then_inc(ev("v_biased"), 1)
                    rstd(P)
                    pool.wait_ge(ev("v_norm"), t + 1)
                    own.link(pool.tensor_tensor(VN[:, t, :], VN[:, t, :], BB[:, 1156:1668], ALU.mult))
                    pool.tensor_tensor(VN[:, t, :], VN[:, t, :], BB[:, 1668:2180], ALU.add).then_inc(ev("v_full"), 1)
                    if t == 4:
                        pool.wait_ge(ev("v_full"), NT)
                        pool.dma_start(O["new_vchunk_sample"][0].rearrange("b t c -> (b t) c"), VN[0:NS, 4, :]).then_inc(ev("vchunk_out"), 16)
            elif kind == "lnA1":
                rstd(rows_of(key[1]))
            elif kind == "proj":
                _, x, f, h = key
                n = pair_no[(x, f, h)]
                z, cols = n % 2, slice(h * HALF, h * HALF + HALF)
                pool.wait_ge(*mm.taken(("gate", x, f, h)))
                own.link(pool.tensor_scalar(GT[:, z, :], GT[:, z, :], 1.0, None, ALU.add))
                pool.wait_ge(*mm.taken(key))
                if x == "A":
                    pool.tensor_tensor(MG[:, f, cols], GT[:, z, :], PJ[:, z, :], ALU.mult).then_inc(ev("merged"), 1)
                else:
                    own.link(pool.tensor_tensor(PJ[:, z, :], GT[:, z, :], PJ[:, z, :], ALU.mult))
                    pool.tensor_tensor(MG[:, f, cols], MG[:, f, cols], PJ[:, z, :], ALU.add).then_inc(ev("merged"), 1)
            elif key == ("kit", 0):
                pool.wait_ge(ev("yct_up"), NT)
                pool.wait_ge(ev("vchunk_out"), 16)
                own.link(pool.memset(QIM, 0.0))
                for j in range(2):
                    for n in range(NKV):
                        q = QIT[:, j, SEQ:NTOK]
                        own.link(pool.tensor_copy(diagonal(A_QM + j * NB * P + n * NS, 0, P), q.rearrange("p (b t) -> p b t", t=ST)))
                        last = pool.tensor_copy(QI2[:, j, n * NS:n * NS + NS], q)
                        own.link(last) if (j, n) != (1, 1) else last.then_inc(ev("qim_ready"), 1)
            elif key == ("kts", 0):
                pool.wait_ge(*at.full(("dots", "s", 3)))
                pool.wait_ge(ev("qim_ready"), 1)
                for z in range(2):
                    own.done(pool.memset(QMN[z][0], 0.0))
                    own.link(pool.memset(QMN[z][1], 0.0))
            elif kind == "lg" and key[1] == "s":
                c = key[2]
                if c >= 2:
                    pool.wait_ge(*at.full(("lg", "s", c - 2)))
                for n in range(NKV):
                    r = slice(n * HD, n * HD + HD)
                    q = QT[r, c, SEQ:NTOK]
                    own.link(pool.tensor_copy(diagonal(A_QM + (c % 2) * 1152 + n * NS, n * HD, HD), q.rearrange("p (b t) -> p b t", t=ST)))
                    last = pool.tensor_copy(QMN[c % 2][1][r, n * NS:n * NS + NS], q)
                    own.link(last) if n == 0 else last.then_inc(ev("qm_ready"), 1)
            elif kind == "wo" and key[2] == 1:
                t = key[1]
                n = rows_of(t)
                if t == 0:
                    pool.wait_ge(ev("rows_in"), 16 * 8)
                rstd(n)
                pool.wait_ge(ev("r_norm"), t + 1)
                own.link(pool.tensor_tensor(X1[0:n, t, :], R[0:n, t % 2, :], BC["lg"][0:n], ALU.mult))
                pool.tensor_tensor(X1[0:n, t, :], X1[0:n, t, :], BC["lb"][0:n], ALU.add).then_inc(ev("x1_ready"), 1)
            elif kind == "lst":
                pool.wait_ge(ev("list_zeroed"), 16)
                pool.wait_ge(ev("slots_ready"), 1)
                for t in range(NT):
                    n = rows_of(t)
                    for a in (I_SA, I_SB):
                        pool.indirect_dma_start(lst_d, bass.IndirectOffsetOnAxis(ints[0:n, a + t:a + t + 1], 0),
                                                con[0:n, K_TOK + t:K_TOK + t + 1], None).then_inc(ev("scattered"), 16)
                pool.wait_ge(ev("scattered"), 32 * NT)
                pool.dma_start(LSTN[0:NE, 0:TS], lst_d[0:FAR_ROWS].rearrange("(e n) a -> e (n a)", n=TS)).then_inc(ev("list_in"), 16)
                pool.dma_start(LSTO[0:NOV], lst_d[FAR_ROWS:SLOTS].rearrange("(r n) a -> r (n a)", n=TO)).then_inc(ev("list2_in"), 16)

        pool.wait_ge(ev("list_int"), 1)
        pool.wait_ge(ev("h2_out0"), 16 * 3)
        pool.wait_ge(ev("h2_out1"), 16 * 2)
        for e in range(NE):
            if e == 2:
                own.link(pool.memset(ZERO, 0.0))
                pool.dma_start(y_d[FAR_ROWS:SLOTS].rearrange("(p n) (h d) -> p (n h) d", p=P, d=512),
                               ZERO.unsqueeze(1).broadcast_to([P, NOV * TO * 2 // P, 512])).then_inc(ev("far_zeroed"), 16)
            if e >= 2:
                pool.wait_ge(ev("gt_full"), e - 1)
            pool.indirect_dma_start(G[0:TS, e % 2, :], None, h2_d, bass.IndirectOffsetOnAxis(ints[0:TS, I_L + e:I_L + e + 1], 0)).then_inc(ev(f"rows_gathered{e % 2}"), 16)
        for p in range(2):
            pool.wait_ge(ev(f"yo_out{p}"), 16 * (NE // 2))
        pool.wait_ge(ev("further_known"), 1)
        nov = pool.value_load(ints[0:1, I_NOV:I_NOV + 1], min_val=0, max_val=NOV)
        pool.wait_ge(ev("far_zeroed"), 16)
        with pool.If(nov > 0):
            pool.wait_ge(ev("further_ids"), 1)
            for s in range(NOV):
                with pool.If(nov > s):
                    pool.wait_ge(ev("gt_full"), NE + s - 1)
                    pool.indirect_dma_start(G[0:TO, s % 2, :], None, h2_d, bass.IndirectOffsetOnAxis(ints[0:TO, I_O + s:I_O + s + 1], 0)).then_inc(ev(f"rows_gathered{s % 2}"), 16)
            for s in range(NOV):
                with pool.If(nov > s):
                    pool.wait_ge(ev(f"yo_out{s % 2}"), 16 * (NE // 2 + s // 2 + 1))
        for t in range(NT + 1):
            if t < NT:
                n = rows_of(t)
                if t >= 2:
                    pool.wait_ge(ev("out_ready"), t - 1)
                for k, a in enumerate((I_SA, I_SB)):
                    pool.indirect_dma_start(GAT[0:n, 2 * (t % 2) + k, :], None, y_d,
                                            bass.IndirectOffsetOnAxis(ints[0:n, a + t:a + t + 1], 0)).then_inc(ev(f"pair_in{t % 2}"), 16)
            if t >= 1:
                d = t - 1
                n = rows_of(d)
                rstd(n)
                pool.wait_ge(ev("o_norm"), d + 1)
                if d >= 2:
                    pool.wait_ge(ev(f"y_stored{d % 2}"), 16 * (d // 2))
                if d == 0:
                    pool.wait_ge(ev("rows2_in"), 64)
                own.link(pool.tensor_tensor(OUT[0:n, d % 2, :], GAT[0:n, 2 * (d % 2), :], BC2[0:n, 2, :], ALU.mult))
                pool.tensor_tensor(OUT[0:n, d % 2, :], OUT[0:n, d % 2, :], BC2[0:n, 3, :], ALU.add).then_inc(ev("out_ready"), 1)

    @block.scalar
    def _(act):
        own = Steps(act, ev("act_own"))
        b_in = I["b_in"][0]
        for r, c, k in ((R_A, 0, 8), (R_K, C_K, 1), (R_QI, C_QI, 2), (R_G, C_G, 24)):
            act.dma_start(PRN[r:r + k, :], b_in[c:c + k * P].rearrange("(r n) -> r n", n=P)).then_inc(ev("small_in"), 16)
        for n in range(NKV):
            act.dma_start(PRN[R_Q:R_Q + 4, n * HD:n * HD + HD],
                          b_in[C_Q + n * 256:C_Q + n * 256 + 256].rearrange("(c d) -> c d", d=HD)).then_inc(ev("small_in"), 16)
            act.dma_start(PRN[R_KI:R_KI + 1, n * HD:n * HD + HD], b_in[C_KI:C_KI + HD].unsqueeze(0)).then_inc(ev("small_in"), 16)
        for r, name in ((R_CB, "conv_b"), (R_LG, "lnA_g"), (R_LB, "lnA_b")):
            act.dma_start(PRN[r:r + 4, :], I[name][0].rearrange("(r n) -> r n", n=P)).then_inc(ev("small_in"), 16)
        act.dma_start(PRN[R_BS:R_BS + NCG, :], I["b_s"][0]).then_inc(ev("small_in"), 16)
        act.dma_start(CKN[0:CW, :], I["conv_k"][0]).then_inc(ev("convk_in"), 16)
        act.dma_start(WSN, I["w_s"][0].rearrange("g t s -> t g s")).then_inc(ev("ws_in"), 16)
        for h in range(2):
            act.dma_start(STN[0:120, h, :], I["state_conv"][0, 4 * h:4 * h + 4].rearrange("b r f -> (b r) f")).then_inc(ev("state_in"), 16)
        act.dma_start(REL[0:NBUCK, :], I["rel_table"]).then_inc(ev("table_parts"), 16)
        act.dma_start(OH[0:NBUCK, :], oh_d).then_inc(ev("table_parts"), 16)
        act.wait_ge(ev("c_in"), 32)
        act.activation(CN[0:9, :], CN[0:9, :], ACT.Silu).then_inc(ev("c_silu"), 1)

        pending = []

        def exps():
            while pending:
                u = pending.pop(0)
                i, c = units[u]
                if i != "s":
                    k = P * (i + 1)
                    for n in range(NKV):
                        act.wait_ge(ev("logits_up"), 2 * u + n + 1)
                        act.activation(LP[:, n, 0:k], LP[:, n, 0:k], ACT.Exp, bias=NEGM[:, n:n + 1], accum_out=RSUM[:, n:n + 1]).then_inc(ev("exp_done"), 1)
                else:
                    act.wait_ge(ev("logits_up"), 32 + u - 15)
                    act.activation(LP[:, 0, 0:320], LP[:, 0, 0:320], ACT.Exp, bias=NEGM[:, 0:1], accum_out=RSUM[:, 0:1]).then_inc(ev("exp_done"), 1)

        for key in plan:
            kind = key[0]
            if kind == "oh":
                h = key[1]
                a, b = (0, 512) if h == 0 else (512, SLEN)
                act.wait_ge(*at.full(key))
                act.activation(TAB[0:8, a:b], at.tile(key)[0:8, 0:b - a], ACT.Copy).then_inc(at.free(key), 1)
                if h == 1:
                    act.wait_ge(*at.taken(("oh", 0)))
                    act.wait_ge(*at.taken(("oh", 1)))
                    act.dma_start(tab_d, TAB[0:8, :].unsqueeze(1).broadcast_to([8, P, SLEN])).then_inc(ev("table_out"), 16)
            elif kind == "ada":
                n = key[1]
                act.wait_ge(*mm.full(key))
                if n >= 2:
                    act.wait_ge(ev(f"mod_out{n % 2}"), 16 * (n // 2))
                    if n < 6:
                        act.wait_ge(*tt.full(("mT", n - 2)))
                act.activation(MOD[0:9, n % 2, :], mm.tile(key)[0:9, :], ACT.Copy).then_inc(mm.free(key), 1)
                act.wait_ge(*mm.taken(key))
                act.sem_inc(ev("mod_raw"), 1)
            elif kind == "xT":
                f = key[1]
                act.wait_ge(*tt.full(key))
                if f == 0:
                    act.wait_ge(ev("modT_up"), 4)
                act.activation(HT[:, f, 0:SEQ], tt.tile(key), ACT.Identity, bias=MT[:, f, 0:1], scale=MT[:, 8 + f, 0:1]).then_inc(tt.free(key), 1)
            elif kind == "fm" and key[1] != "a":
                _, name, j, h = key
                cols = slice(h * HALF, h * HALF + HALF)
                act.wait_ge(*mm.full(key))
                src = mm.tile(key)[:, 0:HALF]
                if name == "ag":
                    n = glu_no[(j, h)]
                    if n == 0:
                        act.wait_ge(ev("params_up"), 1)
                        act.wait_ge(*at.full(("oh", 1)))
                    if n >= 2:
                        act.wait_ge(ev("glu_up"), n - 1)
                    act.activation(LP[:, n % 2, 0:HALF], src, ACT.Tanh, bias=PARH[:, R_A + 4 + j:R_A + 5 + j], scale=0.5).then_inc(mm.free(key), 1)
                else:
                    dst, r = {"q": (QT[:, j], R_Q + j), "k": (KTT, R_K), "ki": (KIT, R_KI), "qi": (QIT[:, j % 2], R_QI + j)}[name]
                    act.activation(dst[:, cols], src, ACT.Identity, bias=PAR[:, r:r + 1]).then_inc(mm.free(key), 1)
            elif kind == "kv":
                t = key[1]
                n = rows_of(t)
                act.wait_ge(*tt.full(key))
                if t >= 2:
                    act.wait_ge(ev(f"kv_out{t % 2}"), 32 * (t // 2))
                ko = SC[0:n, (t % 2) * 192:(t % 2) * 192 + 192]
                act.activation(ko, tt.tile(key)[0:n, 0:192], ACT.Copy).then_inc(tt.free(key), 1)
                act.wait_ge(*tt.taken(key))
                if t < 4:
                    dk = O["new_k_prompt"][0, 0, t * P:t * P + P].rearrange("s n d -> s (n d)")
                    di = O["new_kidx_prompt"][0, 0, t * P:t * P + P]
                else:
                    dk = O["new_k_sample"][0].rearrange("b s n d -> (b s) (n d)")
                    di = O["new_kidx_sample"][0].rearrange("b s d -> (b s) d")
                act.dma_start(dk, ko[:, 0:P]).then_inc(ev(f"kv_out{t % 2}"), 16)
                act.dma_start(di, ko[:, P:192]).then_inc(ev(f"kv_out{t % 2}"), 16)
            elif kind in ("cvp", "cvs"):
                n, dst = (CW - 1, PTT[0:CW - 1, 0, :]) if kind == "cvp" else (NS, PTT[0:NS, 1, :])
                act.wait_ge(*tt.full(key))
                act.activation(dst, tt.tile(key)[0:n, :], ACT.Copy).then_inc(tt.free(key), 1)
                act.wait_ge(*tt.taken(key))
                if kind == "cvp":
                    act.dma_start(O["new_conv_prompt"][0, 0], dst).then_inc(ev("cv_out"), 16)
                else:
                    for b in range(NB):
                        act.dma_start(O["new_conv_sample"][0, b, CW - 1 - ST:CW - 1, :], dst[b * ST:b * ST + ST, :]).then_inc(ev("cv_out"), 16)
            elif kind == "nat":
                _, what, t = key
                act.wait_ge(*mm.full(key))
                src = mm.tile(key)
                if what == "w":
                    own.done(act.activation(VA[:, t, :], src[:, 0:P], ACT.Copy))
                    own.need()
                    act.activation(WI[:, 4 * t:4 * t + 4], src[:, P:NW], ACT.Copy).then_inc(mm.free(key), 1)
                else:
                    act.activation((UN if what == "u" else VN)[:, t, :], src, ACT.Copy).then_inc(mm.free(key), 1)
            elif kind == "lnA2":
                t = key[1]
                n = rows_of(t)
                act.wait_ge(*tt.full(key))
                for j in range(NJ):
                    if j == NJ - 1:
                        own.need()
                    last = act.activation(YT["A"][:, j, t * P:t * P + n], tt.tile(key)[:, j * P:j * P + n], ACT.Silu,
                                          bias=PAR[:, R_LB + j:R_LB + j + 1], scale=PAR[:, R_LG + j:R_LG + j + 1])
                    own.done(last) if j < NJ - 1 else last.then_inc(tt.free(key), 1)
            elif kind == "gate":
                _, x, f, h = key
                n = pair_no[(x, f, h)]
                act.wait_ge(*mm.full(key))
                if n == 0:
                    act.wait_ge(ev("list_zeroed"), 16)
                if n >= 2:
                    act.wait_ge(ev("merged"), n - 1)
                r = R_G + "ABC".index(x) * KT + f
                act.activation(GT[:, n % 2, :], mm.tile(key)[:, 0:HALF], ACT.Tanh, bias=PARH[:, r:r + 1], scale=0.5).then_inc(mm.free(key), 1)
                exps()
            elif kind == "proj":
                _, x, f, h = key
                n = pair_no[(x, f, h)]
                act.wait_ge(*mm.full(key))
                act.activation(PJ[:, n % 2, :], mm.tile(key)[:, 0:HALF], ACT.Copy).then_inc(mm.free(key), 1)
            elif kind == "lg":
                if key[1] == "s":
                    exps()
                pending.append(unit_no[(key[1], key[2])])
                if key[1] == "s":
                    exps()
            elif kind == "h2T":
                _, t, h = key
                n = rows_of(t)
                act.wait_ge(*tt.full(key))
                if t and h == 0:
                    act.wait_ge(*at.full(("rt", t - 1)))
                src = tt.tile(key).rearrange("p (k n) -> p k n", n=P)
                act.activation(H2T[:, 4 * h:4 * h + 4, 0:n], src[:, :, 0:n], ACT.Copy).then_inc(tt.free(key), 1)
            elif kind == "rt":
                t = key[1]
                n = rows_of(t)
                act.wait_ge(*at.full(key))
                act.activation(TH[0:n, t, :], at.tile(key)[0:n, 0:NE], ACT.Tanh, scale=0.5).then_inc(at.free(key), 1)

        def result(d, dq):
            p = 1 - result.p
            act.wait_ge(ev("dn_full"), d + 1)
            if positive(dq):
                act.wait_ge(ev(f"yo_out{p}"), 16 * dq)
            act.activation(YO[0:TS, p, 0:512], banks[5][0:TS, :], ACT.Copy).then_inc(ev("yo_a"), 1)
            rows = y_d[d * TS:d * TS + TS, :] if type(d) is int else y_d[bass.ds(d * TS, TS), :]
            act.wait_ge(ev("yo_a"), d + 1)
            act.wait_ge(ev("yo_b"), d + 1)
            act.dma_start(rows, YO[0:TS, p, :]).then_inc(ev(f"yo_out{p}"), 16)

        def expert(e, q, dq, p):
            act.wait_ge(ev("gt_full"), e + 1)
            act.activation(HG[:, p, 0:4, 0:TS], quarter_tiles(banks[2])[:, :, 0:TS], ACT.Copy).then_inc(ev("gt_a"), 1)
            act.wait_ge(ev("gu_full"), e + 1)
            act.activation(HE[0:TS, p, :], banks[0][0:TS, :], ACT.Silu).then_inc(ev("he_silu"), 1)
            if positive(e):
                result.p = p
                result(e - 1, dq)

        act.wait_ge(ev("x1_ready"), NT)
        each_expert(act, expert)
        result.p = 0
        result(NE - 1, NE // 2 - 1)
        nov = act.value_load(ints[0:1, I_NOV:I_NOV + 1], min_val=0, max_val=NOV)

        def further(s, i, p):
            act.wait_ge(ev("gt_full"), s + NE + 1)
            act.activation(HG[:, p, 0:4, 0:TO], quarter_tiles(banks[2])[:, :, 0:TO], ACT.Copy).then_inc(ev("gt_a"), 1)
            act.wait_ge(ev("gu_full"), s + NE + 1)
            act.activation(HE[:, p, 0:NJ * TO], banks[0][:, 0:NJ * TO], ACT.Silu).then_inc(ev("he_silu"), 1)
            act.wait_ge(ev("dn_full"), s + NE + 1)
            act.wait_ge(ev(f"yo_out{p}"), 16 * (i + NE // 2))
            act.activation(YO[0:TO, p, 0:512], banks[5][0:TO, :], ACT.Copy).then_inc(ev("yo_a"), 1)
            act.wait_ge(ev("yo_a"), s + NE + 1)
            act.wait_ge(ev("yo_b"), s + NE + 1)
            act.wait_ge(ev("far_zeroed"), 16)
            act.dma_start(y_d[bass.ds(s * TO + FAR_ROWS, TO), :], YO[0:TO, p, :]).then_inc(ev(f"yo_out{p}"), 16)
        each_further(act, nov, further)

    @block.vector
    def _(dve):
        own = Steps(dve, ev("dve_own"))
        link, done, need = own.link, own.done, own.need
        ts, tt_, stt = dve.tensor_scalar, dve.tensor_tensor, dve.scalar_tensor_tensor
        stats_n = [0]

        def stats(src, n, width=512):
            for k in range(width // 512):
                done(dve.bn_stats(STAT[0:n, 6 * k:6 * k + 6], src[:, 512 * k:512 * k + 512]))
            need()
            stats_n[0] += 1
            dve.bn_aggr(MV[0:n], STAT[0:n, 0:6 * (width // 512)]).then_inc(ev("var_ready"), 1)
            dve.wait_ge(ev("var_ready"), stats_n[0])
            dve.wait_ge(ev("rstd_ready"), stats_n[0])

        def conv():
            acc_s = [ACC[:, j, SEQ:NTOK].rearrange("p (b t) -> p b t", t=ST) for j in range(NJ)]

            def old_s(j, w):
                v = AES[:, j, 30 + SEQ:EXT].rearrange("p (b x) -> p b x", x=30 + ST)
                return v[:, :, w:w + ST] if type(w) is int else v[:, :, bass.ds(w, ST)]
            conv_n = ev("conv_steps")
            for j in range(NJ):
                ts(ACC[:, j, 0:SEQ], AES[:, j, 0:SEQ], CK[:, j, 0:1], PAR[:, R_CB + j:R_CB + j + 1], ALU.mult, ALU.add).then_inc(conv_n, 1)
            for j in range(NJ):
                ts(acc_s[j], old_s(j, 0), CK[:, j, 0:1], PAR[:, R_CB + j:R_CB + j + 1], ALU.mult, ALU.add).then_inc(conv_n, 1)
            with dve.Fori(1, CW) as w:
                for j in range(NJ):
                    dve.wait_ge(conv_n, w * 8 + (j - 7))
                    stt(ACC[:, j, 0:SEQ], arena[:, bass.ds(w + (A_AE + j * EXT), SEQ)], arena[:, bass.ds(w + (A_CK + j * CW), 1)],
                        ACC[:, j, 0:SEQ], ALU.mult, ALU.add).then_inc(conv_n, 1)
                for j in range(NJ):
                    dve.wait_ge(conv_n, w * 8 + (j - 3))
                    stt(acc_s[j], old_s(j, w), arena[:, bass.ds(w + (A_CK + j * CW), 1)], acc_s[j], ALU.mult, ALU.add).then_inc(conv_n, 1)
            dve.wait_ge(conv_n, 8 * CW)
            dve.nop().then_inc(ev("conv_done"), 1)

        def top_mask(i, width, rounds, k):
            for r in range(rounds):
                link(dve.max(MX8, SC[:, 0:width]))
                link(dve.match_replace(SC[:, 0:width], MX8, SC[:, 0:width], REPL))
            link(ts(PEN[i], SC[:, 0:k], SELD, NEG, ALU.is_gt, ALU.mult))

        def prepare_rows():
            dve.wait_ge(ev("rows_in"), 16 * 8)
            for pick, n in (("p", P), ("s", NS)):
                g1, sc, sh = (BC[name + pick][0:n] for name in ("g1", "sc", "sh"))
                done(ts(g1, g1, 0.5, 0.5, ALU.mult, ALU.add))
                link(ts(sc, sc, 1.0, None, ALU.add))
                link(tt_(H2[0:n, 0, :], sc, BC["lb"][0:n], ALU.mult))
                done(tt_(sh, sh, H2[0:n, 0, :], ALU.add))
                link(tt_(sc, sc, BC["lg"][0:n], ALU.mult))

        def route():
            dve.wait_ge(*at.taken(("rt", 4)))
            dve.wait_ge(ev("router_in"), 48)
            link(ts(TH, TH, 0.5, 0.5, ALU.mult, ALU.add))
            link(tt_(SEL, TH, RB.unsqueeze(1).broadcast_to([P, NT, NE]), ALU.add))
            q = SEL.rearrange("p t (g e) -> p (t g) e", e=4)
            done(tt_(PSUMS[:, :, 0:3], q[:, :, 0:3], q[:, :, 1:4], ALU.add))
            done(tt_(PSUMS[:, :, 3:5], q[:, :, 0:2], q[:, :, 2:4], ALU.add))
            link(tt_(PSUMS[:, :, 5:6], q[:, :, 0:1], q[:, :, 3:4], ALU.add))
            link(dve.tensor_reduce(GS, PSUMS, AX.X, ALU.max))
            link(dve.tensor_copy(GBUF[:, :, 0:4], GS.rearrange("p (t g) -> p t g", g=4)))
            for t in range(NT):
                link(dve.max(MX8, GBUF[:, t, :]))
                link(dve.match_replace(GRES[:, t, :], MX8, GBUF[:, t, :], REPL))
            link(ts(GMK.rearrange("p (t g) -> p t g", g=4), GRES[:, :, 0:4], SELD, NEG, ALU.is_gt, ALU.mult))
            link(tt_(SBUF_[:, :, 0:NE].rearrange("p t (g e) -> p t g e", e=4), SEL.rearrange("p t (g e) -> p t g e", e=4),
                     GMK.rearrange("p (t g) -> p t g", g=4).unsqueeze(3).broadcast_to([P, NT, 4, 4]), ALU.add))
            for t in range(NT):
                link(dve.max(MX8, SBUF_[:, t, :]))
                link(dve.match_replace(SRES[:, t, :], MX8, SBUF_[:, t, :], REPL))
            ts(MSK, SRES[:, :, 0:NE], SELD, None, ALU.is_lt).then_inc(ev("mask_ready"), 1)
            dve.wait_ge(ev("mask_ready"), 1)
            link(tt_(GATE, TH, MSK, ALU.mult))
            link(dve.tensor_reduce(SUM5, GATE, AX.X, ALU.add))
            link(dve.reciprocal(SUM5, SUM5))
            link(tt_(GATE, GATE, SUM5.unsqueeze(2).broadcast_to([P, NT, NE]), ALU.mult))

        def place_tokens(ps):
            cum = ps[:, 0:NT * NE].rearrange("p (t e) -> p t e", e=NE)
            base = con[:, K_SLOT:K_SLOT + NE].unsqueeze(1).broadcast_to([P, NT, NE])
            done(dve.memset(EQ[:, 4, :], 0.0))
            link(dve.memset(SLM[:, 4, :], 0.0))
            link(dve.tensor_copy(CNT, ps[:, NT * NE:(NT + 1) * NE]))
            cmp_ = CMP.rearrange("p a b -> p (a b)")[:, 0:NE * MORE].rearrange("p (e m) -> p e m", m=MORE)
            link(tt_(cmp_, CNT.unsqueeze(2).broadcast_to([P, NE, MORE]), RCON[:, NE * NE:].unsqueeze(1).broadcast_to([P, NE, MORE]), ALU.is_gt))
            link(dve.tensor_reduce(OVER, cmp_, AX.X, ALU.add))
            link(tt_(CMP, OVER.unsqueeze(1).broadcast_to([P, NE, NE]), RCON[:, 0:NE * NE].rearrange("p (a b) -> p a b", b=NE), ALU.mult))
            link(dve.tensor_reduce(BEFORE, CMP, AX.X, ALU.add))
            link(ts(TEXP, BEFORE, float(TO), float(FAR_ROWS - TS), ALU.mult, ALU.add))
            link(stt(TEXP, con[:, K_SLOT:K_SLOT + NE], -1.0, TEXP, ALU.mult, ALU.add))
            link(ts(TEXP, TEXP, -1.0, None, ALU.add))
            link(dve.tensor_copy(SLM[:, 0:4], cum[:, 0:4]))
            link(dve.tensor_copy(SLM[0:NS, 4], cum[0:NS, 4]))
            link(ts(EQ, SLM, float(TS), None, ALU.is_gt))
            link(tt_(EQ, EQ, TEXP.unsqueeze(1).broadcast_to([P, NT, NE]), ALU.mult))
            link(tt_(SLM, SLM, base, ALU.add))
            link(tt_(SLM, SLM, EQ, ALU.add))
            link(stt(EQ, SLM, -FAR, MSK, ALU.add, ALU.mult))
            link(dve.tensor_reduce(SA, EQ, AX.X, ALU.min))
            link(ts(SA, SA, FAR, None, ALU.add))
            link(tt_(SLM, SLM, MSK, ALU.mult))
            link(dve.tensor_reduce(SB_, SLM, AX.X, ALU.max))
            done(dve.tensor_copy(ints[:, I_SA:I_SA + NT], SA))
            link(dve.tensor_copy(ints[:, I_SB:I_SB + NT], SB_))
            dve.sem_inc(at.free(("cum",)), 1)
            dve.sem_inc(ev("slots_ready"), 1)
            for s_, w_ in ((SA, WGA), (SB_, WGB)):
                link(tt_(EQ, SLM, s_.unsqueeze(2).broadcast_to([P, NT, NE]), ALU.is_equal))
                link(tt_(EQ, EQ, GATE, ALU.mult))
                link(dve.tensor_reduce(w_, EQ, AX.X, ALU.add))

        def further_tiles():
            link(tt_(TEXP, BEFORE, OVER, ALU.add))
            done(dve.tensor_copy(ints[:, I_NOV:I_NOV + 1], TEXP[:, NE - 1:NE]))
            link(tt_(CMP, TEXP.unsqueeze(1).broadcast_to([P, NOV, NE]),
                     con[:, K_STEP:K_STEP + NOV].unsqueeze(2).broadcast_to([P, NOV, NE]), ALU.is_le))
            link(dve.tensor_reduce(CNT, CMP, AX.X, ALU.add))
            link(ts(CNT, CNT, NE - 1.0, None, ALU.min))
            link(dve.tensor_copy(ints[:, I_E:I_E + NOV], CNT))
            dve.sem_inc(ev("further_known"), 1)

        for key in plan:
            kind = key[0]
            ring_of = {"M": mm, "T": tt, "A": at}[kinds[kind]]
            mine = kind in ("par", "ck", "ws", "st", "cT", "mT", "xTs", "bd", "lnA1", "mix", "yc", "dots", "kit", "kts", "wo", "cum", "lst")
            if mine:
                dve.wait_ge(*ring_of.full(key))
                ps = ring_of.tile(key)
            if kind == "par":
                link(dve.tensor_copy(PAR, ps[:, 0:NR]))
                ts(PARH, PAR, 0.5, None, ALU.mult).then_inc(ev("params_up"), 1)
                dve.wait_ge(ev("params_up"), 1)
                dve.sem_inc(ring_of.free(key), 1)
            elif kind == "ck":
                dve.tensor_copy(CK, ps[:, 0:NJ * CW].rearrange("p (j w) -> p j w", w=CW)).then_inc(tt.free(key), 1)
            elif kind == "ws":
                h = key[1]
                if h == 0:
                    dve.wait_ge(ev("consts"), 16)
                tt_(WS[:, 4 * h:4 * h + 4, :], quarter_tiles(ps), tri.unsqueeze(1).broadcast_to([P, 4, P]), ALU.mult).then_inc(tt.free(key), 1)
            elif kind == "bd":
                for b in range(NB):
                    done(ts(BD[0:NS, :, b, :], ps[0:NS, 0:NCG * ST].rearrange("p (g t) -> p g t", t=ST),
                            con[0:NS, K_BLK + b:K_BLK + b + 1], None, ALU.mult))
                dve.tensor_copy(BS2, ps[:, NCG * ST:NCG * ST + NCG]).then_inc(at.free(key), 1)
            elif kind == "st":
                h = key[1]
                ext = AES[:, :, 30 + SEQ:EXT].rearrange("p j (b x) -> p j b x", x=30 + ST)
                src = ps[:, 0:4 * 120].rearrange("p (j b r) -> p j b r", j=NJ, b=4)
                for j in range(NJ):
                    last = dve.tensor_copy(ext[:, j, 4 * h:4 * h + 4, 0:30], src[:, j])
                    last.then_inc(tt.free(key), 1) if j == NJ - 1 else link(last)
            elif kind == "cT":
                dve.tensor_copy(CT, ps[:, 0:KT * 9].rearrange("p (k n) -> p k n", n=9)).then_inc(tt.free(key), 1)
            elif kind == "mT":
                n = key[1]
                src = ps[:, 0:36].rearrange("p (k n) -> p k n", n=9)
                ts(MT[:, 4 * n:4 * n + 4, :], src, 1.0 if n >= 2 else 0.0, None, ALU.add).then_inc(tt.free(key), 1)
                dve.wait_ge(*tt.taken(key))
                dve.sem_inc(ev("modT_up"), 1)
            elif kind == "xTs":
                dst = HT[:, :, SEQ:NTOK].rearrange("p f (b t) -> p f b t", t=ST)
                src = ps.rearrange("p (f b t) -> p f b t", f=KT, b=NB)
                for f in range(KT):
                    done(tt_(dst[:, f], src[:, f], MT[:, KT + f, 1:9].unsqueeze(2).broadcast_to([P, NB, ST]), ALU.mult))
                need()
                for f in range(KT):
                    done(tt_(dst[:, f], dst[:, f], MT[:, f, 1:9].unsqueeze(2).broadcast_to([P, NB, ST]), ALU.add))
                need()
                dve.tensor_copy(HT[:, :, NTOK:NTOK + NS], HT[:, :, SEQ:NTOK]).then_inc(tt.free(key), 1)
            elif kind == "fm" and key[1] == "a":
                _, _, j, h = key
                n = glu_no[(j, h)]
                dve.wait_ge(*mm.taken(("fm", "ag", j, h)))
                gate = LP[:, n % 2, 0:HALF]
                link(ts(gate, gate, 0.5, 0.5, ALU.mult, ALU.add))
                dve.wait_ge(*mm.full(key))
                ps = mm.tile(key)
                if n == 0:
                    dve.wait_ge(ev("pool_own"), 3)
                bias = PAR[:, R_A + j:R_A + j + 1]
                if h == 0:
                    link(stt(AES[:, j, 30:30 + HALF], ps[:, 0:HALF], bias, gate, ALU.add, ALU.mult))
                else:
                    m = SEQ - HALF
                    done(stt(AES[:, j, 30 + HALF:30 + SEQ], ps[:, 0:m], bias, gate[:, 0:m], ALU.add, ALU.mult))
                    ext = AES[:, j, 30 + SEQ:EXT].rearrange("p (b x) -> p b x", x=30 + ST)
                    link(stt(ext[:, :, 30:30 + ST], ps[:, m:HALF].rearrange("p (b t) -> p b t", t=ST), bias,
                             gate[:, m:HALF].rearrange("p (b t) -> p b t", t=ST), ALU.add, ALU.mult))
                dve.sem_inc(mm.free(key), 1)
                dve.sem_inc(ev("glu_up"), 1)
                if n == 2 * NJ - 1:
                    ext = AES[:, :, 30 + SEQ:EXT].rearrange("p j (b x) -> p j b x", x=30 + ST)
                    for j in range(NJ):
                        last = dve.tensor_copy(CVS[:, j, :].rearrange("p (b t) -> p b t", t=ST), ext[:, j, :, 30:30 + ST])
                        last.then_inc(ev("cvs_staged"), 1) if j == NJ - 1 else link(last)
                    conv()
            elif kind == "lnA1":
                t = key[1]
                n = rows_of(t)
                stats(ps[0:n], n)
                if t == 0:
                    dve.wait_ge(ev("cv_out"), 16 * 9)
                if t >= 2:
                    dve.wait_ge(*tt.full(("lnA2", t - 2)))
                ts(LP[0:n, t % 2, :], ps[0:n], MV[0:n, 0:1], RSTD[0:n], ALU.subtract, ALU.mult).then_inc(tt.free(key), 1)
            elif kind == "nat" and key[1] == "v":
                t = key[2]
                dve.wait_ge(ev("v_biased"), t + 1)
                stats(VN[:, t, :], P)
                ts(VN[:, t, :], VN[:, t, :], MV[:, 0:1], RSTD, ALU.subtract, ALU.mult).then_inc(ev("v_norm"), 1)
            elif kind == "mix":
                t = key[1]
                n = rows_of(t)
                bs = (PAR[:, R_BS:R_BS + NCG] if t < 4 else BS2)[0:n].unsqueeze(2).broadcast_to([n, NCG, HD])
                if t:
                    dve.wait_ge(ev("sgu_up"), t)
                tmp = TMP[0:n].rearrange("p (g d) -> p g d", d=HD)
                tt_(tmp, ps[0:n].rearrange("p (g d) -> p g d", d=HD), bs, ALU.add).then_inc(at.free(key), 1)
                dve.wait_ge(*at.taken(key))
                dve.wait_ge(ev("u_biased"), t + 1)
                tt_(UN[0:n, t, :], TMP[0:n], UN[0:n, t, :], ALU.mult).then_inc(ev("sgu_up"), 1)
            elif kind == "yc":
                t = key[1]
                n = rows_of(t)
                if t == 0:
                    dve.wait_ge(ev("mod_out0"), 16 * 6)
                    dve.wait_ge(ev("mod_out1"), 16 * 6)
                dve.tensor_copy(YT["C"][:, :, t * P:t * P + n], quarter_tiles(ps)[:, :, 0:n]).then_inc(tt.free(key), 1)
                dve.wait_ge(*tt.taken(key))
                dve.sem_inc(ev("yct_up"), 1)
            elif kind == "dots":
                _, i, h = key
                t = 4 if i == "s" else i
                k = 320 if i == "s" else P * (i + 1)
                w = WI[:, 4 * t + h:4 * t + h + 1]
                if (i, h) == (1, 0):
                    dve.wait_ge(ev("w_biased"), NT)
                    dve.wait_ge(ev("kv_out0"), 32 * 3)
                    dve.wait_ge(ev("kv_out1"), 32 * 2)
                if h == 0:
                    ts(SC[:, 0:k], ps[:, 0:k], 0.0, w, ALU.max, ALU.mult).then_inc(at.free(key), 1)
                    dve.wait_ge(*at.taken(key))
                else:
                    ts(TMP[:, 0:k], ps[:, 0:k], 0.0, w, ALU.max, ALU.mult).then_inc(at.free(key), 1)
                    dve.wait_ge(*at.taken(key))
                    link(tt_(SC[:, 0:k], SC[:, 0:k], TMP[:, 0:k], ALU.add))
                if h == 3:
                    if i == "s":
                        done(dve.memset(SC[:, k:k + 6], BIG))
                        link(tt_(SC[:, PAST:k], SC[:, PAST:k], con[:, K_PENS:K_PENS + NS], ALU.add))
                        top_mask(i, k + 6, (TOPK_S + 6) // 8, k)
                    else:
                        link(tt_(SC[:, k - P:k], SC[:, k - P:k], PEN[0], ALU.add))
                        top_mask(i, k, TOPK_P // 8, k)
            elif kind == "kit" or kind == "kts":
                g = key[1]
                if key == ("kit", 0):
                    dve.wait_ge(ev("yct_up"), NT)
                    dve.wait_ge(ev("vchunk_out"), 16)
                dve.tensor_copy(KTS[:, 2 * g:2 * g + 2, :], ps.rearrange("p (b s) -> p b s", s=PAST)).then_inc(tt.free(key), 1)
            elif kind == "lg":
                _, i, c = key
                u = unit_no[(i, c)]
                k = 320 if i == "s" else P * (i + 1)
                heads = [0] if i == "s" else [0, 1]
                if u:
                    prev = ("pt",) + units[u - 1]
                    dve.wait_ge(*tt.full(prev if units[u - 1][0] == "s" else prev + (1,)))
                else:
                    dve.wait_ge(*tt.full(("lnA2", 4)))
                dve.wait_ge(ev("bias_in"), bias_need[(i, c)])
                for n in heads:
                    kk = key if i == "s" else key + (n,)
                    dve.wait_ge(*at.full(kk))
                    done(stt(LP[:, n, 0:k], at.tile(kk)[:, 0:k], HD ** -0.5, BM[:, n, 0:k], ALU.mult, ALU.add))
                    need()
                    dve.sem_inc(at.free(kk), 1)
                    link(dve.tensor_tensor_reduce(out=LP[:, n, 0:k], in0=LP[:, n, 0:k], in1=PEN[i], scale=1.0, scalar=REPL,
                                                  op0=ALU.add, op1=ALU.max, accum_out=NEGM[:, n:n + 1]))
                    ts(NEGM[:, n:n + 1], NEGM[:, n:n + 1], -1.0, None, ALU.mult).then_inc(ev("logits_up"), 1)
                for n in heads:
                    dve.wait_ge(ev("exp_done"), (2 * u + n + 1) if i != "s" else 32 + u - 15)
                    link(dve.reciprocal(RINV[:, n:n + 1], RSUM[:, n:n + 1]))
                    ts(LP[:, n, 0:k], LP[:, n, 0:k], RINV[:, n:n + 1], None, ALU.mult).then_inc(ev("probs_ready"), 1)
            elif kind == "pt":
                _, i, c = key
                u = unit_no[(i, c)]
                if u:
                    dve.wait_ge(*at.full(("pv",) + units[u - 1]))
                else:
                    dve.wait_ge(ev("cv_out"), 16 * 9)
                if i != "s":
                    k = P * (i + 1)
                    for n in range(NKV):
                        kk = key + (n,)
                        dve.wait_ge(*tt.full(kk))
                        dve.tensor_copy(PTT[:, n, 0:k], tt.tile(kk)[:, 0:k]).then_inc(tt.free(kk), 1)
                else:
                    dve.wait_ge(*tt.full(key))
                    done(dve.tensor_copy(PTT[:, 0, 0:256], tt.tile(key)[:, 0:256]))
                    dve.tensor_copy(PTT[0:NS, 0, 256:384], tt.tile(key)[0:NS, 256:384]).then_inc(tt.free(key), 1)
            elif kind == "pv":
                _, i, c = key
                dve.wait_ge(*at.full(key))
                ps = at.tile(key)
                if key == ("pv", 0, 0):
                    dve.wait_ge(ev("v_full"), NT)
                    dve.wait_ge(ev("u_biased"), NT)
                if i != "s":
                    dve.tensor_copy(YT["B"][:, c, i * P:i * P + P], ps[:, 0:P]).then_inc(at.free(key), 1)
                else:
                    done(dve.tensor_copy(YT["B"][0:HD, c, SEQ:NTOK], ps[0:HD, 0:NS]))
                    need()
                    dve.tensor_copy(YT["B"][HD:P, c, SEQ:NTOK], ps[HD:P, NS:P]).then_inc(at.free(key), 1)
                dve.wait_ge(*at.taken(key))
                dve.sem_inc(ev("yb_up"), 1)
                if key == ("pv", "s", NC - 1):
                    prepare_rows()
            elif kind == "wo":
                _, t, h = key
                n = rows_of(t)
                r, x = R[0:n, t % 2, :], XR[0:n, t % 2, :]
                cols = slice(512 * h, 512 * h + 512)
                pick = "p" if t < 4 else "s"
                if h == 0 and t == 0:
                    dve.wait_ge(ev("merged"), 48)
                    link(dve.memset(TH[:, 4, :], 0.0))
                    done(dve.memset(GBUF, BIG))
                    link(dve.memset(SBUF_, BIG))
                if h == 0 and t >= 2:
                    dve.wait_ge(ev("x1_ready"), t - 1)
                tt_(r[:, cols], ps[0:n], BC["g1" + pick][0:n, cols], ALU.mult).then_inc(mm.free(key), 1)
                if h == 1:
                    dve.wait_ge(*mm.taken(("wo", t, 0)))
                    dve.wait_ge(*mm.taken(key))
                    dve.wait_ge(ev(f"xr_in{t % 2}"), 16 * (t // 2 + 1))
                    stt(r, x, ALPHA, r, ALU.mult, ALU.add).then_inc(ev("x_added"), 1)
                    dve.wait_ge(ev("x_added"), t + 1)
                    stats(r, n, D)
                    ts(r, r, MV[0:n, 0:1], RSTD[0:n], ALU.subtract, ALU.mult).then_inc(ev("r_norm"), 1)
                    dve.wait_ge(ev("r_norm"), t + 1)
                    h2 = H2[0:n, t % 2, :]
                    if t >= 2:
                        dve.wait_ge(ev(f"h2_out{t % 2}"), 16 * (t // 2))
                        dve.wait_ge(*tt.full(("h2T", t - 2, 1)))
                    link(tt_(h2, r, BC["sc" + pick][0:n], ALU.mult))
                    tt_(h2, h2, BC["sh" + pick][0:n], ALU.add).then_inc(ev("h2_ready"), 1)
            elif kind == "cum":
                place_tokens(ps)
            elif kind == "lst":
                link(dve.tensor_copy(ints[0:TS, I_L:I_L + NE], ps[0:TS, 0:NE]))
                dve.sem_inc(tt.free(key), 1)
                dve.sem_inc(ev("list_int"), 1)
                further_tiles()
            if key == ("rt", 4):
                route()

        def result(d, dq, p):
            dve.wait_ge(ev("dn_full"), d + 1)
            if positive(dq):
                dve.wait_ge(ev(f"yo_out{p}"), 16 * dq)
            dve.tensor_copy(YO[0:TS, p, 512:D], banks[6][0:TS, :]).then_inc(ev("yo_b"), 1)

        def expert(e, q, dq, p):
            dve.wait_ge(ev("gt_full"), e + 1)
            dve.tensor_copy(HG[:, p, 4:8, 0:TS], quarter_tiles(banks[3])[:, :, 0:TS]).then_inc(ev("gt_b"), 1)
            dve.wait_ge(ev("gu_full"), e + 1)
            dve.wait_ge(ev("he_silu"), e + 1)
            tt_(HE[0:TS, p, :], HE[0:TS, p, :], banks[1][0:TS, :], ALU.mult).then_inc(ev("he_ready"), 1)
            if positive(e):
                result(e - 1, dq, 1 - p)
            if type(e) is int and e == 1:
                dve.wait_ge(ev("list2_full"), 1)
                dve.tensor_copy(ints[0:TO, I_O:I_O + NOV], banks[7][0:TO, 0:NOV]).then_inc(ev("further_ids"), 1)
            dve.wait_ge(ev("het_full"), e + 1)
            dve.tensor_copy(HET[:, p, :, 0:TS], quarter_tiles(banks[4])[:, :, 0:TS]).then_inc(ev("het_up"), 1)

        dve.wait_ge(ev("x1_ready"), NT)
        each_expert(dve, expert)
        result(NE - 1, NE // 2 - 1, 1)
        nov = dve.value_load(ints[0:1, I_NOV:I_NOV + 1], min_val=0, max_val=NOV)

        def further(s, i, p):
            dve.wait_ge(ev("gt_full"), s + NE + 1)
            dve.tensor_copy(HG[:, p, 4:8, 0:TO], quarter_tiles(banks[3])[:, :, 0:TO]).then_inc(ev("gt_b"), 1)
            dve.wait_ge(ev("gu_full"), s + NE + 1)
            dve.wait_ge(ev("he_silu"), s + NE + 1)
            tt_(further_hidden(p), HE[:, p, 0:NJ * TO].rearrange("p (k n) -> p k n", n=TO),
                banks[1][:, 0:NJ * TO].rearrange("p (k n) -> p k n", n=TO), ALU.mult).then_inc(ev("he_ready"), 1)
            dve.wait_ge(ev("dn_full"), s + NE + 1)
            dve.wait_ge(ev(f"yo_out{p}"), 16 * (i + NE // 2))
            dve.tensor_copy(YO[0:TO, p, 512:D], banks[6][0:TO, :]).then_inc(ev("yo_b"), 1)
        each_further(dve, nov, further)
        dve.wait_ge(ev("rows2_in"), 64)
        done(ts(BC2[:, 0, :], BC2[:, 0, :], 1.0, None, ALU.add))
        link(ts(BC2[0:NS, 1, :], BC2[0:NS, 1, :], 1.0, None, ALU.add))
        for t in range(NT):
            n = rows_of(t)
            a, b = GAT[0:n, 2 * (t % 2), :], GAT[0:n, 2 * (t % 2) + 1, :]
            dve.wait_ge(ev(f"pair_in{t % 2}"), 32 * (t // 2 + 1))
            link(ts(a, a, WGA[0:n, t:t + 1], None, ALU.mult))
            link(stt(a, b, WGB[0:n, t:t + 1], a, ALU.mult, ALU.add))
            link(tt_(a, a, BC2[0:n, 0 if t < 4 else 1, :], ALU.mult))
            link(stt(a, X1[0:n, t, :], ALPHA, a, ALU.mult, ALU.add))
            stats(a, n, D)
            ts(a, a, MV[0:n, 0:1], RSTD[0:n], ALU.subtract, ALU.mult).then_inc(ev("o_norm"), 1)

    @block.tensor
    def _(pe):
        def group(out, pairs_):
            for k, (a, b) in enumerate(pairs_):
                last = pe.matmul(out, a, b, start=k == 0, stop=k == len(pairs_) - 1)
            return last

        def flip(out, src):
            return pe.transpose(out, src, ident[0:src.shape[0], 0:src.shape[0]])

        def got(key):
            pe.wait_ge(*arrived_at[key])

        slot8 = lambda key: wslot(key).rearrange("p (k n) -> p k n", k=KT)
        slot4 = lambda key: wslot(key).rearrange("p (k n) -> p k n", k=NJ)
        pe.wait_ge(ev("consts"), 16)
        for key in plan:
            kind = key[0]
            ring_of = {"M": mm, "T": tt, "A": at}[kinds[kind]]
            split = kind in ("lg", "pt") and key[1] != "s"
            if not split:
                if ring_of.old(key):
                    pe.wait_ge(*ring_of.room(key))
                ps = ring_of.tile(key)
            if kind == "par":
                pe.wait_ge(ev("small_in"), 16 * 12)
                last = flip(ps[:, 0:NR], PRN[0:NR, :])
            elif kind == "ck":
                pe.wait_ge(ev("convk_in"), 16)
                for j in range(NJ):
                    last = flip(ps[:, j * CW:j * CW + CW], CKN[0:CW, j * P:j * P + P])
            elif kind == "ws":
                pe.wait_ge(ev("ws_in"), 16)
                for g in range(4):
                    last = flip(ps[:, g * P:g * P + P], WSN[:, 4 * key[1] + g, :])
            elif kind == "bd":
                pe.wait_ge(*tt.taken(("ws", 0)))
                pe.wait_ge(*tt.taken(("ws", 1)))
                pe.wait_ge(ev("params_up"), 1)
                e8 = con[0:ST, K_E8:K_E8 + P]
                for g in range(NCG):
                    pe.matmul(ps[:, g * ST:g * ST + ST], e8, WS[0:ST, g, 0:ST], start=True, stop=True)
                last = pe.matmul(ps[:, NCG * ST:NCG * ST + NCG], e8, PAR[0:ST, R_BS:R_BS + NCG], start=True, stop=True)
            elif kind == "st":
                pe.wait_ge(ev("state_in"), 32)
                for j in range(NJ):
                    last = flip(ps[:, j * 120:j * 120 + 120], STN[0:120, key[1], j * P:j * P + P])
            elif kind == "oh":
                pe.wait_ge(ev("table_parts"), 32)
                a, b = (0, 512) if key[1] == 0 else (512, SLEN)
                last = pe.matmul(ps[0:8, 0:b - a], REL[0:NBUCK, :], OH[0:NBUCK, a:b], start=True, stop=True)
            elif kind == "cT":
                pe.wait_ge(ev("c_silu"), 1)
                for k in range(KT):
                    last = flip(ps[:, k * 9:k * 9 + 9], CN[0:9, k * P:k * P + P])
            elif kind == "ada":
                if key[1] == 0:
                    pe.wait_ge(*tt.taken(("cT",)))
                w = slot8(key)
                got(key)
                last = group(ps[0:9, :], [(CT[:, k, :], w[:, k, :]) for k in range(KT)])
            elif kind == "mT":
                n = key[1]
                pe.wait_ge(ev("mod_row"), n + 1)
                for k in range(4):
                    last = flip(ps[:, k * 9:k * 9 + 9], MOD[0:9, n % 2, k * P:k * P + P])
            elif kind == "xT":
                f = key[1]
                if f == 0:
                    pe.wait_ge(ev("x_in"), 16 * NT)
                for t in range(4):
                    last = flip(ps[:, t * P:t * P + P], X[:, t, f * P:f * P + P])
            elif kind == "xTs":
                for f in range(KT):
                    last = flip(ps[:, f * NS:f * NS + NS], X[0:NS, 4, f * P:f * P + P])
            elif kind == "fm":
                _, name, j, h = key
                if (name, j, h) == ("ag", 0, 0):
                    for f in range(KT):
                        pe.wait_ge(*tt.taken(("xT", f)))
                    pe.wait_ge(*tt.taken(("xTs",)))
                lk, a = {"a": (("a", 0), j * P), "ag": (("a", 1), j * P), "q": (("q",), j * P), "k": (("k",), 0),
                         "ki": (("k",), P), "qi": (("k",), 2 * P + j * P)}[name]
                got(lk)
                w = slot8(lk)
                last = group(ps[:, 0:HALF], [(w[:, k, a:a + P], HT[:, k, h * HALF:h * HALF + HALF]) for k in range(KT)])
            elif kind == "kv":
                t = key[1]
                n = rows_of(t)
                for x in range(2):
                    pe.wait_ge(*mm.taken(("fm", "k", 0, x)))
                    pe.wait_ge(*mm.taken(("fm", "ki", 0, x)))
                flip(ps[0:n, 0:P], KTT[:, t * P:t * P + n])
                last = flip(ps[0:n, P:192], KIT[0:HD, t * P:t * P + n])
            elif kind == "cvp":
                pe.wait_ge(ev("glu_up"), 2 * NJ)
                for j in range(NJ):
                    last = flip(ps[0:CW - 1, j * P:j * P + P], AES[:, j, SEQ:SEQ + CW - 1])
            elif kind == "cvs":
                pe.wait_ge(ev("cvs_staged"), 1)
                for j in range(NJ):
                    last = flip(ps[0:NS, j * P:j * P + P], CVS[:, j, :])
            elif kind == "nat":
                _, what, t = key
                if what == "w":
                    pe.wait_ge(ev("w132_in"), 32)
                    last = group(ps[:, 0:NW], [(HT[:, k, t * P:t * P + P], W1[:, k, :]) for k in range(KT)])
                else:
                    got((what,))
                    w = slot8((what,))
                    last = group(ps, [(HT[:, k, t * P:t * P + P], w[:, k, :]) for k in range(KT)])
            elif kind == "lnA1":
                t = key[1]
                pe.wait_ge(ev("conv_done"), 1)
                for j in range(NJ):
                    last = flip(ps[0:rows_of(t), j * P:j * P + P], ACC[:, j, t * P:t * P + rows_of(t)])
            elif kind == "lnA2":
                t = key[1]
                n = rows_of(t)
                pe.wait_ge(*tt.taken(("lnA1", t)))
                for j in range(NJ):
                    last = flip(ps[:, j * P:j * P + n], LP[0:n, t % 2, j * P:j * P + P])
            elif kind == "mix":
                t = key[1]
                pe.wait_ge(ev("v_full"), t + 1)
                for g in range(NCG):
                    v = VN[0:rows_of(t), t, g * HD:g * HD + HD]
                    w = WS[:, g, :] if t < 4 else BD[0:NS, g, :, :].rearrange("p b t -> p (b t)")
                    last = pe.matmul(ps[0:rows_of(t), g * HD:g * HD + HD], w, v, start=True, stop=True)
            elif kind == "yc":
                t = key[1]
                n = rows_of(t)
                pe.wait_ge(ev("sgu_up"), t + 1)
                for j in range(NJ):
                    last = flip(ps[:, j * P:j * P + n], UN[0:n, t, j * P:j * P + P])
            elif kind == "dots":
                _, i, h = key
                r = slice((h % 2) * HD, (h % 2) * HD + HD)
                if (i, h) == (1, 0):
                    for x in range(2):
                        for j in range(2):
                            pe.wait_ge(*mm.taken(("fm", "qi", j, x)))
                if i != "s":
                    last = pe.matmul(ps[:, 0:P * (i + 1)], QIT[r, h // 2, i * P:i * P + P], KIT[r, 0:P * (i + 1)], start=True, stop=True)
                else:
                    if h == 0:
                        pe.wait_ge(ev("qim_ready"), 1)
                        pe.wait_ge(*tt.taken(("kit", 2)))
                        pe.wait_ge(*tt.taken(("kit", 3)))
                    group(ps[:, 0:PAST], [(QIM[r, h // 2, b, :], KTS[r, b, :]) for b in range(NB)])
                    last = pe.matmul(ps[:, PAST:PAST + NS], QI2[r, h // 2, :], KIT[r, SEQ:NTOK], start=True, stop=True)
            elif kind in ("kit", "kts"):
                g = key[1]
                if g == 0:
                    pe.wait_ge(ev("pages_in" if kind == "kit" else "kpages_in"), 16 * 16 * (3 if kind == "kit" else 1))
                for z in range(4):
                    last = flip(ps[:, z * P:z * P + P], KP[:, 4 * g + z, :])
            elif kind == "lg":
                _, i, c = key
                if i != "s":
                    if (i, c) == (0, 0):
                        for x in range(2):
                            for c2 in range(NC):
                                pe.wait_ge(*mm.taken(("fm", "q", c2, x)))
                    for n in range(NKV):
                        kk = key + (n,)
                        if at.old(kk):
                            pe.wait_ge(*at.room(kk))
                        r = slice(n * HD, n * HD + HD)
                        last = pe.matmul(at.tile(kk)[:, 0:P * (i + 1)], QT[r, c, i * P:i * P + P], KTT[r, 0:P * (i + 1)], start=True, stop=True)
                        last.then_inc(at.full_sem, 1)
                else:
                    q, qn = QMN[c % 2]
                    pe.wait_ge(ev("qm_ready"), c + 1)
                    if c == 0:
                        pe.wait_ge(*tt.taken(("kts", 2)))
                        pe.wait_ge(*tt.taken(("kts", 3)))
                    group(ps[:, 0:PAST], [(q[:, b, :], KTS[:, b, :]) for b in range(NB)])
                    last = pe.matmul(ps[:, PAST:PAST + NS], qn, KTT[:, SEQ:NTOK], start=True, stop=True)
            elif kind == "pt":
                _, i, c = key
                u = unit_no[(i, c)]
                if i != "s":
                    for n in range(NKV):
                        kk = key + (n,)
                        if tt.old(kk):
                            pe.wait_ge(*tt.room(kk))
                        pe.wait_ge(ev("probs_ready"), 2 * u + n + 1)
                        for k in range(i + 1):
                            last = flip(tt.tile(kk)[:, k * P:k * P + P], LP[:, n, k * P:k * P + P])
                        last.then_inc(tt.full_sem, 1)
                else:
                    pe.wait_ge(ev("probs_ready"), 32 + u - 15)
                    flip(ps[:, 0:P], LP[:, 0, 0:P])
                    flip(ps[:, P:2 * P], LP[:, 0, P:2 * P])
                    last = flip(ps[0:NS, 2 * P:3 * P], LP[:, 0, 2 * P:2 * P + NS])
            elif kind == "pv":
                _, i, c = key
                if i != "s":
                    for n in range(NKV):
                        pe.wait_ge(*tt.taken(("pt", i, c, n)))
                    if (i, c) == (0, 0):
                        pe.wait_ge(ev("w_biased"), NT)
                    for n in range(NKV):
                        last = group(ps[n * HD:n * HD + HD, 0:P],
                                     [(VA[:, k, n * HD:n * HD + HD], PTT[:, n, k * P:k * P + P]) for k in range(i + 1)])
                else:
                    pe.wait_ge(*tt.taken(("pt", i, c)))
                    pe.matmul(ps[:, 0:P], VA[0:NS, 4, :], PTT[0:NS, 0, 256:384], start=True, stop=False)
                    out4 = ps[:, 0:P].rearrange("p (n b t) -> p n b t", n=NKV, b=NB)
                    for b in range(NB):
                        for k in range(NPG):
                            pt4 = PTT[:, 0, k * P:k * P + P].rearrange("p (n b t) -> p n b t", n=NKV, b=NB)
                            last = pe.matmul(out4[:, :, b, :], VP[:, NPG * b + k, :], pt4[:, :, b, :], start=False, stop=(b, k) == (NB - 1, NPG - 1))
            elif kind == "gate":
                _, x, f, h = key
                lk = ("g", x, f // 4)
                got(lk)
                w = slot8(lk)
                a = (f % 4) * P
                last = group(ps[:, 0:HALF], [(w[:, k, a:a + P], HT[:, k, h * HALF:h * HALF + HALF]) for k in range(KT)])
            elif kind == "proj":
                _, x, f, h = key
                got(("p", x))
                if (f, h) == (0, 0):
                    if x == "A":
                        for t in (3, 4):
                            pe.wait_ge(*tt.taken(("lnA2", t)))
                    elif x == "C":
                        pe.wait_ge(ev("yct_up"), NT)
                    else:
                        pe.wait_ge(ev("yb_up"), 20)
                w = slot4(("p", x))
                last = group(ps[:, 0:HALF], [(w[:, k, f * P:f * P + P], YT[x][:, k, h * HALF:h * HALF + HALF]) for k in range(NJ)])
            elif kind == "wo":
                _, t, h = key
                n = rows_of(t)
                pe.wait_ge(ev("merged"), 48)
                got(("wo", h))
                w = slot8(("wo", h))
                last = group(ps[0:n], [(MG[:, k, t * P:t * P + n], w[:, k, :]) for k in range(KT)])
            elif kind == "h2T":
                _, t, h = key
                n = rows_of(t)
                pe.wait_ge(ev("h2_ready"), t + 1)
                for k in range(4):
                    last = flip(ps[:, k * P:k * P + n], H2[0:n, t % 2, (4 * h + k) * P:(4 * h + k + 1) * P])
            elif kind == "rt":
                t = key[1]
                n = rows_of(t)
                pe.wait_ge(ev("router_in"), 48)
                for h in range(2):
                    pe.wait_ge(*tt.taken(("h2T", t, h)))
                last = group(ps[0:n, 0:NE], [(H2T[:, k, 0:n], WRT[:, k, :]) for k in range(KT)])
            elif kind == "cum":
                pe.wait_ge(ev("mask_ready"), 1)
                for t in range(NT):
                    n = rows_of(t)
                    out = ps[0:n, t * NE:t * NE + NE]
                    group(out, [(ones[:, 0:n], MSK[:, s_, :]) for s_ in range(t)] + [(tri[0:n, 0:n], MSK[0:n, t, :])])
                last = group(ps[:, NT * NE:(NT + 1) * NE],
                             [(ones[0:rows_of(t)], MSK[0:rows_of(t), t, :]) for t in range(NT)])
            elif kind == "lst":
                pe.wait_ge(ev("list_in"), 16)
                last = flip(ps[0:TS, 0:NE], LSTN[0:NE, 0:TS])
            if not split:
                last.then_inc(ring_of.full_sem, 1)
            for lk in released:
                if last_use[lk] == pos[key]:
                    pe.wait_ge(ring_of.full_sem, ring_of.at[key] + 1)
                    pe.sem_inc(slot_out, 1)

        def gathered(e_next, q, p):
            pe.wait_ge(ev(f"rows_gathered{p}"), 16 * q + 16)
            if positive(e_next):
                pe.wait_ge(ev("gt_a"), e_next)
                pe.wait_ge(ev("gt_b"), e_next)
            for k in range(KT):
                last = pe.transpose(banks[2 + k // 4][:, (k % 4) * P:(k % 4) * P + TS], G[0:TS, p, k * P:k * P + P], ident[0:TS, 0:TS])
            last.then_inc(ev("gt_full"), 1)

        def down(d, dq, p):
            pe.wait_ge(ev("het_up"), d + 1)
            pe.wait_ge(ev(f"w_in{3 * p + 2}"), 16 * dq + 16)
            if positive(d):
                pe.wait_ge(ev("yo_a"), d)
                pe.wait_ge(ev("yo_b"), d)
            w = ring[3 * p + 2].rearrange("p (k n) -> p k n", k=NJ)
            group(banks[5][0:TS, :], [(HET[:, p, k, 0:TS], w[:, k, 0:512]) for k in range(NJ)])
            group(banks[6][0:TS, :], [(HET[:, p, k, 0:TS], w[:, k, 512:D]) for k in range(NJ)]).then_inc(ev("dn_full"), 1)
            pe.wait_ge(ev("dn_full"), d + 1)
            pe.sem_inc(ev(f"w_used{3 * p + 2}"), 1)

        def expert(e, q, dq, p):
            pe.wait_ge(ev("gt_a"), e + 1)
            pe.wait_ge(ev("gt_b"), e + 1)
            wg, wu = (ring[3 * p + z].rearrange("p (k n) -> p k n", k=KT) for z in range(2))
            pe.wait_ge(ev(f"w_in{3 * p}"), 16 * q + 16)
            if positive(e):
                pe.wait_ge(ev("he_ready"), e)
            group(banks[0][0:TS, :], [(HG[:, p, k, 0:TS], wg[:, k, :]) for k in range(KT)]).then_inc(ev(f"w_used{3 * p}"), 1)
            pe.wait_ge(ev(f"w_in{3 * p + 1}"), 16 * q + 16)
            group(banks[1][0:TS, :], [(HG[:, p, k, 0:TS], wu[:, k, :]) for k in range(KT)]).then_inc(ev("gu_full"), 1)
            pe.wait_ge(ev("gu_full"), e + 1)
            pe.sem_inc(ev(f"w_used{3 * p + 1}"), 1)
            if type(e) is int and e == 1:
                pe.wait_ge(ev("list2_in"), 16)
                flip(banks[7][0:TO, 0:NOV], LSTO[0:NOV, 0:TO]).then_inc(ev("list2_full"), 1)
            if type(e) is not int or e < NE - 1:
                gathered(e + 1, q + p, 1 - p)
            if positive(e):
                down(e - 1, dq, 1 - p)
            pe.wait_ge(ev("he_ready"), e + 1)
            for k in range(NJ):
                last = pe.transpose(banks[4][:, k * P:k * P + TS], HE[0:TS, p, k * P:k * P + P], ident[0:TS, 0:TS])
            last.then_inc(ev("het_full"), 1)

        gathered(0, 0, 0)
        each_expert(pe, expert)
        down(NE - 1, NE // 2 - 1, 1)
        nov = pe.value_load(ints[0:1, I_NOV:I_NOV + 1], min_val=0, max_val=NOV)

        def further(s, i, p):
            gathered(s + NE, i + NE // 2, p)
            wg, wu = (ring[3 * p + z].rearrange("p (k n) -> p k n", k=KT) for z in range(2))
            wd = ring[3 * p + 2].rearrange("p (k n) -> p k n", k=NJ)
            he = further_hidden(p)
            pe.wait_ge(ev("gt_a"), s + NE + 1)
            pe.wait_ge(ev("gt_b"), s + NE + 1)
            pe.wait_ge(ev("he_ready"), s + NE)
            for z, (bank, w) in enumerate(((banks[0], wg), (banks[1], wu))):
                pe.wait_ge(ev(f"w_in{3 * p + z}"), 16 * (i + NE // 2 + 1))
                for j in range(NJ):
                    last = group(bank[:, j * TO:j * TO + TO], [(w[:, k, j * P:j * P + P], HG[:, p, k, 0:TO]) for k in range(KT)])
                last.then_inc(ev(f"w_used{3 * p}") if z == 0 else ev("gu_full"), 1)
            pe.wait_ge(ev("gu_full"), s + NE + 1)
            pe.sem_inc(ev(f"w_used{3 * p + 1}"), 1)
            pe.wait_ge(ev("he_ready"), s + NE + 1)
            pe.wait_ge(ev(f"w_in{3 * p + 2}"), 16 * (i + NE // 2 + 1))
            pe.wait_ge(ev("yo_a"), s + NE)
            pe.wait_ge(ev("yo_b"), s + NE)
            group(banks[5][0:TO, :], [(he[:, k, :], wd[:, k, 0:512]) for k in range(NJ)])
            group(banks[6][0:TO, :], [(he[:, k, :], wd[:, k, 512:D]) for k in range(NJ)]).then_inc(ev("dn_full"), 1)
            pe.wait_ge(ev("dn_full"), s + NE + 1)
            pe.sem_inc(ev(f"w_used{3 * p + 2}"), 1)
        each_further(pe, nov, further)


def buckets():
    n = np.maximum(TABLE_END - np.arange(SLEN), 0)
    exact = NBUCK // 2
    nf = np.maximum(n, 1).astype(np.float32)
    large = exact + (np.log(nf / np.float32(exact)) / np.float32(math.log(MAXD / exact)) * (NBUCK - exact)).astype(np.int32)
    b = np.where(n < exact, n, np.minimum(large, NBUCK - 1))
    return (np.arange(NBUCK)[:, None] == b[None, :]).astype(np.float32)


def constants():
    c = np.zeros((P, K_ALL), np.float32)
    p, f = np.arange(P)[:, None], np.arange(P)[None, :]
    c[:, K_ID:K_ID + P] = p == f
    c[:, K_PEN:K_PEN + P] = np.where(f <= p, 0.0, NEG)
    c[:, K_TRI:K_TRI + P] = p <= f
    c[:, K_ONE:K_ONE + P] = 1.0
    row, col = p % NS, np.arange(NS)[None, :]
    c[:, K_PENS:K_PENS + NS] = np.where((row // ST == col // ST) & (col <= row), 0.0, NEG)
    c[0:ST, K_E8:K_E8 + P] = np.arange(ST)[:, None] == f % ST
    c[:, K_BLK:K_BLK + NB] = row // ST == np.arange(NB)[None, :]
    c[:, K_SLOT:K_SLOT + NE] = np.arange(NE)[None, :] * TS - 1.0
    c[:, K_TOK:K_TOK + NT] = p + P * np.arange(NT)[None, :]
    c[:, K_STEP:K_STEP + NOV] = np.arange(NOV)[None, :]
    c[:, K_N:K_N + NE * NE] = (np.arange(NE)[:, None] > np.arange(NE)[None, :]).reshape(1, -1)
    c[:, K_N + NE * NE:] = TS + TO * np.arange(MORE)[None, :]
    return c


INPUTS = ["x_prompt", "x_sample", "cache_k", "cache_v", "cache_kidx", "state_conv", "page_table", "c_prompt", "c_sample",
          "w_ada", "b_ada", "w_in", "b_in", "conv_k", "conv_b", "lnA_g", "lnA_b", "lnC_g", "lnC_b", "w_s", "b_s",
          "w_pa", "w_pb", "w_pc", "w_o", "ln1_g", "ln1_b", "ln2_g", "ln2_b", "rel_table", "w_router", "router_bias",
          "w_e_gate", "w_e_up", "w_e_down"]
OUTPUTS = [("y_prompt", (1, SEQ, D)), ("y_sample", (NB, ST, D)),
           ("new_k_prompt", (1, 1, SEQ, NKV, HD)), ("new_v_prompt", (1, 1, SEQ, NKV, HD)), ("new_kidx_prompt", (1, 1, SEQ, HD)),
           ("new_conv_prompt", (1, 1, CW - 1, DA)),
           ("new_k_sample", (1, NB, ST, NKV, HD)), ("new_v_sample", (1, NB, ST, NKV, HD)), ("new_kidx_sample", (1, NB, ST, HD)),
           ("new_conv_sample", (1, NB, CW - 1, DA)), ("new_vchunk_sample", (1, NB, ST, 512))]


def kernel(**inputs):
    import concourse.bacc as bacc
    from concourse.bass_utils import run_bass_kernel_spmd

    nc = bacc.Bacc("TRN2", target_bir_lowering=False, num_devices=1)
    arrays, I, O = {}, {}, {}
    for name in INPUTS:
        a = np.ascontiguousarray(inputs[name])
        if name == "router_bias":
            a = a.reshape(1, -1)
        arrays["in_" + name] = a
        I[name] = nc.dram_tensor("in_" + name, a.shape, mybir.dt.from_np(a.dtype), kind="ExternalInput").ap()
    for name, a in (("constants", constants()), ("buckets", buckets())):
        arrays[name] = a
        I[name] = nc.dram_tensor(name, a.shape, F32, kind="ExternalInput").ap()
    for name, shape in OUTPUTS:
        O[name] = nc.dram_tensor(name, shape, F32, kind="ExternalOutput").ap()
    build(nc, I, O, I["constants"], I["buckets"])
    r = run_bass_kernel_spmd(nc, [arrays], core_ids=[0])
    return tuple(r.results[0][name] for name, _ in OUTPUTS)
```

```python
import math
from contextlib import ExitStack

import numpy as np
import concourse.bass as bass
from concourse import mybir

F32 = mybir.dt.float32
I32 = mybir.dt.int32
ALU = mybir.AluOpType
ACT = mybir.ActivationFunctionType
AX = mybir.AxisListType

P = 128
D = 1024
KT = D // P
SEQ, NB, ST = 512, 8, 8
NS = NB * ST
NTOK = SEQ + NS
NT = 5
HALF = NTOK // 2
PAST, PAGE, NPOOL = 256, 128, 20
NPG = PAST // PAGE
DA, CW = 512, 31
NJ = DA // P
NKV, HD, NC = 2, 64, 4
NBUCK, MAXD = 32, 128
NCG, CHUNK = 8, 128
NE, NG, DE = 16, 4, 512
TOPK_P, TOPK_S = 128, 66
ALPHA = 2.0 ** 0.25
EPS = 1e-5
SLEN = 640
TABLE_END = 511
NEG, REPL, SELD = -1e30, -3e38, -2e38
BIG = 1e30
TS = 128
MORE = -(-(NTOK - TS) // TS)
NOV = 2 * NTOK // TS - 1
NHI = NE + NOV
FAR_ROWS = NE * TS
SLOTS = NHI * TS
FAR = 65536.0

C_A, C_AG, C_Q, C_K, C_V, C_QI, C_KI, C_WI, C_U, C_VV, C_G = 0, 512, 1024, 1536, 1664, 1792, 2048, 2112, 2116, 2628, 3140
D_IN = 6212
NW = 132

R_A, R_Q, R_K, R_QI, R_KI, R_G, R_CB, R_LG, R_LB, R_BS, NR = 0, 8, 12, 13, 15, 16, 40, 44, 48, 52, 60

K_ID, K_PEN, K_TRI, K_ONE, K_PENS, K_E8, K_BLK, K_SLOT, K_TOK, K_STEP, K_N = 0, 128, 256, 384, 512, 576, 704, 712, 728, 736, 744

R_LT, R_THR, R_HI, R_LO = 0, NE * NE, NE * NE + MORE, NE * NE + MORE + NHI + 1
R_ALL = R_LO + TS
K_ALL = K_N + R_ALL

SLOT = 4096
A_CON = 0
A_RING = K_N
A_MG = A_RING + 3 * SLOT
A_HT = A_MG + 8 * NTOK
A_YA = A_HT + KT * 640
A_YB = A_YA + NJ * NTOK
A_YC = A_YB + NJ * NTOK
A_W = A_YC + NJ * NTOK
A_AE = A_W + KT * NW
EXT = 30 + SEQ + NB * (30 + ST)
A_UN = A_AE + NJ * EXT
A_VN = A_UN + NT * 512
A_QK = A_VN + NT * 512
A_WS = A_QK + 8 * NTOK
A_BD = A_WS + NCG * P
A_VA = A_BD + NCG * NS
A_PAR = A_VA + NT * P
A_CK = A_PAR + 2 * NR
A_MT = A_CK + NJ * CW
A_CT = A_MT + 16 * 9
A_SC = A_CT + KT * 9
A_PEN = A_SC + 512
A_BM = A_PEN + 256 + 384 + 512 + 320
A_LP = A_BM + 1024
A_PT = A_LP + 1024
A_GT = A_PT + 1024
A_SM = A_GT + 4 * HALF + 70
A_END = A_SM + 164
A_X = A_UN
A_WSN = A_MG
A_STN = A_WSN + 1024
A_CN = A_STN + 1024
A_CKN = A_CN + 1024
A_PRN = A_CKN + 512
A_TAB = A_BM
A_OH = A_LP
A_REL = A_PRN + 128
A_MOD = A_YC
A_BB = A_YB
A_KP = A_AE
A_KTS = A_KP + 16 * P
A_QM = A_KTS + NB * PAST
A_VP = A_QM + 2 * (NB * P + P)
A_RING2 = A_HT
A_BC = A_AE
A_X1 = A_BC + 8 * D
A_XR = A_X1 + NT * D
A_R = A_XR + 2 * D
A_H2 = A_R + 2 * D
A_H2T = A_H2 + 2 * D
A_RO = A_H2T + D
assert A_VP + 16 * P <= A_QK and A_RING2 + 3 * SLOT <= A_AE and A_RO + 1119 + R_ALL <= A_SM and A_OH + SLEN <= A_PT
A_G = A_BC
A_HG = A_G + 2 * D
A_HE = A_HG + 2 * D
A_HET = A_HE + 2 * DE
A_Y = A_HET + 2 * DE
A_GA = A_RING
A_BC2 = A_XR
A_O = A_H2


def make_plan():
    plan = [("cT",), ("ada", 0), ("ada", 1), ("mT", 0), ("ada", 2), ("mT", 1), ("ada", 3), ("mT", 2), ("ck",), ("mT", 3), ("par",)]
    plan += [("xT", f) for f in range(KT)] + [("xTs",)]
    plan += [("ws", 0), ("ws", 1), ("st", 0), ("st", 1), ("oh", 0), ("oh", 1), ("bd",)]
    for name, chunks in ((("ag", "a"), range(NJ)), (("q",), range(NC))):
        plan += [("fm", n, j, h) for j in chunks for n in name for h in range(2)]
    plan += [("ada", 4)]
    plan += [("fm", n, j, h) for n, j in (("k", 0), ("ki", 0), ("qi", 0), ("qi", 1)) for h in range(2)]
    plan += [("ada", 5), ("cvp",), ("ada", 6), ("cvs",)]
    for t in range(NT):
        plan += [("nat", "w", t)] + ([("kv", t // 2)] if t % 2 == 0 else [])
    plan += [("nat", "v", 0), ("kv", 3), ("nat", "v", 1), ("kv", 4), ("ada", 7), ("nat", "v", 2), ("nat", "v", 3), ("ada", 8)]
    plan += [("nat", "v", 4), ("lnA1", 0), ("nat", "u", 0), ("lnA1", 1), ("nat", "u", 1), ("lnA2", 0), ("ada", 9)]
    plan += [("lnA1", 2), ("lnA2", 1), ("nat", "u", 2), ("mix", 0), ("lnA1", 3), ("lnA2", 2), ("ada", 10)]
    plan += [("nat", "u", 3), ("mix", 1), ("lnA1", 4), ("lnA2", 3), ("ada", 11), ("nat", "u", 4), ("lnA2", 4), ("yc", 0), ("mix", 2), ("yc", 1), ("mix", 3), ("yc", 2)]
    sides = {n: [] for n in range(32)}

    def unit(at, i, c):
        sides[at] += [("lg", i, c)]
        sides[at + 1] += [("pt", i, c)]
        sides[at + 2] += [("pv", i, c)]

    def dots(at, i):
        sides[at] += [("dots", i, 0), ("dots", i, 1)]
        sides[at + 1] += [("dots", i, 2), ("dots", i, 3)]

    def pick(at, i, a, b):
        sides[at] += [("tk", i, a, b)]
    sides[0] += [("mix", 4), ("yc", 3)]
    sides[1] += [("yc", 4)]
    dots(1, 1)
    for c in range(NC):
        unit(3 + c, 0, c)
        pick(3 + c, 1, 4 * c, 4 * c + 4)
    dots(7, 2)
    for c in range(NC):
        unit(7 + c, 1, c)
    for n in range(5):
        pick(8 + n, 2, 3 * n, 3 * n + 3 if n < 4 else 16)
    dots(12, 3)
    for c in range(NC):
        unit(13 + c, 2, c)
    for n in range(5):
        pick(14 + n, 3, 3 * n, 3 * n + 3 if n < 4 else 16)
    for c in range(NC):
        unit(19 + c, 3, c)
    sides[15] = [("kit", g) for g in range(4)] + sides[15]
    for h in range(4):
        sides[19 + h] += [("dots", "s", h)]
    pick(23, "s", 0, 5)
    pick(24, "s", 5, (TOPK_S + 6) // 8)
    sides[22] += [("kts", 0), ("kts", 1)]
    sides[23] += [("kts", 2), ("kts", 3)]
    for c in range(NC):
        at = 24 + 2 * c
        sides[at] += [("lg", "s", c)]
        sides[at + 1] += [("pt", "s", c)]
        if c < NC - 1:
            sides[at + 2] += [("pv", "s", c)]
    return plan, sides


def full_plan():
    plan, sides = make_plan()
    n = 0
    for x in "AC":
        for f in range(KT):
            for h in range(2):
                plan += [("gate", x, f, h), ("proj", x, f, h)] + sides[n]
                n += 1
    for f in range(KT):
        for h in range(2):
            plan += [("gate", "B", f, h)] + ([("pv", "s", NC - 1)] if (f, h) == (0, 0) else []) + [("proj", "B", f, h)]
    for t in range(NT):
        plan += [("wo", t, 0)]
        if t >= 2:
            plan += [("rt", t - 2)]
        plan += [("wo", t, 1)]
        if t:
            plan += [("h2T", t - 1, 0), ("h2T", t - 1, 1)]
    plan += [("rt", 3), ("h2T", 4, 0), ("h2T", 4, 1), ("rt", 4), ("cum",), ("lst",)]
    return plan


def load_plan():
    w = [("ada", n) for n in range(4)] + [("a", 0), ("a", 1), ("q",), ("ada", 4), ("k",), ("ada", 5), ("ada", 6), ("v",)]
    w += [("ada", 7), ("ada", 8), ("ada", 9), ("u",), ("ada", 10), ("ada", 11)]
    for x in "ACB":
        w += [("g", x, 0), ("p", x), ("g", x, 1)]
    return w + [("wo", 0), ("wo", 1)]


class Banks:

    def __init__(self, tiles, keys, full, free):
        self.tiles, self.full_sem, self.free_sems = tiles, full, free
        self.at = {k: n for n, k in enumerate(keys)}

    def tile(self, key):
        return self.tiles[self.at[key] % len(self.tiles)]

    def old(self, key):
        return self.at[key] >= len(self.tiles)

    def room(self, key):
        n, b = self.at[key], len(self.tiles)
        return self.free_sems[n % b], n // b

    def full(self, key):
        return self.full_sem, self.at[key] + 1

    def free(self, key):
        return self.free_sems[self.at[key] % len(self.tiles)]

    def taken(self, key):
        n, b = self.at[key], len(self.tiles)
        return self.free_sems[n % b], n // b + 1


class Steps:

    def __init__(self, eng, sem):
        self.eng, self.sem, self.n = eng, sem, 0

    def done(self, ins):
        ins.then_inc(self.sem, 1)
        self.n += 1
        return self.n

    def need(self, n=None):
        self.eng.wait_ge(self.sem, self.n if n is None else n)

    def link(self, ins):
        self.done(ins)
        self.need()


def build(nc, I, O, con_d, oh_d):
    tab_d = nc.dram_tensor("tables", [8, P, SLEN], F32).ap()
    mod_d = nc.dram_tensor("mod", [9, 6 * D], F32).ap()
    h2_d = nc.dram_tensor("h2", [NTOK, D], F32).ap()
    y_d = nc.dram_tensor("expert_rows", [SLOTS, D], F32).ap()
    with ExitStack() as ctx:
        build_in(nc, ctx, I, O, con_d, oh_d, tab_d, mod_d, h2_d, y_d)


def build_in(nc, ctx, I, O, con_d, oh_d, tab_d, mod_d, h2_d, y_d):
    arena = ctx.enter_context(nc.sbuf_tensor("arena", [P, A_END], F32))
    ints = ctx.enter_context(nc.sbuf_tensor("ints", [P, 64], I32))
    sem = lambda name: ctx.enter_context(nc.semaphore(name))

    def V(at, *dims):
        n = int(np.prod(dims))
        v = arena[:, at:at + n]
        if len(dims) == 2:
            v = v.rearrange("p (a b) -> p a b", b=dims[1])
        elif len(dims) == 3:
            v = v.rearrange("p (a b c) -> p a b c", b=dims[1], c=dims[2])
        elif len(dims) == 4:
            v = v.rearrange("p (a b c d) -> p a b c d", b=dims[1], c=dims[2], d=dims[3])
        return v

    con = V(A_CON, K_N)
    ident = con[:, K_ID:K_ID + P]
    tri = con[:, K_TRI:K_TRI + P]
    ones = con[:, K_ONE:K_ONE + P]
    ring = [V(A_RING + s * SLOT, SLOT) for s in range(3)] + [V(A_RING2 + s * SLOT, SLOT) for s in range(3)]
    MG = V(A_MG, KT, NTOK)
    HT = V(A_HT, KT, 640)
    YT = {"A": V(A_YA, NJ, NTOK), "B": V(A_YB, NJ, NTOK), "C": V(A_YC, NJ, NTOK)}
    ACC = YT["A"]
    W1 = V(A_W, KT, NW)
    TMP = V(A_W, 512)
    AE = V(A_AE, NJ, EXT)
    AES = arena[:, A_AE:A_AE + NJ * EXT].rearrange("p (j x) -> p j x", x=EXT)
    UN, VN = V(A_UN, NT, 512), V(A_VN, NT, 512)
    QT, KTT, QIT, KIT = V(A_QK, NC, NTOK), V(A_QK + 4 * NTOK, NTOK), V(A_QK + 5 * NTOK, 2, NTOK), V(A_QK + 7 * NTOK, NTOK)
    WS, BD, VA = V(A_WS, NCG, P), V(A_BD, NCG, NB, ST), V(A_VA, NT, P)
    PAR, PARH = V(A_PAR, NR), V(A_PAR + NR, NR)
    CK, MT, CT = V(A_CK, NJ, CW), V(A_MT, 16, 9), V(A_CT, KT, 9)
    SC = V(A_SC, 512)
    PEN = {0: con[:, K_PEN:K_PEN + P], 1: V(A_PEN, 256), 2: V(A_PEN + 256, 384), 3: V(A_PEN + 640, 512), "s": V(A_PEN + 1152, 320)}
    BM, LP, PTT = V(A_BM, 2, 512), V(A_LP, 2, 512), V(A_PT, 2, 512)
    GT, PJ = V(A_GT, 2, HALF), V(A_GT + 2 * HALF, 2, HALF)
    sm = lambda o, n: arena[:, A_SM + o:A_SM + o + n]
    WI, MX8, STAT, MV, RSTD, NEGM, RSUM, RINV = sm(0, 20), sm(20, 8), sm(28, 12), sm(40, 2), sm(42, 1), sm(43, 2), sm(45, 2), sm(47, 2)
    VEPS, HALFN, BS2 = sm(49, 1), sm(50, 1), sm(51, 8)
    X = V(A_X, NT, D)
    WSN, STN, CN, CKN, PRN = V(A_WSN, NCG, P), V(A_STN, 2, 512), V(A_CN, D), V(A_CKN, 512), V(A_PRN, P)
    TAB, OH, REL = V(A_TAB, SLEN), V(A_OH, SLEN), V(A_REL, 8)
    CVS = V(A_BM + 768, NJ, NS)
    MOD, BAD = V(A_MOD, 2, 512), V(A_MOD + 1024, 2, 512)
    mod_buf = lambda n: V(A_GT, 2, 512)[0:9, n - 2, :] if n in (2, 3) else MOD[0:9, n % 2, :]
    bada_buf = lambda n: PTT[0:9, n - 2, :] if n in (2, 3) else BAD[0:9, n % 2, :]
    bada_in = lambda n: (f"bada_in{n}" if n < 4 else f"bada_in{n % 2}", 16 if n < 4 else 16 * (n // 2))
    BB = V(A_BB, 512 + 512 + NW + 1024)
    KP, VP, KTS = V(A_KP, 16, P), V(A_VP, 16, P), V(A_KTS, NB, PAST)
    QIM = V(A_QM, 2, NB, P)
    QI2 = V(A_QM + 2 * NB * P, 2, P)
    QMN = [(V(A_QM + z * 1152, NB, P), V(A_QM + z * 1152 + 1024, P)) for z in range(2)]
    BC = {n: V(A_BC + k * D, D) for k, n in enumerate(["g1p", "g1s", "scp", "scs", "shp", "shs", "lg", "lb"])}
    X1, XR, R, H2, H2T = V(A_X1, NT, D), V(A_XR, 2, D), V(A_R, 2, D), V(A_H2, 2, D), V(A_H2T, KT, P)
    r0 = A_RO
    TH, SEL, MSK, GATE = (V(r0 + k * 80, NT, NE) for k in range(4))
    PSUMS, GS, GBUF, GRES = V(r0 + 320, 20, 6), V(r0 + 440, 20), V(r0 + 460, NT, 11), V(r0 + 515, NT, 11)
    SBUF_, SRES = V(r0 + 570, NT, 22), V(r0 + 680, NT, 22)
    RB, SUM5, SA, SB_, WGA, WGB = V(r0 + 790, 16), V(r0 + 806, 5), V(r0 + 811, 5), V(r0 + 816, 5), V(r0 + 821, 5), V(r0 + 826, 5)
    SLM, EQ = V(r0 + 831, NT, NE), V(r0 + 911, NT, NE)
    WRT = V(r0 + 991, KT, NE)
    CNT, OVER, BEFORE, TEXP = sm(92, 16), sm(108, 16), sm(124, 16), sm(140, 16)
    MV2, RSTD2, VAR2 = sm(156, 4).rearrange("p (z n) -> p z n", n=2), sm(160, 2), sm(162, 2)
    RCON = V(r0 + 1119, R_ALL)
    OHL, GE, OHH = V(A_XR, 2 * NT, TS), V(A_XR + 2 * NT * TS, 2 * NT, NHI + 1), V(A_XR + 2 * NT * (TS + NHI + 1), 2 * NT, NHI)
    SAB, HIS = V(r0 + 811, 2 * NT), V(A_XR + 2 * NT * (TS + 2 * NHI + 1), 2 * NT)
    CMP = V(A_H2T, NE, NE)
    ZERO = V(A_MG + 4 * D, 512)
    GMK = sm(62, 20)
    GM8 = sm(84, 8)
    I_PG, I_SA, I_SB, I_L, I_NOV, I_E = 0, 16, 21, 26, 50, 52
    G, HG, HE, HET, YO = V(A_G, 2, D), V(A_HG, 2, KT, P), V(A_HE, 2, DE), V(A_HET, 2, 4, P), V(A_Y, 2, D)
    GAT, BC2, OUT = V(A_GA, 2 * NT, D), V(A_BC2, 4, D), V(A_O, 2, D)

    banks = [ctx.enter_context(nc.psum_tensor(f"bank{b}", [P, 512], F32))[:, :] for b in range(8)]
    plan = full_plan()
    kinds = {"ada": "M", "fm": "M", "nat": "M", "gate": "M", "proj": "M", "wo": "M",
             "par": "T", "ck": "T", "ws": "T", "st": "T", "cT": "T", "mT": "T", "xT": "T", "xTs": "T", "kv": "T", "cvp": "T",
             "cvs": "T", "lnA1": "T", "lnA2": "T", "yc": "T", "pt": "T", "kit": "T", "kts": "T", "h2T": "T", "lst": "T",
             "bd": "A", "oh": "A", "mix": "A", "dots": "A", "lg": "A", "pv": "A", "rt": "A", "cum": "A", "tk": None}

    def keys_of(kind):
        out = []
        for s in plan:
            if kinds[s[0]] != kind:
                continue
            two = s[0] == "pt" and s[1] != "s" or s[0] == "lg" and s[1] != "s"
            out += [s + (0,), s + (1,)] if two else [s]
        return out

    mm = Banks(banks[0:3], keys_of("M"), sem("mm_full"), [sem(f"mm_free{b}") for b in range(3)])
    tt = Banks(banks[3:5], keys_of("T"), sem("t_full"), [sem(f"t_free{b}") for b in range(2)])
    at = Banks(banks[5:8], keys_of("A"), sem("at_full"), [sem(f"at_free{b}") for b in range(3)])

    loads = load_plan()
    index = {k: n for n, k in enumerate(loads)}
    slot_in = [sem(f"slot_in{s}") for s in range(3)]
    slot_out = sem("slot_out")
    parts = {("q",): 8, ("k",): 4, ("p", "B"): 2}
    arrived_at, total = {}, [0, 0, 0]
    for n, k in enumerate(loads):
        total[n % 3] += 16 * parts.get(k, 1)
        arrived_at[k] = (slot_in[n % 3], total[n % 3])
    released = [k for k in loads if k[0] in ("ada", "a", "q", "k", "v", "u")]
    for x in "ACB":
        released += [("g", x, 0), ("g", x, 1), ("p", x)]
    released += [("wo", 0), ("wo", 1)]
    rel = {k: n + 1 for n, k in enumerate(released)}
    wslot = lambda k: ring[index[k] % 3]


    def quarter_tiles(bank):
        return bank.rearrange("p (k n) -> p k n", n=P)

    def positive(x):
        return type(x) is not int or x > 0

    def each_expert(eng, one):
        for e in range(3):
            one(e, e // 2, (e - 1) // 2, e % 2)
        with eng.Fori(1, NE // 2 - 1) as i:
            one(2 * i + 1, i, i, 1)
            one(2 * i + 2, i + 1, i, 0)
        one(NE - 1, NE // 2 - 1, NE // 2 - 1, 1)

    def each_further(eng, nov, one):
        with eng.If(nov > 0):
            with eng.Fori(0, NOV // 2) as i:
                for p in range(2):
                    with eng.If(nov > 2 * i + p):
                        one(2 * i + p, i, p)

    named = {}

    def ev(name):
        if name not in named:
            named[name] = sem(name)
        return named[name]

    pos = {k: n for n, k in enumerate(plan)}
    pairs = [(x, f, h) for x in "ACB" for f in range(KT) for h in range(2)]
    pair_no = {k: n for n, k in enumerate(pairs)}
    units = [(i, c) for i in range(4) for c in range(NC)] + [("s", c) for c in range(NC)]
    unit_no = {u: n for n, u in enumerate(units)}
    glu_no = {(j, h): 2 * j + h for j in range(NJ) for h in range(2)}
    rows_of = lambda t: P if t < 4 else NS
    block = ctx.enter_context(nc.Block())

    def diagonal(at, row, rows):
        v = arena[row:row + rows, at:at + (NB - 1) * (P + ST) + ST]
        return bass.AP(v.tensor, v.offset, [list(v.ap[0]), [P + ST, NB], [1, ST]])

    def w_in_cols(a, b):
        return I["w_in"][0][:, a:b].rearrange("(k p) n -> p k n", p=P)

    def load_weights(sp, n):
        key = loads[n]
        slot, inc = ring[n % 3], slot_in[n % 3]
        if n >= 3:
            sp.wait_ge(slot_out, rel[loads[n - 3]])
        kn = slot.rearrange("p (k n) -> p k n", k=KT)
        if key[0] == "ada":
            sp.dma_start(kn, I["w_ada"][0][:, 512 * key[1]:512 * key[1] + 512].rearrange("(k p) n -> p k n", p=P)).then_inc(inc, 16)
        elif key[0] == "a":
            sp.dma_start(kn, w_in_cols(512 * key[1], 512 * key[1] + 512)).then_inc(inc, 16)
        elif key[0] == "q":
            for c in range(NC):
                for n2 in range(NKV):
                    a = C_Q + n2 * 256 + c * HD
                    sp.dma_start(kn[:, :, c * P + n2 * HD:c * P + n2 * HD + HD], w_in_cols(a, a + HD)).then_inc(inc, 16)
        elif key[0] == "k":
            sp.dma_start(kn[:, :, 0:128], w_in_cols(C_K, C_K + 128)).then_inc(inc, 16)
            sp.dma_start(kn[:, :, 128:192], w_in_cols(C_KI, C_KI + 64)).then_inc(inc, 16)
            sp.dma_start(kn[:, :, 192:256], w_in_cols(C_KI, C_KI + 64)).then_inc(inc, 16)
            sp.dma_start(kn[:, :, 256:512], w_in_cols(C_QI, C_QI + 256)).then_inc(inc, 16)
        elif key[0] in "uv":
            a = C_U if key[0] == "u" else C_VV
            sp.dma_start(kn, w_in_cols(a, a + 512)).then_inc(inc, 16)
        elif key[0] == "g":
            a = C_G + "ABC".index(key[1]) * D + 512 * key[2]
            sp.dma_start(kn, w_in_cols(a, a + 512)).then_inc(inc, 16)
        elif key[0] == "p":
            w = I["w_p" + key[1].lower()][0]
            kf = slot.rearrange("p (k n) -> p k n", k=NJ)
            if key[1] == "B":
                for n2 in range(NKV):
                    sp.dma_start(kf[n2 * HD:n2 * HD + HD], w[n2 * 256:n2 * 256 + 256, :].rearrange("(c d) f -> d c f", d=HD)).then_inc(inc, 16)
            else:
                sp.dma_start(kf, w.rearrange("(k p) n -> p k n", p=P)).then_inc(inc, 16)
        else:
            sp.dma_start(kn, I["w_o"][0][:, 512 * key[1]:512 * key[1] + 512].rearrange("(k p) n -> p k n", p=P)).then_inc(inc, 16)

    def load_bias(act, i, c):
        t = tab_d.tensor
        if i != "s":
            k = P * (i + 1)
            for n in range(NKV):
                src = bass.AP(t, (4 * n + c) * P * SLEN + P - 1 + 384 - P * i, [[SLEN - 1, P], [1, k]])
                act.dma_start(BM[:, n, 0:k], src).then_inc(ev("bias_in"), 16)
        else:
            for n in range(NKV):
                rows = BM[n * NS:n * NS + NS, 0, :]
                h0 = (4 * n + c) * P * SLEN + TABLE_END
                act.dma_start(rows[:, 0:PAST], bass.AP(t, h0 - PAST, [[0, NB], [SLEN - 1, ST], [1, PAST]])).then_inc(ev("bias_in"), 16)
                act.dma_start(rows[:, PAST:PAST + ST], bass.AP(t, h0, [[0, NB], [SLEN - 1, ST], [1, ST]])).then_inc(ev("bias_in"), 16)

    bias_need = {}
    total_bias = 0
    for u_ in units:
        total_bias += 32 if u_[0] != "s" else 64
        bias_need[u_] = total_bias

    last_use = {}
    for k in plan:
        if k[0] in ("ada", "wo"):
            last_use[k[:2] if k[0] == "ada" else ("wo", k[2])] = pos[k]
        elif k[0] == "fm":
            last_use[("a", 0) if k[1] in ("a", "ag") else ("q",) if k[1] == "q" else ("k",)] = pos[k]
        elif k[0] == "nat" and k[1] in "uv":
            last_use[(k[1],)] = pos[k]
        elif k[0] == "gate":
            last_use[("g", k[1], k[2] // 4)] = pos[k]
        elif k[0] == "proj":
            last_use[("p", k[1])] = pos[k]
    last_use[("a", 1)] = last_use[("a", 0)]
    released.sort(key=lambda k: last_use[k])
    rel.update({k: n + 1 for n, k in enumerate(released)})
    sp_order = [(last_use[loads[n - 3]] if n >= 3 else -3 + n, "ring", n) for n in range(len(loads))]
    sp_order += [(pos[("gate", "A", 3 + g, 0)] + 0.6, "pages", g) for g in range(4)]
    sp_order += [(pos[("kit", 3)] + 0.6 + 0.01 * g, "kpages", g) for g in range(4)]
    sp_order += [(pos[("pv", "s", NC - 1)] + 0.6, "rows", 0)]
    sp_order.sort(key=lambda x: x[0])

    def expert_weights(sp, e, z):
        name, k = [("w_e_gate", KT), ("w_e_up", KT), ("w_e_down", NJ)][z % 3]
        w = I[name][0]
        w = w[e] if type(e) is int else w[bass.ds(e, 1)].rearrange("e k n -> (e k) n")
        sp.dma_start(ring[z].rearrange("p (k n) -> p k n", k=k), w.rearrange("(k p) n -> p k n", p=P)).then_inc(ev(f"w_in{z}"), 16)

    @block.sync
    def _(sp):
        sp.dma_start(CN[0:1, :], I["c_prompt"]).then_inc(ev("c_in"), 16)
        sp.dma_start(CN[1:9, :], I["c_sample"]).then_inc(ev("c_in"), 16)
        sp.dma_start(con, con_d[:, 0:K_N]).then_inc(ev("consts"), 16)
        sp.dma_start(ints[0:1, I_PG:I_PG + 16], I["page_table"].rearrange("b g -> (b g)").unsqueeze(0)).then_inc(ev("page_ids"), 16)
        sp.dma_start(O["new_conv_sample"][0, :, 0:CW - 1 - ST, :], I["state_conv"][0, :, ST:CW - 1, :]).then_inc(ev("state_out"), 16)
        def load_rows():
            sp.wait_ge(ev("mod_out0"), 16 * 6)
            sp.wait_ge(ev("mod_out1"), 16 * 6)
            sp.wait_ge(ev("yb_up"), 20)

            def mod_rows(cols):
                return (mod_d[0:1, cols:cols + D].partition_broadcast(P),
                        bass.AP(mod_d.tensor, 6 * D + cols, [[6 * D, NB], [0, ST], [1, D]]))
            for name, cols in (("g1", 2 * D), ("sc", 4 * D), ("sh", 3 * D)):
                whole, samples = mod_rows(cols)
                sp.dma_start(BC[name + "p"], whole).then_inc(ev("rows_in"), 16)
                sp.dma_start(BC[name + "s"][0:NS], samples).then_inc(ev("rows_in"), 16)
            sp.dma_start(BC["lg"], I["ln1_g"].partition_broadcast(P)).then_inc(ev("rows_in"), 16)
            sp.dma_start(BC["lb"], I["ln1_b"].partition_broadcast(P)).then_inc(ev("rows_in"), 16)

        for _, what, n in sp_order:
            if what == "ring":
                if n == 4:
                    for t in range(NT):
                        src = I["x_prompt"][0, t * P:t * P + P, :] if t < 4 else I["x_sample"].rearrange("b t f -> (b t) f")
                        sp.dma_start(X[0:rows_of(t), t, :], src).then_inc(ev("x_in"), 16)
                    sp.dma_start(W1[:, :, 0:128], w_in_cols(C_V, C_V + 128)).then_inc(ev("w132_in"), 16)
                    sp.dma_start(W1[:, :, 128:132], w_in_cols(C_WI, C_WI + 4)).then_inc(ev("w132_in"), 16)
                load_weights(sp, n)
            elif what == "pages":
                if n == 0:
                    sp.wait_ge(ev("yct_up"), NT)
                    sp.wait_ge(ev("vchunk_out"), 16)
                    sp.wait_ge(ev("page_ids"), 16)
                with sp.Fori(4 * n, 4 * n + 4) as g:
                    page = sp.value_load(ints[0:1, bass.ds(g, 1)], min_val=0, max_val=NPOOL - 1)
                    sp.dma_start(arena[:, bass.ds(g * P + A_KP, P)].rearrange("p (z d) -> p z d", z=2),
                                 I["cache_kidx"][0, bass.ds(page, 1)].rearrange("a s d -> (a s) d").unsqueeze(1).broadcast_to([P, 2, HD])).then_inc(ev("pages_in"), 16)
                    sp.dma_start(arena[:, bass.ds(g * P + A_VP, P)],
                                 I["cache_v"][0, bass.ds(page, 1)].rearrange("a s n d -> (a s) (n d)")).then_inc(ev("pages_in"), 16)
            elif what == "rows":
                load_rows()
            else:
                if n == 0:
                    sp.wait_ge(*tt.full(("kit", 3)))
                with sp.Fori(4 * n, 4 * n + 4) as g:
                    page = sp.value_load(ints[0:1, bass.ds(g, 1)], min_val=0, max_val=NPOOL - 1)
                    sp.dma_start(arena[:, bass.ds(g * P + A_KP, P)],
                                 I["cache_k"][0, bass.ds(page, 1)].rearrange("a s n d -> (a s) (n d)")).then_inc(ev("kpages_in"), 16)
        sp.wait_ge(ev("merged"), 48)
        sp.dma_start(WRT, I["w_router"].rearrange("(k p) e -> p k e", p=P)).then_inc(ev("router_in"), 16)
        sp.dma_start(RCON, con_d[:, K_N:K_ALL]).then_inc(ev("router_in"), 16)
        sp.dma_start(RB, I["router_bias"][0:1, :].partition_broadcast(P)).then_inc(ev("router_in"), 16)
        for t in range(NT):
            if t >= 2:
                sp.wait_ge(ev("x_added"), t - 1)
            src = I["x_prompt"][0, t * P:t * P + P, :] if t < 4 else I["x_sample"].rearrange("b t f -> (b t) f")
            sp.dma_start(XR[0:rows_of(t), t % 2, :], src).then_inc(ev(f"xr_in{t % 2}"), 16)
            if t == 1:
                for z in range(3):
                    expert_weights(sp, 1, 3 + z)
            if t >= 1:
                sp.wait_ge(ev("h2_ready"), t)
                sp.dma_start(h2_d[(t - 1) * P:t * P, :], H2[:, (t - 1) % 2, :]).then_inc(ev(f"h2_out{(t - 1) % 2}"), 16)
        sp.wait_ge(ev("h2_ready"), NT)
        sp.dma_start(h2_d[SEQ:NTOK, :], H2[0:NS, 0, :]).then_inc(ev("h2_out0"), 16)
        sp.wait_ge(slot_out, rel[("wo", 1)])
        for z in range(3):
            expert_weights(sp, 0, z)
        with sp.Fori(1, NE // 2) as i:
            for z in range(6):
                sp.wait_ge(ev(f"w_used{z}"), i)
                expert_weights(sp, 2 * i + z // 3, z)
        sp.wait_ge(ev("x1_ready"), NT)
        sp.wait_ge(*tt.full(("lst",)))
        sp.dma_start(BC2[:, 0, :], mod_d[0:1, 5 * D:6 * D].partition_broadcast(P)).then_inc(ev("rows2_in"), 16)
        sp.dma_start(BC2[0:NS, 1, :], bass.AP(mod_d.tensor, 6 * D + 5 * D, [[6 * D, NB], [0, ST], [1, D]])).then_inc(ev("rows2_in"), 16)
        sp.dma_start(BC2[:, 2, :], I["ln2_g"].partition_broadcast(P)).then_inc(ev("rows2_in"), 16)
        sp.dma_start(BC2[:, 3, :], I["ln2_b"].partition_broadcast(P)).then_inc(ev("rows2_in"), 16)
        sp.wait_ge(ev("further_known"), 1)
        nov = sp.value_load(ints[0:1, I_NOV:I_NOV + 1], min_val=0, max_val=NOV)

        def further_weights(s, i, p):
            e = sp.value_load(ints[0:1, bass.ds(s + I_E, 1)], min_val=0, max_val=NE - 1)
            for z in range(3):
                sp.wait_ge(ev(f"w_used{3 * p + z}"), NE // 2 + i)
                expert_weights(sp, e, 3 * p + z)
        each_further(sp, nov, further_weights)
        for t in range(NT):
            sp.wait_ge(ev("out_ready"), t + 1)
            dst = O["y_prompt"][0, t * P:t * P + P, :] if t < 4 else O["y_sample"].rearrange("b t f -> (b t) f")
            sp.dma_start(dst, OUT[0:rows_of(t), t % 2, :]).then_inc(ev(f"y_stored{t % 2}"), 16)
        sp.wait_ge(ev("y_stored0"), 16 * 3)
        sp.wait_ge(ev("y_stored1"), 16 * 2)
        sp.wait_ge(ev("kv_out0"), 32 * 3)
        sp.wait_ge(ev("kv_out1"), 32 * 2)
        sp.wait_ge(ev("cv_out"), 16 * (1 + NB))
        sp.wait_ge(ev("state_out"), 16)
        sp.wait_ge(ev("newv_out"), 16 * NT)
        sp.wait_ge(ev("vchunk_out"), 16)

    @block.gpsimd
    def _(pool):
        own = Steps(pool, ev("pool_own"))
        own.done(pool.memset(AE[:, :, 0:30], 0.0))
        own.done(pool.memset(HALFN, -0.5))
        def load_bada(n):
            if n >= 4:
                pool.wait_ge(ev("mod_row"), n - 1)
            pool.dma_start(bada_buf(n), I["b_ada"][:, 512 * n:512 * n + 512].partition_broadcast(9)).then_inc(ev(bada_in(n)[0]), 16)
        for n in range(4):
            load_bada(n)
        b_in = I["b_in"]
        for a, b, c in ((0, C_U, 1024), (1024, C_V, 128), (1152, C_WI, 4)):
            pool.dma_start(BB[:, a:a + c], b_in[:, b:b + c].partition_broadcast(P)).then_inc(ev("biasb"), 16)
        pool.dma_start(BB[:, 1156:1668], I["lnC_g"].partition_broadcast(P)).then_inc(ev("biasb"), 16)
        pool.dma_start(BB[:, 1668:2180], I["lnC_b"].partition_broadcast(P)).then_inc(ev("biasb"), 16)

        rstds = [0]

        def rstd(n):
            rstds[0] += 1
            pool.wait_ge(ev("var_ready"), rstds[0])
            own.link(pool.tensor_scalar(VEPS[0:n], MV[0:n, 1:2], EPS, None, ALU.add))
            pool.tensor_tensor(RSTD[0:n], VEPS[0:n], HALFN[0:n], ALU.pow).then_inc(ev("rstd_ready"), 1)

        for key in plan:
            kind = key[0]
            if kind == "ada":
                n = key[1]
                pool.wait_ge(ev("mod_raw"), n + 1)
                pool.wait_ge(ev(bada_in(n)[0]), bada_in(n)[1])
                pool.tensor_tensor(mod_buf(n), mod_buf(n), bada_buf(n), ALU.add).then_inc(ev("mod_row"), 1)
                pool.wait_ge(ev("mod_row"), n + 1)
                pool.dma_start(mod_d[:, 512 * n:512 * n + 512], mod_buf(n)).then_inc(ev(f"mod_out{n % 2}"), 16)
                if 4 <= n + 2 < 12:
                    load_bada(n + 2)
            elif kind == "nat":
                _, what, t = key
                if what == "w" and t == 0:
                    pool.wait_ge(ev("biasb"), 80)
                pool.wait_ge(*mm.taken(key))
                if what == "w":
                    own.done(pool.tensor_tensor(VA[:, t, :], VA[:, t, :], BB[:, 1024:1152], ALU.add))
                    pool.tensor_tensor(WI[:, 4 * t:4 * t + 4], WI[:, 4 * t:4 * t + 4], BB[:, 1152:1156], ALU.add).then_inc(ev("w_biased"), 1)
                    own.need()
                    if t < 4:
                        dst = O["new_v_prompt"][0, 0, t * P:t * P + P].rearrange("s n d -> s (n d)")
                    else:
                        dst = O["new_v_sample"][0].rearrange("b s n d -> (b s) (n d)")
                    pool.dma_start(dst, VA[0:rows_of(t), t, :]).then_inc(ev("newv_out"), 16)
                elif what == "u":
                    pool.tensor_tensor(UN[:, t, :], UN[:, t, :], BB[:, 0:512], ALU.add).then_inc(ev("u_biased"), 1)
                else:
                    pool.tensor_tensor(VN[:, t, :], VN[:, t, :], BB[:, 512:1024], ALU.add).then_inc(ev("v_biased"), 1)
                    rstd(P)
                    pool.wait_ge(ev("v_norm"), t + 1)
                    own.link(pool.tensor_tensor(VN[:, t, :], VN[:, t, :], BB[:, 1156:1668], ALU.mult))
                    pool.tensor_tensor(VN[:, t, :], VN[:, t, :], BB[:, 1668:2180], ALU.add).then_inc(ev("v_full"), 1)
                    if t == 4:
                        pool.wait_ge(ev("v_full"), NT)
                        pool.dma_start(O["new_vchunk_sample"][0].rearrange("b t c -> (b t) c"), VN[0:NS, 4, :]).then_inc(ev("vchunk_out"), 16)
            elif kind == "lnA1":
                rstd(rows_of(key[1]))
            elif kind == "proj":
                _, x, f, h = key
                n = pair_no[(x, f, h)]
                z, cols = n % 2, slice(h * HALF, h * HALF + HALF)
                pool.wait_ge(*mm.taken(("gate", x, f, h)))
                own.link(pool.tensor_scalar(GT[:, z, :], GT[:, z, :], 1.0, None, ALU.add))
                pool.wait_ge(*mm.taken(key))
                if x == "A":
                    pool.tensor_tensor(MG[:, f, cols], GT[:, z, :], PJ[:, z, :], ALU.mult).then_inc(ev("merged"), 1)
                else:
                    own.link(pool.tensor_tensor(PJ[:, z, :], GT[:, z, :], PJ[:, z, :], ALU.mult))
                    pool.tensor_tensor(MG[:, f, cols], MG[:, f, cols], PJ[:, z, :], ALU.add).then_inc(ev("merged"), 1)
            elif key == ("kit", 0):
                pool.wait_ge(ev("yct_up"), NT)
                pool.wait_ge(ev("vchunk_out"), 16)
                own.link(pool.memset(QIM, 0.0))
                for j in range(2):
                    for n in range(NKV):
                        q = QIT[:, j, SEQ:NTOK]
                        own.link(pool.tensor_copy(diagonal(A_QM + j * NB * P + n * NS, 0, P), q.rearrange("p (b t) -> p b t", t=ST)))
                        last = pool.tensor_copy(QI2[:, j, n * NS:n * NS + NS], q)
                        own.link(last) if (j, n) != (1, 1) else last.then_inc(ev("qim_ready"), 1)
            elif key == ("kts", 0):
                pool.wait_ge(*at.full(("dots", "s", 3)))
                pool.wait_ge(ev("qim_ready"), 1)
                for z in range(2):
                    own.done(pool.memset(QMN[z][0], 0.0))
                    own.link(pool.memset(QMN[z][1], 0.0))
            elif kind == "lg" and key[1] == "s":
                c = key[2]
                if c >= 2:
                    pool.wait_ge(*at.full(("lg", "s", c - 2)))
                for n in range(NKV):
                    r = slice(n * HD, n * HD + HD)
                    q = QT[r, c, SEQ:NTOK]
                    own.link(pool.tensor_copy(diagonal(A_QM + (c % 2) * 1152 + n * NS, n * HD, HD), q.rearrange("p (b t) -> p b t", t=ST)))
                    last = pool.tensor_copy(QMN[c % 2][1][r, n * NS:n * NS + NS], q)
                    own.link(last) if n == 0 else last.then_inc(ev("qm_ready"), 1)
            elif kind == "wo" and key[2] == 1:
                t = key[1]
                n = rows_of(t)
                if t == 0:
                    pool.wait_ge(ev("rows_in"), 16 * 8)
                rstd(n)
                pool.wait_ge(ev("r_norm"), t + 1)
                own.link(pool.tensor_tensor(X1[0:n, t, :], R[0:n, t % 2, :], BC["lg"][0:n], ALU.mult))
                pool.tensor_tensor(X1[0:n, t, :], X1[0:n, t, :], BC["lb"][0:n], ALU.add).then_inc(ev("x1_ready"), 1)

        pool.wait_ge(ev("list_int"), 1)
        pool.wait_ge(ev("h2_out0"), 16 * 3)
        pool.wait_ge(ev("h2_out1"), 16 * 2)
        for e in range(NE):
            if e == 2:
                own.link(pool.memset(ZERO, 0.0))
                pool.dma_start(y_d[FAR_ROWS:SLOTS].rearrange("(p n) (h d) -> p (n h) d", p=P, d=512),
                               ZERO.unsqueeze(1).broadcast_to([P, NOV * TS * 2 // P, 512])).then_inc(ev("far_zeroed"), 16)
            if 4 <= e < 4 + NT:
                t = e - 4
                pool.tensor_scalar(X1[0:rows_of(t), t, :], X1[0:rows_of(t), t, :], ALPHA, None, ALU.mult).then_inc(ev("x1_scaled"), 1)
            if e >= 2:
                pool.wait_ge(ev("gt_full"), e - 1)
            pool.indirect_dma_start(G[0:TS, e % 2, :], None, h2_d, bass.IndirectOffsetOnAxis(ints[0:TS, I_L + e:I_L + e + 1], 0)).then_inc(ev(f"rows_gathered{e % 2}"), 16)
        pool.wait_ge(ev("further_known"), 1)
        nov = pool.value_load(ints[0:1, I_NOV:I_NOV + 1], min_val=0, max_val=NOV)
        for s in range(NOV):
            with pool.If(nov > s):
                pool.wait_ge(ev("gt_full"), NE + s - 1)
                pool.indirect_dma_start(G[:, s % 2, :], None, h2_d, bass.IndirectOffsetOnAxis(ints[:, I_L + NE + s:I_L + NE + s + 1], 0)).then_inc(ev(f"rows_gathered{s % 2}"), 16)
        pool.wait_ge(ev("far_zeroed"), 16)
        for p in range(2):
            pool.wait_ge(ev(f"yo_out{p}"), 16 * (NE // 2))
        for s in range(NOV):
            with pool.If(nov > s):
                pool.wait_ge(ev(f"yo_out{s % 2}"), 16 * (NE // 2 + s // 2 + 1))
        for t in range(NT):
            n = rows_of(t)
            for k, a in enumerate((I_SA, I_SB)):
                pool.indirect_dma_start(GAT[0:n, 2 * t + k, :], None, y_d,
                                        bass.IndirectOffsetOnAxis(ints[0:n, a + t:a + t + 1], 0)).then_inc(ev(f"pair_in{t}"), 16)
        pool.wait_ge(ev("rows2_in"), 64)
        for t in range(NT + 1):
            if t < NT:
                n = rows_of(t)
                pool.wait_ge(ev("last_var"), t + 1)
                own.link(pool.tensor_scalar(VAR2[0:n, t % 2:t % 2 + 1], MV2[0:n, t % 2, 1:2], EPS, None, ALU.add))
                pool.tensor_tensor(RSTD2[0:n, t % 2:t % 2 + 1], VAR2[0:n, t % 2:t % 2 + 1], HALFN[0:n], ALU.pow).then_inc(ev("last_rstd"), 1)
            if t >= 1:
                d = t - 1
                n = rows_of(d)
                pool.wait_ge(ev("o_norm"), d + 1)
                if d >= 2:
                    pool.wait_ge(ev(f"y_stored{d % 2}"), 16 * (d // 2))
                own.link(pool.tensor_tensor(OUT[0:n, d % 2, :], GAT[0:n, 2 * d, :], BC2[0:n, 2, :], ALU.mult))
                pool.tensor_tensor(OUT[0:n, d % 2, :], OUT[0:n, d % 2, :], BC2[0:n, 3, :], ALU.add).then_inc(ev("out_ready"), 1)

    @block.scalar
    def _(act):
        own = Steps(act, ev("act_own"))
        b_in = I["b_in"][0]
        act.wait_ge(ev("c_in"), 32)
        act.activation(CN[0:9, :], CN[0:9, :], ACT.Silu).then_inc(ev("c_silu"), 1)
        for r, c, k in ((R_A, 0, 8), (R_K, C_K, 1), (R_QI, C_QI, 2), (R_G, C_G, 24)):
            act.dma_start(PRN[r:r + k, :], b_in[c:c + k * P].rearrange("(r n) -> r n", n=P)).then_inc(ev("small_in"), 16)
        for n in range(NKV):
            act.dma_start(PRN[R_Q:R_Q + 4, n * HD:n * HD + HD],
                          b_in[C_Q + n * 256:C_Q + n * 256 + 256].rearrange("(c d) -> c d", d=HD)).then_inc(ev("small_in"), 16)
            act.dma_start(PRN[R_KI:R_KI + 1, n * HD:n * HD + HD], b_in[C_KI:C_KI + HD].unsqueeze(0)).then_inc(ev("small_in"), 16)
        for r, name in ((R_CB, "conv_b"), (R_LG, "lnA_g"), (R_LB, "lnA_b")):
            act.dma_start(PRN[r:r + 4, :], I[name][0].rearrange("(r n) -> r n", n=P)).then_inc(ev("small_in"), 16)
        act.dma_start(PRN[R_BS:R_BS + NCG, :], I["b_s"][0]).then_inc(ev("small_in"), 16)
        act.dma_start(CKN[0:CW, :], I["conv_k"][0]).then_inc(ev("convk_in"), 16)
        act.dma_start(WSN, I["w_s"][0].rearrange("g t s -> t g s")).then_inc(ev("ws_in"), 16)
        for h in range(2):
            act.dma_start(STN[0:120, h, :], I["state_conv"][0, 4 * h:4 * h + 4].rearrange("b r f -> (b r) f")).then_inc(ev("state_in"), 16)
        act.dma_start(REL[0:NBUCK, :], I["rel_table"]).then_inc(ev("table_parts"), 16)
        act.dma_start(OH[0:NBUCK, :], oh_d).then_inc(ev("table_parts"), 16)

        def exps(u):
            i, c = units[u]
            if i != "s":
                k = P * (i + 1)
                for n in range(NKV):
                    act.wait_ge(ev("logits_up"), 2 * u + n + 1)
                    act.activation(LP[:, n, 0:k], LP[:, n, 0:k], ACT.Exp, bias=NEGM[:, n:n + 1], accum_out=RSUM[:, n:n + 1]).then_inc(ev("exp_done"), 1)
            else:
                act.wait_ge(ev("logits_up"), 32 + u - 15)
                act.activation(LP[:, 0, 0:320], LP[:, 0, 0:320], ACT.Exp, bias=NEGM[:, 0:1], accum_out=RSUM[:, 0:1]).then_inc(ev("exp_done"), 1)

        for key in plan:
            kind = key[0]
            if kind == "oh":
                h = key[1]
                a, b = (0, 512) if h == 0 else (512, SLEN)
                act.wait_ge(*at.full(key))
                act.activation(TAB[0:8, a:b], at.tile(key)[0:8, 0:b - a], ACT.Copy).then_inc(at.free(key), 1)
                if h == 1:
                    act.wait_ge(*at.taken(("oh", 0)))
                    act.wait_ge(*at.taken(("oh", 1)))
                    act.dma_start(tab_d, TAB[0:8, :].unsqueeze(1).broadcast_to([8, P, SLEN])).then_inc(ev("table_out"), 16)
            elif kind == "ada":
                n = key[1]
                act.wait_ge(*mm.full(key))
                if n >= 4:
                    act.wait_ge(ev(f"mod_out{n % 2}"), 16 * (n // 2))
                    if n < 6:
                        act.wait_ge(*tt.full(("mT", n - 2)))
                for g in range(4):
                    last = act.activation(mod_buf(n)[:, g * P:g * P + P], mm.tile(key)[32 * g:32 * g + 9, 0:P], ACT.Copy)
                    own.done(last) if g < 3 else last.then_inc(mm.free(key), 1)
                own.need()
                act.wait_ge(*mm.taken(key))
                act.sem_inc(ev("mod_raw"), 1)
            elif kind == "xT":
                f = key[1]
                act.wait_ge(*tt.full(key))
                if f == 0:
                    act.wait_ge(ev("modT_up"), 4)
                act.activation(HT[:, f, 0:SEQ], tt.tile(key), ACT.Identity, bias=MT[:, f, 0:1], scale=MT[:, 8 + f, 0:1]).then_inc(tt.free(key), 1)
            elif kind == "fm" and key[1] != "a":
                _, name, j, h = key
                cols = slice(h * HALF, h * HALF + HALF)
                act.wait_ge(*mm.full(key))
                src = mm.tile(key)[:, 0:HALF]
                if name == "ag":
                    n = glu_no[(j, h)]
                    if n == 0:
                        act.wait_ge(ev("params_up"), 1)
                        act.wait_ge(*at.full(("oh", 1)))
                    if n >= 2:
                        act.wait_ge(ev("glu_up"), n - 1)
                    act.activation(LP[:, n % 2, 0:HALF], src, ACT.Tanh, bias=PARH[:, R_A + 4 + j:R_A + 5 + j], scale=0.5).then_inc(mm.free(key), 1)
                else:
                    dst, r = {"q": (QT[:, j], R_Q + j), "k": (KTT, R_K), "ki": (KIT, R_KI), "qi": (QIT[:, j % 2], R_QI + j)}[name]
                    act.activation(dst[:, cols], src, ACT.Identity, bias=PAR[:, r:r + 1]).then_inc(mm.free(key), 1)
            elif kind == "kv":
                t = key[1]
                n = rows_of(t)
                act.wait_ge(*tt.full(key))
                if t >= 2:
                    act.wait_ge(ev(f"kv_out{t % 2}"), 32 * (t // 2))
                ko = SC[0:n, (t % 2) * 192:(t % 2) * 192 + 192]
                act.activation(ko, tt.tile(key)[0:n, 0:192], ACT.Copy).then_inc(tt.free(key), 1)
                act.wait_ge(*tt.taken(key))
                if t < 4:
                    dk = O["new_k_prompt"][0, 0, t * P:t * P + P].rearrange("s n d -> s (n d)")
                    di = O["new_kidx_prompt"][0, 0, t * P:t * P + P]
                else:
                    dk = O["new_k_sample"][0].rearrange("b s n d -> (b s) (n d)")
                    di = O["new_kidx_sample"][0].rearrange("b s d -> (b s) d")
                act.dma_start(dk, ko[:, 0:P]).then_inc(ev(f"kv_out{t % 2}"), 16)
                act.dma_start(di, ko[:, P:192]).then_inc(ev(f"kv_out{t % 2}"), 16)
            elif kind in ("cvp", "cvs"):
                n, dst = (CW - 1, PTT[0:CW - 1, 0, :]) if kind == "cvp" else (NS, PTT[0:NS, 1, :])
                act.wait_ge(*tt.full(key))
                act.activation(dst, tt.tile(key)[0:n, :], ACT.Copy).then_inc(tt.free(key), 1)
                act.wait_ge(*tt.taken(key))
                if kind == "cvp":
                    act.dma_start(O["new_conv_prompt"][0, 0], dst).then_inc(ev("cv_out"), 16)
                else:
                    for b in range(NB):
                        act.dma_start(O["new_conv_sample"][0, b, CW - 1 - ST:CW - 1, :], dst[b * ST:b * ST + ST, :]).then_inc(ev("cv_out"), 16)
                    act.wait_ge(ev("table_out"), 16)
                    load_bias(act, *units[0])
            elif kind == "nat":
                _, what, t = key
                act.wait_ge(*mm.full(key))
                src = mm.tile(key)
                if what == "w":
                    own.done(act.activation(VA[:, t, :], src[:, 0:P], ACT.Copy))
                    own.need()
                    act.activation(WI[:, 4 * t:4 * t + 4], src[:, P:NW], ACT.Copy).then_inc(mm.free(key), 1)
                else:
                    act.activation((UN if what == "u" else VN)[:, t, :], src, ACT.Copy).then_inc(mm.free(key), 1)
            elif kind == "lnA2":
                t = key[1]
                n = rows_of(t)
                act.wait_ge(*tt.full(key))
                for j in range(NJ):
                    if j == NJ - 1:
                        own.need()
                    last = act.activation(YT["A"][:, j, t * P:t * P + n], tt.tile(key)[:, j * P:j * P + n], ACT.Silu,
                                          bias=PAR[:, R_LB + j:R_LB + j + 1], scale=PAR[:, R_LG + j:R_LG + j + 1])
                    own.done(last) if j < NJ - 1 else last.then_inc(tt.free(key), 1)
            elif kind == "gate":
                _, x, f, h = key
                n = pair_no[(x, f, h)]
                act.wait_ge(*mm.full(key))
                if n >= 2:
                    act.wait_ge(ev("merged"), n - 1)
                r = R_G + "ABC".index(x) * KT + f
                act.activation(GT[:, n % 2, :], mm.tile(key)[:, 0:HALF], ACT.Tanh, bias=PARH[:, r:r + 1], scale=0.5).then_inc(mm.free(key), 1)
            elif kind == "proj":
                _, x, f, h = key
                n = pair_no[(x, f, h)]
                act.wait_ge(*mm.full(key))
                act.activation(PJ[:, n % 2, :], mm.tile(key)[:, 0:HALF], ACT.Copy).then_inc(mm.free(key), 1)
            elif kind == "lg":
                u = unit_no[(key[1], key[2])]
                exps(u)
                if u + 1 < len(units):
                    load_bias(act, *units[u + 1])
            elif kind == "h2T":
                _, t, h = key
                n = rows_of(t)
                act.wait_ge(*tt.full(key))
                if t and h == 0:
                    act.wait_ge(*at.full(("rt", t - 1)))
                src = tt.tile(key).rearrange("p (k n) -> p k n", n=P)
                act.activation(H2T[:, 4 * h:4 * h + 4, 0:n], src[:, :, 0:n], ACT.Copy).then_inc(tt.free(key), 1)
            elif kind == "rt":
                t = key[1]
                n = rows_of(t)
                act.wait_ge(*at.full(key))
                act.activation(TH[0:n, t, :], at.tile(key)[0:n, 0:NE], ACT.Tanh, scale=0.5).then_inc(at.free(key), 1)

        def result(d, dq, p):
            act.wait_ge(ev("dn_full"), d + 1)
            if positive(dq):
                act.wait_ge(ev(f"yo_out{p}"), 16 * dq)
            act.activation(YO[0:TS, p, 0:512], banks[5][0:TS, :], ACT.Copy).then_inc(ev("yo_a"), 1)
            rows = y_d[d * TS:d * TS + TS, :] if type(d) is int else y_d[bass.ds(d * TS, TS), :]
            act.wait_ge(ev("yo_a"), d + 1)
            act.wait_ge(ev("yo_b"), d + 1)
            act.dma_start(rows, YO[0:TS, p, :]).then_inc(ev(f"yo_out{p}"), 16)

        def rows_up(e, p):
            act.wait_ge(ev("gt_full"), e + 1)
            act.activation(HG[:, p, 0:4, :], quarter_tiles(banks[2]), ACT.Copy).then_inc(ev("gt_a"), 1)

        def expert(e, q, dq, p):
            act.wait_ge(ev("gu_full"), e + 1)
            act.activation(HE[:, p, :], banks[0], ACT.Silu).then_inc(ev("he_silu"), 1)
            if type(e) is not int or e < NE - 1:
                rows_up(e + 1, 1 - p)
            if positive(e):
                result(e - 1, dq, 1 - p)

        act.wait_ge(ev("x1_ready"), NT)
        rows_up(0, 0)
        each_expert(act, expert)
        result(NE - 1, NE // 2 - 1, 1)
        nov = act.value_load(ints[0:1, I_NOV:I_NOV + 1], min_val=0, max_val=NOV)

        def further(s, i, p):
            rows_up(s + NE, p)
            act.wait_ge(ev("gu_full"), s + NE + 1)
            act.activation(HE[:, p, :], banks[0], ACT.Silu).then_inc(ev("he_silu"), 1)
            act.wait_ge(ev("far_zeroed"), 16)
            result(s + NE, i + NE // 2, p)
        each_further(act, nov, further)
        for t in range(NT):
            n = rows_of(t)
            act.wait_ge(ev(f"pair_in{t}"), 32)
            act.activation(GAT[0:n, 2 * t, :], GAT[0:n, 2 * t, :], ACT.Copy, scale=WGA[0:n, t:t + 1]).then_inc(ev("pair_scaled"), 1)

    @block.vector
    def _(dve):
        own = Steps(dve, ev("dve_own"))
        link, done, need = own.link, own.done, own.need
        ts, tt_, stt = dve.tensor_scalar, dve.tensor_tensor, dve.scalar_tensor_tensor
        stats_n = [0]

        def stats(src, n, width=512):
            for k in range(width // 512):
                done(dve.bn_stats(STAT[0:n, 6 * k:6 * k + 6], src[:, 512 * k:512 * k + 512]))
            need()
            stats_n[0] += 1
            dve.bn_aggr(MV[0:n], STAT[0:n, 0:6 * (width // 512)]).then_inc(ev("var_ready"), 1)
            dve.wait_ge(ev("var_ready"), stats_n[0])
            dve.wait_ge(ev("rstd_ready"), stats_n[0])

        def conv():
            acc_s = [ACC[:, j, SEQ:NTOK].rearrange("p (b t) -> p b t", t=ST) for j in range(NJ)]

            def old_s(j, w):
                v = AES[:, j, 30 + SEQ:EXT].rearrange("p (b x) -> p b x", x=30 + ST)
                return v[:, :, w:w + ST] if type(w) is int else v[:, :, bass.ds(w, ST)]
            conv_n = ev("conv_steps")
            for j in range(NJ):
                ts(ACC[:, j, 0:SEQ], AES[:, j, 0:SEQ], CK[:, j, 0:1], PAR[:, R_CB + j:R_CB + j + 1], ALU.mult, ALU.add).then_inc(conv_n, 1)
            for j in range(NJ):
                ts(acc_s[j], old_s(j, 0), CK[:, j, 0:1], PAR[:, R_CB + j:R_CB + j + 1], ALU.mult, ALU.add).then_inc(conv_n, 1)
            with dve.Fori(1, CW) as w:
                for j in range(NJ):
                    dve.wait_ge(conv_n, w * 8 + (j - 7))
                    stt(ACC[:, j, 0:SEQ], arena[:, bass.ds(w + (A_AE + j * EXT), SEQ)], arena[:, bass.ds(w + (A_CK + j * CW), 1)],
                        ACC[:, j, 0:SEQ], ALU.mult, ALU.add).then_inc(conv_n, 1)
                for j in range(NJ):
                    dve.wait_ge(conv_n, w * 8 + (j - 3))
                    stt(acc_s[j], old_s(j, w), arena[:, bass.ds(w + (A_CK + j * CW), 1)], acc_s[j], ALU.mult, ALU.add).then_inc(conv_n, 1)
            dve.wait_ge(conv_n, 8 * CW)
            dve.nop().then_inc(ev("conv_done"), 1)

        def top_rounds(i, a, b):
            k, rounds, extra = (320, (TOPK_S + 6) // 8, 6) if i == "s" else (P * (i + 1), TOPK_P // 8, 0)
            width = k + extra
            for r in range(a, b):
                link(dve.max(MX8, SC[:, 0:width]))
                link(dve.match_replace(SC[:, 0:width], MX8, SC[:, 0:width], REPL))
            if b == rounds:
                link(ts(PEN[i], SC[:, 0:k], SELD, NEG, ALU.is_gt, ALU.mult))

        def prepare_rows():
            dve.wait_ge(ev("rows_in"), 16 * 8)
            for pick, n in (("p", P), ("s", NS)):
                g1, sc, sh = (BC[name + pick][0:n] for name in ("g1", "sc", "sh"))
                done(ts(g1, g1, 0.5, 0.5, ALU.mult, ALU.add))
                link(ts(sc, sc, 1.0, None, ALU.add))
                link(tt_(H2[0:n, 0, :], sc, BC["lb"][0:n], ALU.mult))
                done(tt_(sh, sh, H2[0:n, 0, :], ALU.add))
                link(tt_(sc, sc, BC["lg"][0:n], ALU.mult))

        def route():
            dve.wait_ge(*at.taken(("rt", 4)))
            dve.wait_ge(ev("router_in"), 48)
            link(ts(TH, TH, 0.5, 0.5, ALU.mult, ALU.add))
            link(tt_(SEL, TH, RB.unsqueeze(1).broadcast_to([P, NT, NE]), ALU.add))
            q = SEL.rearrange("p t (g e) -> p (t g) e", e=4)
            done(tt_(PSUMS[:, :, 0:3], q[:, :, 0:3], q[:, :, 1:4], ALU.add))
            done(tt_(PSUMS[:, :, 3:5], q[:, :, 0:2], q[:, :, 2:4], ALU.add))
            link(tt_(PSUMS[:, :, 5:6], q[:, :, 0:1], q[:, :, 3:4], ALU.add))
            link(dve.tensor_reduce(GS, PSUMS, AX.X, ALU.max))
            link(dve.tensor_copy(GBUF[:, :, 0:4], GS.rearrange("p (t g) -> p t g", g=4)))
            for t in range(NT):
                link(dve.max(MX8, GBUF[:, t, :]))
                link(dve.match_replace(GRES[:, t, :], MX8, GBUF[:, t, :], REPL))
            link(ts(GMK.rearrange("p (t g) -> p t g", g=4), GRES[:, :, 0:4], SELD, NEG, ALU.is_gt, ALU.mult))
            link(tt_(SBUF_[:, :, 0:NE].rearrange("p t (g e) -> p t g e", e=4), SEL.rearrange("p t (g e) -> p t g e", e=4),
                     GMK.rearrange("p (t g) -> p t g", g=4).unsqueeze(3).broadcast_to([P, NT, 4, 4]), ALU.add))
            for t in range(NT):
                link(dve.max(MX8, SBUF_[:, t, :]))
                link(dve.match_replace(SRES[:, t, :], MX8, SBUF_[:, t, :], REPL))
            ts(MSK, SRES[:, :, 0:NE], SELD, None, ALU.is_lt).then_inc(ev("mask_ready"), 1)
            dve.wait_ge(ev("mask_ready"), 1)
            link(tt_(GATE, TH, MSK, ALU.mult))
            link(dve.tensor_reduce(SUM5, GATE, AX.X, ALU.add))
            link(dve.reciprocal(SUM5, SUM5))
            link(tt_(GATE, GATE, SUM5.unsqueeze(2).broadcast_to([P, NT, NE]), ALU.mult))

        def place_tokens(ps):
            cum = ps[:, 0:NT * NE].rearrange("p (t e) -> p t e", e=NE)
            base = con[:, K_SLOT:K_SLOT + NE].unsqueeze(1).broadcast_to([P, NT, NE])
            done(dve.memset(EQ[:, 4, :], 0.0))
            link(dve.memset(SLM[:, 4, :], 0.0))
            link(dve.tensor_copy(CNT, ps[:, NT * NE:(NT + 1) * NE]))
            cmp_ = CMP.rearrange("p a b -> p (a b)")[:, 0:NE * MORE].rearrange("p (e m) -> p e m", m=MORE)
            link(tt_(cmp_, CNT.unsqueeze(2).broadcast_to([P, NE, MORE]), RCON[:, R_THR:R_HI].unsqueeze(1).broadcast_to([P, NE, MORE]), ALU.is_gt))
            link(dve.tensor_reduce(OVER, cmp_, AX.X, ALU.add))
            link(tt_(CMP, OVER.unsqueeze(1).broadcast_to([P, NE, NE]), RCON[:, R_LT:R_THR].rearrange("p (a b) -> p a b", b=NE), ALU.mult))
            link(dve.tensor_reduce(BEFORE, CMP, AX.X, ALU.add))
            link(ts(TEXP, BEFORE, float(TS), float(FAR_ROWS - TS), ALU.mult, ALU.add))
            link(stt(TEXP, con[:, K_SLOT:K_SLOT + NE], -1.0, TEXP, ALU.mult, ALU.add))
            link(ts(TEXP, TEXP, -1.0, None, ALU.add))
            link(dve.tensor_copy(SLM[:, 0:4], cum[:, 0:4]))
            link(dve.tensor_copy(SLM[0:NS, 4], cum[0:NS, 4]))
            link(ts(EQ, SLM, float(TS), None, ALU.is_gt))
            link(tt_(EQ, EQ, TEXP.unsqueeze(1).broadcast_to([P, NT, NE]), ALU.mult))
            link(tt_(SLM, SLM, base, ALU.add))
            link(tt_(SLM, SLM, EQ, ALU.add))
            link(stt(EQ, SLM, -FAR, MSK, ALU.add, ALU.mult))
            link(dve.tensor_reduce(SA, EQ, AX.X, ALU.min))
            link(ts(SA, SA, FAR, None, ALU.add))
            link(tt_(SLM, SLM, MSK, ALU.mult))
            link(dve.tensor_reduce(SB_, SLM, AX.X, ALU.max))
            done(dve.tensor_copy(ints[:, I_SA:I_SA + NT], SA))
            link(dve.tensor_copy(ints[:, I_SB:I_SB + NT], SB_))
            dve.sem_inc(at.free(("cum",)), 1)
            link(tt_(GE, SAB.unsqueeze(2).broadcast_to([P, 2 * NT, NHI + 1]), RCON[:, R_HI:R_LO].unsqueeze(1).broadcast_to([P, 2 * NT, NHI + 1]), ALU.is_ge))
            link(dve.tensor_reduce(HIS, GE, AX.X, ALU.add))
            link(stt(HIS, HIS, -float(TS), SAB, ALU.mult, ALU.add))
            done(tt_(OHH, GE[:, :, 0:NHI], GE[:, :, 1:NHI + 1], ALU.subtract))
            link(tt_(OHL, HIS.unsqueeze(2).broadcast_to([P, 2 * NT, TS]), RCON[:, R_LO:].unsqueeze(1).broadcast_to([P, 2 * NT, TS]), ALU.is_equal))
            tokens = con[:, K_TOK:K_TOK + NT].unsqueeze(2).broadcast_to([P, NT, NHI])
            done(tt_(OHH[:, 0:NT], OHH[:, 0:NT], tokens, ALU.mult))
            link(tt_(OHH[:, NT:2 * NT], OHH[:, NT:2 * NT], tokens, ALU.mult))
            dve.sem_inc(ev("slots_ready"), 1)
            for s_, w_ in ((SA, WGA), (SB_, WGB)):
                link(tt_(EQ, SLM, s_.unsqueeze(2).broadcast_to([P, NT, NE]), ALU.is_equal))
                link(tt_(EQ, EQ, GATE, ALU.mult))
                link(dve.tensor_reduce(w_, EQ, AX.X, ALU.add))

        def further_tiles():
            link(tt_(TEXP, BEFORE, OVER, ALU.add))
            done(dve.tensor_copy(ints[:, I_NOV:I_NOV + 1], TEXP[:, NE - 1:NE]))
            sel = CMP[:, 0:NOV, :]
            link(tt_(sel, TEXP.unsqueeze(1).broadcast_to([P, NOV, NE]),
                     con[:, K_STEP:K_STEP + NOV].unsqueeze(2).broadcast_to([P, NOV, NE]), ALU.is_le))
            link(dve.tensor_reduce(CNT[:, 0:NOV], sel, AX.X, ALU.add))
            link(ts(CNT[:, 0:NOV], CNT[:, 0:NOV], NE - 1.0, None, ALU.min))
            link(dve.tensor_copy(ints[:, I_E:I_E + NOV], CNT[:, 0:NOV]))
            dve.sem_inc(ev("further_known"), 1)

        for key in plan:
            kind = key[0]
            if kind == "tk":
                top_rounds(*key[1:])
                continue
            ring_of = {"M": mm, "T": tt, "A": at}[kinds[kind]]
            mine = kind in ("par", "ck", "ws", "st", "cT", "mT", "xTs", "bd", "lnA1", "mix", "yc", "dots", "kit", "kts", "wo", "cum", "lst")
            if mine:
                dve.wait_ge(*ring_of.full(key))
                ps = ring_of.tile(key)
            if kind == "par":
                link(dve.tensor_copy(PAR, ps[:, 0:NR]))
                ts(PARH, PAR, 0.5, None, ALU.mult).then_inc(ev("params_up"), 1)
                dve.wait_ge(ev("params_up"), 1)
                dve.sem_inc(ring_of.free(key), 1)
            elif kind == "ck":
                dve.tensor_copy(CK, ps[:, 0:NJ * CW].rearrange("p (j w) -> p j w", w=CW)).then_inc(tt.free(key), 1)
            elif kind == "ws":
                h = key[1]
                if h == 0:
                    dve.wait_ge(ev("consts"), 16)
                tt_(WS[:, 4 * h:4 * h + 4, :], quarter_tiles(ps), tri.unsqueeze(1).broadcast_to([P, 4, P]), ALU.mult).then_inc(tt.free(key), 1)
            elif kind == "bd":
                for b in range(NB):
                    done(ts(BD[0:NS, :, b, :], ps[0:NS, 0:NCG * ST].rearrange("p (g t) -> p g t", t=ST),
                            con[0:NS, K_BLK + b:K_BLK + b + 1], None, ALU.mult))
                dve.tensor_copy(BS2, ps[:, NCG * ST:NCG * ST + NCG]).then_inc(at.free(key), 1)
            elif kind == "st":
                h = key[1]
                ext = AES[:, :, 30 + SEQ:EXT].rearrange("p j (b x) -> p j b x", x=30 + ST)
                src = ps[:, 0:4 * 120].rearrange("p (j b r) -> p j b r", j=NJ, b=4)
                for j in range(NJ):
                    last = dve.tensor_copy(ext[:, j, 4 * h:4 * h + 4, 0:30], src[:, j])
                    last.then_inc(tt.free(key), 1) if j == NJ - 1 else link(last)
            elif kind == "cT":
                dve.tensor_copy(CT, ps[:, 0:KT * 9].rearrange("p (k n) -> p k n", n=9)).then_inc(tt.free(key), 1)
            elif kind == "mT":
                n = key[1]
                src = ps[:, 0:36].rearrange("p (k n) -> p k n", n=9)
                ts(MT[:, 4 * n:4 * n + 4, :], src, 1.0 if n >= 2 else 0.0, None, ALU.add).then_inc(tt.free(key), 1)
                dve.wait_ge(*tt.taken(key))
                dve.sem_inc(ev("modT_up"), 1)
            elif kind == "xTs":
                dst = HT[:, :, SEQ:NTOK].rearrange("p f (b t) -> p f b t", t=ST)
                src = ps.rearrange("p (f b t) -> p f b t", f=KT, b=NB)
                for f in range(KT):
                    done(tt_(dst[:, f], src[:, f], MT[:, KT + f, 1:9].unsqueeze(2).broadcast_to([P, NB, ST]), ALU.mult))
                need()
                for f in range(KT):
                    done(tt_(dst[:, f], dst[:, f], MT[:, f, 1:9].unsqueeze(2).broadcast_to([P, NB, ST]), ALU.add))
                need()
                dve.tensor_copy(HT[:, :, NTOK:NTOK + NS], HT[:, :, SEQ:NTOK]).then_inc(tt.free(key), 1)
            elif kind == "fm" and key[1] == "a":
                _, _, j, h = key
                n = glu_no[(j, h)]
                dve.wait_ge(*mm.taken(("fm", "ag", j, h)))
                gate = LP[:, n % 2, 0:HALF]
                link(ts(gate, gate, 0.5, 0.5, ALU.mult, ALU.add))
                dve.wait_ge(*mm.full(key))
                ps = mm.tile(key)
                if n == 0:
                    dve.wait_ge(ev("pool_own"), 2)
                bias = PAR[:, R_A + j:R_A + j + 1]
                if h == 0:
                    link(stt(AES[:, j, 30:30 + HALF], ps[:, 0:HALF], bias, gate, ALU.add, ALU.mult))
                else:
                    m = SEQ - HALF
                    done(stt(AES[:, j, 30 + HALF:30 + SEQ], ps[:, 0:m], bias, gate[:, 0:m], ALU.add, ALU.mult))
                    ext = AES[:, j, 30 + SEQ:EXT].rearrange("p (b x) -> p b x", x=30 + ST)
                    link(stt(ext[:, :, 30:30 + ST], ps[:, m:HALF].rearrange("p (b t) -> p b t", t=ST), bias,
                             gate[:, m:HALF].rearrange("p (b t) -> p b t", t=ST), ALU.add, ALU.mult))
                dve.sem_inc(mm.free(key), 1)
                dve.sem_inc(ev("glu_up"), 1)
                if n == 2 * NJ - 1:
                    ext = AES[:, :, 30 + SEQ:EXT].rearrange("p j (b x) -> p j b x", x=30 + ST)
                    for j in range(NJ):
                        last = dve.tensor_copy(CVS[:, j, :].rearrange("p (b t) -> p b t", t=ST), ext[:, j, :, 30:30 + ST])
                        last.then_inc(ev("cvs_staged"), 1) if j == NJ - 1 else link(last)
                    conv()
            elif kind == "lnA1":
                t = key[1]
                n = rows_of(t)
                stats(ps[0:n], n)
                if t == 0:
                    dve.wait_ge(ev("cv_out"), 16 * 9)
                if t >= 2:
                    dve.wait_ge(*tt.full(("lnA2", t - 2)))
                ts(LP[0:n, t % 2, :], ps[0:n], MV[0:n, 0:1], RSTD[0:n], ALU.subtract, ALU.mult).then_inc(tt.free(key), 1)
            elif kind == "nat" and key[1] == "v":
                t = key[2]
                dve.wait_ge(ev("v_biased"), t + 1)
                stats(VN[:, t, :], P)
                ts(VN[:, t, :], VN[:, t, :], MV[:, 0:1], RSTD, ALU.subtract, ALU.mult).then_inc(ev("v_norm"), 1)
            elif kind == "mix":
                t = key[1]
                n = rows_of(t)
                bs = (PAR[:, R_BS:R_BS + NCG] if t < 4 else BS2)[0:n].unsqueeze(2).broadcast_to([n, NCG, HD])
                if t:
                    dve.wait_ge(ev("sgu_up"), t)
                tmp = TMP[0:n].rearrange("p (g d) -> p g d", d=HD)
                tt_(tmp, ps[0:n].rearrange("p (g d) -> p g d", d=HD), bs, ALU.add).then_inc(at.free(key), 1)
                dve.wait_ge(*at.taken(key))
                dve.wait_ge(ev("u_biased"), t + 1)
                tt_(UN[0:n, t, :], TMP[0:n], UN[0:n, t, :], ALU.mult).then_inc(ev("sgu_up"), 1)
            elif kind == "yc":
                t = key[1]
                n = rows_of(t)
                if t == 0:
                    dve.wait_ge(ev("mod_out0"), 16 * 6)
                    dve.wait_ge(ev("mod_out1"), 16 * 6)
                dve.tensor_copy(YT["C"][:, :, t * P:t * P + n], quarter_tiles(ps)[:, :, 0:n]).then_inc(tt.free(key), 1)
                dve.wait_ge(*tt.taken(key))
                dve.sem_inc(ev("yct_up"), 1)
            elif kind == "dots":
                _, i, h = key
                t = 4 if i == "s" else i
                k = 320 if i == "s" else P * (i + 1)
                w = WI[:, 4 * t + h:4 * t + h + 1]
                if (i, h) == (1, 0):
                    dve.wait_ge(ev("w_biased"), NT)
                    dve.wait_ge(ev("kv_out0"), 32 * 3)
                    dve.wait_ge(ev("kv_out1"), 32 * 2)
                if h == 0:
                    ts(SC[:, 0:k], ps[:, 0:k], 0.0, w, ALU.max, ALU.mult).then_inc(at.free(key), 1)
                    dve.wait_ge(*at.taken(key))
                else:
                    ts(TMP[:, 0:k], ps[:, 0:k], 0.0, w, ALU.max, ALU.mult).then_inc(at.free(key), 1)
                    dve.wait_ge(*at.taken(key))
                    link(tt_(SC[:, 0:k], SC[:, 0:k], TMP[:, 0:k], ALU.add))
                if h == 3:
                    if i == "s":
                        done(dve.memset(SC[:, k:k + 6], BIG))
                        link(tt_(SC[:, PAST:k], SC[:, PAST:k], con[:, K_PENS:K_PENS + NS], ALU.add))
                    else:
                        link(tt_(SC[:, k - P:k], SC[:, k - P:k], PEN[0], ALU.add))
            elif kind == "kit" or kind == "kts":
                g = key[1]
                if key == ("kit", 0):
                    dve.wait_ge(ev("yct_up"), NT)
                    dve.wait_ge(ev("vchunk_out"), 16)
                dve.tensor_copy(KTS[:, 2 * g:2 * g + 2, :], ps.rearrange("p (b s) -> p b s", s=PAST)).then_inc(tt.free(key), 1)
            elif kind == "lg":
                _, i, c = key
                u = unit_no[(i, c)]
                k = 320 if i == "s" else P * (i + 1)
                heads = [0] if i == "s" else [0, 1]
                if u:
                    prev = ("pt",) + units[u - 1]
                    dve.wait_ge(*tt.full(prev if units[u - 1][0] == "s" else prev + (1,)))
                else:
                    dve.wait_ge(*tt.full(("lnA2", 4)))
                dve.wait_ge(ev("bias_in"), bias_need[(i, c)])
                for n in heads:
                    kk = key if i == "s" else key + (n,)
                    dve.wait_ge(*at.full(kk))
                    if i != "s":
                        done(stt(LP[:, n, 0:k], at.tile(kk)[:, 0:k], HD ** -0.5, BM[:, n, 0:k], ALU.mult, ALU.add))
                    else:
                        done(stt(LP[:, 0, 0:PAST], at.tile(kk)[:, 0:PAST], HD ** -0.5, BM[:, 0, 0:PAST], ALU.mult, ALU.add))
                        by_b = lambda v: v.rearrange("p (b t) -> p b t", t=ST)
                        done(stt(by_b(LP[:, 0, PAST:k]), by_b(at.tile(kk)[:, PAST:k]), HD ** -0.5,
                                 BM[:, 0, PAST:PAST + ST].unsqueeze(1).broadcast_to([P, NB, ST]), ALU.mult, ALU.add))
                    need()
                    dve.sem_inc(at.free(kk), 1)
                    link(dve.tensor_tensor_reduce(out=LP[:, n, 0:k], in0=LP[:, n, 0:k], in1=PEN[i], scale=1.0, scalar=REPL,
                                                  op0=ALU.add, op1=ALU.max, accum_out=NEGM[:, n:n + 1]))
                    ts(NEGM[:, n:n + 1], NEGM[:, n:n + 1], -1.0, None, ALU.mult).then_inc(ev("logits_up"), 1)
                for n in heads:
                    dve.wait_ge(ev("exp_done"), (2 * u + n + 1) if i != "s" else 32 + u - 15)
                    link(dve.reciprocal(RINV[:, n:n + 1], RSUM[:, n:n + 1]))
                    ts(LP[:, n, 0:k], LP[:, n, 0:k], RINV[:, n:n + 1], None, ALU.mult).then_inc(ev("probs_ready"), 1)
            elif kind == "pt":
                _, i, c = key
                u = unit_no[(i, c)]
                if u:
                    dve.wait_ge(*at.full(("pv",) + units[u - 1]))
                else:
                    dve.wait_ge(ev("cv_out"), 16 * 9)
                if i != "s":
                    k = P * (i + 1)
                    for n in range(NKV):
                        kk = key + (n,)
                        dve.wait_ge(*tt.full(kk))
                        dve.tensor_copy(PTT[:, n, 0:k], tt.tile(kk)[:, 0:k]).then_inc(tt.free(kk), 1)
                else:
                    dve.wait_ge(*tt.full(key))
                    done(dve.tensor_copy(PTT[:, 0, 0:256], tt.tile(key)[:, 0:256]))
                    dve.tensor_copy(PTT[0:NS, 0, 256:384], tt.tile(key)[0:NS, 256:384]).then_inc(tt.free(key), 1)
            elif kind == "pv":
                _, i, c = key
                dve.wait_ge(*at.full(key))
                ps = at.tile(key)
                if key == ("pv", 0, 0):
                    dve.wait_ge(ev("v_full"), NT)
                    dve.wait_ge(ev("u_biased"), NT)
                if i != "s":
                    dve.tensor_copy(YT["B"][:, c, i * P:i * P + P], ps[:, 0:P]).then_inc(at.free(key), 1)
                else:
                    done(dve.tensor_copy(YT["B"][0:HD, c, SEQ:NTOK], ps[0:HD, 0:NS]))
                    need()
                    dve.tensor_copy(YT["B"][HD:P, c, SEQ:NTOK], ps[HD:P, NS:P]).then_inc(at.free(key), 1)
                dve.wait_ge(*at.taken(key))
                dve.sem_inc(ev("yb_up"), 1)
                if key == ("pv", "s", NC - 1):
                    prepare_rows()
            elif kind == "wo":
                _, t, h = key
                n = rows_of(t)
                r, x = R[0:n, t % 2, :], XR[0:n, t % 2, :]
                cols = slice(512 * h, 512 * h + 512)
                pick = "p" if t < 4 else "s"
                if h == 0 and t == 0:
                    dve.wait_ge(ev("merged"), 48)
                    link(dve.memset(TH[:, 4, :], 0.0))
                    done(dve.memset(GBUF, BIG))
                    link(dve.memset(SBUF_, BIG))
                if h == 0 and t >= 2:
                    dve.wait_ge(ev("x1_ready"), t - 1)
                tt_(r[:, cols], ps[0:n], BC["g1" + pick][0:n, cols], ALU.mult).then_inc(mm.free(key), 1)
                if h == 1:
                    dve.wait_ge(*mm.taken(("wo", t, 0)))
                    dve.wait_ge(*mm.taken(key))
                    dve.wait_ge(ev(f"xr_in{t % 2}"), 16 * (t // 2 + 1))
                    stt(r, x, ALPHA, r, ALU.mult, ALU.add).then_inc(ev("x_added"), 1)
                    dve.wait_ge(ev("x_added"), t + 1)
                    stats(r, n, D)
                    ts(r, r, MV[0:n, 0:1], RSTD[0:n], ALU.subtract, ALU.mult).then_inc(ev("r_norm"), 1)
                    dve.wait_ge(ev("r_norm"), t + 1)
                    h2 = H2[0:n, t % 2, :]
                    if t >= 2:
                        dve.wait_ge(ev(f"h2_out{t % 2}"), 16 * (t // 2))
                        dve.wait_ge(*tt.full(("h2T", t - 2, 1)))
                    link(tt_(h2, r, BC["sc" + pick][0:n], ALU.mult))
                    tt_(h2, h2, BC["sh" + pick][0:n], ALU.add).then_inc(ev("h2_ready"), 1)
            elif kind == "cum":
                place_tokens(ps)
            elif kind == "lst":
                link(dve.tensor_copy(ints[:, I_L:I_L + NHI], ps[:, 0:NHI]))
                dve.sem_inc(tt.free(key), 1)
                dve.sem_inc(ev("list_int"), 1)
                further_tiles()
            if key == ("rt", 4):
                route()

        def result(d, dq, p):
            dve.wait_ge(ev("dn_full"), d + 1)
            if positive(dq):
                dve.wait_ge(ev(f"yo_out{p}"), 16 * dq)
            dve.tensor_copy(YO[0:TS, p, 512:D], banks[6][0:TS, :]).then_inc(ev("yo_b"), 1)

        def rows_up(e, p):
            dve.wait_ge(ev("gt_full"), e + 1)
            dve.tensor_copy(HG[:, p, 4:8, :], quarter_tiles(banks[3])).then_inc(ev("gt_b"), 1)

        def expert(e, q, dq, p):
            dve.wait_ge(ev("gu_full"), e + 1)
            dve.wait_ge(ev("he_silu"), e + 1)
            tt_(HE[:, p, :], HE[:, p, :], banks[1], ALU.mult).then_inc(ev("he_ready"), 1)
            if type(e) is not int or e < NE - 1:
                rows_up(e + 1, 1 - p)
            if positive(e):
                result(e - 1, dq, 1 - p)
            dve.wait_ge(ev("het_full"), e + 1)
            dve.tensor_copy(HET[:, p, :, 0:TS], quarter_tiles(banks[4])[:, :, 0:TS]).then_inc(ev("het_up"), 1)

        dve.wait_ge(ev("x1_ready"), NT)
        rows_up(0, 0)
        each_expert(dve, expert)
        result(NE - 1, NE // 2 - 1, 1)
        nov = dve.value_load(ints[0:1, I_NOV:I_NOV + 1], min_val=0, max_val=NOV)

        def further(s, i, p):
            rows_up(s + NE, p)
            dve.wait_ge(ev("gu_full"), s + NE + 1)
            dve.wait_ge(ev("he_silu"), s + NE + 1)
            tt_(HE[:, p, :], HE[:, p, :], banks[1], ALU.mult).then_inc(ev("he_ready"), 1)
            dve.wait_ge(ev("het_full"), s + NE + 1)
            dve.tensor_copy(HET[:, p, :, :], quarter_tiles(banks[4])).then_inc(ev("het_up"), 1)
            result(s + NE, i + NE // 2, p)
        each_further(dve, nov, further)
        dve.wait_ge(ev("rows2_in"), 64)
        done(ts(BC2[:, 0, :], BC2[:, 0, :], 1.0, None, ALU.add))
        link(ts(BC2[0:NS, 1, :], BC2[0:NS, 1, :], 1.0, None, ALU.add))
        dve.wait_ge(ev("x1_scaled"), NT)
        for t in range(NT + 1):
            if t < NT:
                n, z = rows_of(t), t % 2
                a, b = GAT[0:n, 2 * t, :], GAT[0:n, 2 * t + 1, :]
                dve.wait_ge(ev(f"pair_in{t}"), 32)
                dve.wait_ge(ev("pair_scaled"), t + 1)
                link(stt(a, b, WGB[0:n, t:t + 1], a, ALU.mult, ALU.add))
                link(tt_(a, a, BC2[0:n, 0 if t < 4 else 1, :], ALU.mult))
                link(tt_(a, a, X1[0:n, t, :], ALU.add))
                for k in range(2):
                    done(dve.bn_stats(STAT[0:n, 6 * k:6 * k + 6], a[:, 512 * k:512 * k + 512]))
                need()
                dve.bn_aggr(MV2[0:n, z, :], STAT[0:n, 0:12]).then_inc(ev("last_var"), 1)
                dve.wait_ge(ev("last_var"), t + 1)
            if t >= 1:
                d = t - 1
                n, z = rows_of(d), d % 2
                a = GAT[0:n, 2 * d, :]
                dve.wait_ge(ev("last_rstd"), d + 1)
                ts(a, a, MV2[0:n, z, 0:1], RSTD2[0:n, z:z + 1], ALU.subtract, ALU.mult).then_inc(ev("o_norm"), 1)

    @block.tensor
    def _(pe):
        def group(out, pairs_):
            for k, (a, b) in enumerate(pairs_):
                last = pe.matmul(out, a, b, start=k == 0, stop=k == len(pairs_) - 1)
            return last

        def flip(out, src):
            return pe.transpose(out, src, ident[0:src.shape[0], 0:src.shape[0]])

        def got(key):
            pe.wait_ge(*arrived_at[key])

        slot8 = lambda key: wslot(key).rearrange("p (k n) -> p k n", k=KT)
        slot4 = lambda key: wslot(key).rearrange("p (k n) -> p k n", k=NJ)
        pe.wait_ge(ev("consts"), 16)
        for key in plan:
            kind = key[0]
            if kind == "tk":
                continue
            ring_of = {"M": mm, "T": tt, "A": at}[kinds[kind]]
            split = kind in ("lg", "pt") and key[1] != "s"
            if not split:
                if ring_of.old(key):
                    pe.wait_ge(*ring_of.room(key))
                ps = ring_of.tile(key)
            if kind == "par":
                pe.wait_ge(ev("small_in"), 16 * 12)
                last = flip(ps[:, 0:NR], PRN[0:NR, :])
            elif kind == "ck":
                pe.wait_ge(ev("convk_in"), 16)
                for j in range(NJ):
                    last = flip(ps[:, j * CW:j * CW + CW], CKN[0:CW, j * P:j * P + P])
            elif kind == "ws":
                pe.wait_ge(ev("ws_in"), 16)
                for g in range(4):
                    last = flip(ps[:, g * P:g * P + P], WSN[:, 4 * key[1] + g, :])
            elif kind == "bd":
                pe.wait_ge(*tt.taken(("ws", 0)))
                pe.wait_ge(*tt.taken(("ws", 1)))
                pe.wait_ge(ev("params_up"), 1)
                e8 = con[0:ST, K_E8:K_E8 + P]
                for g in range(NCG):
                    pe.matmul(ps[:, g * ST:g * ST + ST], e8, WS[0:ST, g, 0:ST], start=True, stop=True)
                last = pe.matmul(ps[:, NCG * ST:NCG * ST + NCG], e8, PAR[0:ST, R_BS:R_BS + NCG], start=True, stop=True)
            elif kind == "st":
                pe.wait_ge(ev("state_in"), 32)
                for j in range(NJ):
                    last = flip(ps[:, j * 120:j * 120 + 120], STN[0:120, key[1], j * P:j * P + P])
            elif kind == "oh":
                pe.wait_ge(ev("table_parts"), 32)
                a, b = (0, 512) if key[1] == 0 else (512, SLEN)
                last = pe.matmul(ps[0:8, 0:b - a], REL[0:NBUCK, :], OH[0:NBUCK, a:b], start=True, stop=True)
            elif kind == "cT":
                pe.wait_ge(ev("c_silu"), 1)
                for k in range(KT):
                    last = flip(ps[:, k * 9:k * 9 + 9], CN[0:9, k * P:k * P + P])
            elif kind == "ada":
                if key[1] == 0:
                    pe.wait_ge(*tt.taken(("cT",)))
                w = slot8(key)
                got(key)
                for k in range(KT):
                    for g in range(4):
                        last = pe.matmul(ps[32 * g:32 * g + 9, 0:P], CT[:, k, :], w[:, k, g * P:g * P + P], start=k == 0, stop=k == KT - 1)
            elif kind == "mT":
                n = key[1]
                pe.wait_ge(ev("mod_row"), n + 1)
                for k in range(4):
                    last = flip(ps[:, k * 9:k * 9 + 9], mod_buf(n)[:, k * P:k * P + P])
            elif kind == "xT":
                f = key[1]
                if f == 0:
                    pe.wait_ge(ev("x_in"), 16 * NT)
                for t in range(4):
                    last = flip(ps[:, t * P:t * P + P], X[:, t, f * P:f * P + P])
            elif kind == "xTs":
                for f in range(KT):
                    last = flip(ps[:, f * NS:f * NS + NS], X[0:NS, 4, f * P:f * P + P])
            elif kind == "fm":
                _, name, j, h = key
                if (name, j, h) == ("ag", 0, 0):
                    for f in range(KT):
                        pe.wait_ge(*tt.taken(("xT", f)))
                    pe.wait_ge(*tt.taken(("xTs",)))
                lk, a = {"a": (("a", 0), j * P), "ag": (("a", 1), j * P), "q": (("q",), j * P), "k": (("k",), 0),
                         "ki": (("k",), P), "qi": (("k",), 2 * P + j * P)}[name]
                got(lk)
                w = slot8(lk)
                last = group(ps[:, 0:HALF], [(w[:, k, a:a + P], HT[:, k, h * HALF:h * HALF + HALF]) for k in range(KT)])
            elif kind == "kv":
                t = key[1]
                n = rows_of(t)
                for x in range(2):
                    pe.wait_ge(*mm.taken(("fm", "k", 0, x)))
                    pe.wait_ge(*mm.taken(("fm", "ki", 0, x)))
                flip(ps[0:n, 0:P], KTT[:, t * P:t * P + n])
                last = flip(ps[0:n, P:192], KIT[0:HD, t * P:t * P + n])
            elif kind == "cvp":
                pe.wait_ge(ev("glu_up"), 2 * NJ)
                for j in range(NJ):
                    last = flip(ps[0:CW - 1, j * P:j * P + P], AES[:, j, SEQ:SEQ + CW - 1])
            elif kind == "cvs":
                pe.wait_ge(ev("cvs_staged"), 1)
                for j in range(NJ):
                    last = flip(ps[0:NS, j * P:j * P + P], CVS[:, j, :])
            elif kind == "nat":
                _, what, t = key
                if what == "w":
                    pe.wait_ge(ev("w132_in"), 32)
                    last = group(ps[:, 0:NW], [(HT[:, k, t * P:t * P + P], W1[:, k, :]) for k in range(KT)])
                else:
                    got((what,))
                    w = slot8((what,))
                    last = group(ps, [(HT[:, k, t * P:t * P + P], w[:, k, :]) for k in range(KT)])
            elif kind == "lnA1":
                t = key[1]
                pe.wait_ge(ev("conv_done"), 1)
                for j in range(NJ):
                    last = flip(ps[0:rows_of(t), j * P:j * P + P], ACC[:, j, t * P:t * P + rows_of(t)])
            elif kind == "lnA2":
                t = key[1]
                n = rows_of(t)
                pe.wait_ge(*tt.taken(("lnA1", t)))
                for j in range(NJ):
                    last = flip(ps[:, j * P:j * P + n], LP[0:n, t % 2, j * P:j * P + P])
            elif kind == "mix":
                t = key[1]
                pe.wait_ge(ev("v_full"), t + 1)
                for g in range(NCG):
                    v = VN[0:rows_of(t), t, g * HD:g * HD + HD]
                    w = WS[:, g, :] if t < 4 else BD[0:NS, g, :, :].rearrange("p b t -> p (b t)")
                    last = pe.matmul(ps[0:rows_of(t), g * HD:g * HD + HD], w, v, start=True, stop=True)
            elif kind == "yc":
                t = key[1]
                n = rows_of(t)
                pe.wait_ge(ev("sgu_up"), t + 1)
                for j in range(NJ):
                    last = flip(ps[:, j * P:j * P + n], UN[0:n, t, j * P:j * P + P])
            elif kind == "dots":
                _, i, h = key
                r = slice((h % 2) * HD, (h % 2) * HD + HD)
                if (i, h) == (1, 0):
                    for x in range(2):
                        for j in range(2):
                            pe.wait_ge(*mm.taken(("fm", "qi", j, x)))
                if i != "s":
                    last = pe.matmul(ps[:, 0:P * (i + 1)], QIT[r, h // 2, i * P:i * P + P], KIT[r, 0:P * (i + 1)], start=True, stop=True)
                else:
                    if h == 0:
                        pe.wait_ge(ev("qim_ready"), 1)
                        pe.wait_ge(*tt.taken(("kit", 2)))
                        pe.wait_ge(*tt.taken(("kit", 3)))
                    group(ps[:, 0:PAST], [(QIM[r, h // 2, b, :], KTS[r, b, :]) for b in range(NB)])
                    last = pe.matmul(ps[:, PAST:PAST + NS], QI2[r, h // 2, :], KIT[r, SEQ:NTOK], start=True, stop=True)
            elif kind in ("kit", "kts"):
                g = key[1]
                if g == 0:
                    pe.wait_ge(ev("pages_in" if kind == "kit" else "kpages_in"), 16 * 16 * (2 if kind == "kit" else 1))
                for z in range(4):
                    last = flip(ps[:, z * P:z * P + P], KP[:, 4 * g + z, :])
            elif kind == "lg":
                _, i, c = key
                if i != "s":
                    if (i, c) == (0, 0):
                        for x in range(2):
                            for c2 in range(NC):
                                pe.wait_ge(*mm.taken(("fm", "q", c2, x)))
                    for n in range(NKV):
                        kk = key + (n,)
                        if at.old(kk):
                            pe.wait_ge(*at.room(kk))
                        r = slice(n * HD, n * HD + HD)
                        last = pe.matmul(at.tile(kk)[:, 0:P * (i + 1)], QT[r, c, i * P:i * P + P], KTT[r, 0:P * (i + 1)], start=True, stop=True)
                        last.then_inc(at.full_sem, 1)
                else:
                    q, qn = QMN[c % 2]
                    pe.wait_ge(ev("qm_ready"), c + 1)
                    if c == 0:
                        pe.wait_ge(*tt.taken(("kts", 2)))
                        pe.wait_ge(*tt.taken(("kts", 3)))
                    group(ps[:, 0:PAST], [(q[:, b, :], KTS[:, b, :]) for b in range(NB)])
                    last = pe.matmul(ps[:, PAST:PAST + NS], qn, KTT[:, SEQ:NTOK], start=True, stop=True)
            elif kind == "pt":
                _, i, c = key
                u = unit_no[(i, c)]
                if i != "s":
                    for n in range(NKV):
                        kk = key + (n,)
                        if tt.old(kk):
                            pe.wait_ge(*tt.room(kk))
                        pe.wait_ge(ev("probs_ready"), 2 * u + n + 1)
                        for k in range(i + 1):
                            last = flip(tt.tile(kk)[:, k * P:k * P + P], LP[:, n, k * P:k * P + P])
                        last.then_inc(tt.full_sem, 1)
                else:
                    pe.wait_ge(ev("probs_ready"), 32 + u - 15)
                    flip(ps[:, 0:P], LP[:, 0, 0:P])
                    flip(ps[:, P:2 * P], LP[:, 0, P:2 * P])
                    last = flip(ps[0:NS, 2 * P:3 * P], LP[:, 0, 2 * P:2 * P + NS])
            elif kind == "pv":
                _, i, c = key
                if i != "s":
                    for n in range(NKV):
                        pe.wait_ge(*tt.taken(("pt", i, c, n)))
                    if (i, c) == (0, 0):
                        pe.wait_ge(ev("w_biased"), NT)
                    for n in range(NKV):
                        last = group(ps[n * HD:n * HD + HD, 0:P],
                                     [(VA[:, k, n * HD:n * HD + HD], PTT[:, n, k * P:k * P + P]) for k in range(i + 1)])
                else:
                    pe.wait_ge(*tt.taken(("pt", i, c)))
                    pe.matmul(ps[:, 0:P], VA[0:NS, 4, :], PTT[0:NS, 0, 256:384], start=True, stop=False)
                    out4 = ps[:, 0:P].rearrange("p (n b t) -> p n b t", n=NKV, b=NB)
                    for b in range(NB):
                        for k in range(NPG):
                            pt4 = PTT[:, 0, k * P:k * P + P].rearrange("p (n b t) -> p n b t", n=NKV, b=NB)
                            last = pe.matmul(out4[:, :, b, :], VP[:, NPG * b + k, :], pt4[:, :, b, :], start=False, stop=(b, k) == (NB - 1, NPG - 1))
            elif kind == "gate":
                _, x, f, h = key
                lk = ("g", x, f // 4)
                got(lk)
                w = slot8(lk)
                a = (f % 4) * P
                last = group(ps[:, 0:HALF], [(w[:, k, a:a + P], HT[:, k, h * HALF:h * HALF + HALF]) for k in range(KT)])
            elif kind == "proj":
                _, x, f, h = key
                got(("p", x))
                if (f, h) == (0, 0):
                    if x == "A":
                        for t in (3, 4):
                            pe.wait_ge(*tt.taken(("lnA2", t)))
                    elif x == "C":
                        pe.wait_ge(ev("yct_up"), NT)
                    else:
                        pe.wait_ge(ev("yb_up"), 20)
                w = slot4(("p", x))
                last = group(ps[:, 0:HALF], [(w[:, k, f * P:f * P + P], YT[x][:, k, h * HALF:h * HALF + HALF]) for k in range(NJ)])
            elif kind == "wo":
                _, t, h = key
                n = rows_of(t)
                pe.wait_ge(ev("merged"), 48)
                got(("wo", h))
                w = slot8(("wo", h))
                last = group(ps[0:n], [(MG[:, k, t * P:t * P + n], w[:, k, :]) for k in range(KT)])
            elif kind == "h2T":
                _, t, h = key
                n = rows_of(t)
                pe.wait_ge(ev("h2_ready"), t + 1)
                for k in range(4):
                    last = flip(ps[:, k * P:k * P + n], H2[0:n, t % 2, (4 * h + k) * P:(4 * h + k + 1) * P])
            elif kind == "rt":
                t = key[1]
                n = rows_of(t)
                pe.wait_ge(ev("router_in"), 48)
                for h in range(2):
                    pe.wait_ge(*tt.taken(("h2T", t, h)))
                last = group(ps[0:n, 0:NE], [(H2T[:, k, 0:n], WRT[:, k, :]) for k in range(KT)])
            elif kind == "cum":
                pe.wait_ge(ev("mask_ready"), 1)
                for t in range(NT):
                    n = rows_of(t)
                    out = ps[0:n, t * NE:t * NE + NE]
                    group(out, [(ones[:, 0:n], MSK[:, s_, :]) for s_ in range(t)] + [(tri[0:n, 0:n], MSK[0:n, t, :])])
                last = group(ps[:, NT * NE:(NT + 1) * NE],
                             [(ones[0:rows_of(t)], MSK[0:rows_of(t), t, :]) for t in range(NT)])
            elif kind == "lst":
                pe.wait_ge(ev("slots_ready"), 1)
                last = group(ps[:, 0:NHI], [(OHL[0:rows_of(t), NT * c + t, :], OHH[0:rows_of(t), NT * c + t, :]) for c in range(2) for t in range(NT)])
            if not split:
                last.then_inc(ring_of.full_sem, 1)
            for lk in released:
                if last_use[lk] == pos[key]:
                    pe.wait_ge(ring_of.full_sem, ring_of.at[key] + 1)
                    pe.sem_inc(slot_out, 1)

        def gathered(e_next, q, p):
            pe.wait_ge(ev(f"rows_gathered{p}"), 16 * q + 16)
            if positive(e_next):
                pe.wait_ge(ev("gt_a"), e_next)
                pe.wait_ge(ev("gt_b"), e_next)
            for k in range(KT):
                last = pe.transpose(banks[2 + k // 4][:, (k % 4) * P:(k % 4) * P + TS], G[0:TS, p, k * P:k * P + P], ident[0:TS, 0:TS])
            last.then_inc(ev("gt_full"), 1)

        def down(d, dq, p):
            pe.wait_ge(ev("het_up"), d + 1)
            pe.wait_ge(ev(f"w_in{3 * p + 2}"), 16 * dq + 16)
            if positive(d):
                pe.wait_ge(ev("yo_a"), d)
                pe.wait_ge(ev("yo_b"), d)
            w = ring[3 * p + 2].rearrange("p (k n) -> p k n", k=NJ)
            group(banks[5][0:TS, :], [(HET[:, p, k, 0:TS], w[:, k, 0:512]) for k in range(NJ)])
            group(banks[6][0:TS, :], [(HET[:, p, k, 0:TS], w[:, k, 512:D]) for k in range(NJ)]).then_inc(ev("dn_full"), 1)
            pe.wait_ge(ev("dn_full"), d + 1)
            pe.sem_inc(ev(f"w_used{3 * p + 2}"), 1)

        def hidden(e, q, p):
            pe.wait_ge(ev("gt_a"), e + 1)
            pe.wait_ge(ev("gt_b"), e + 1)
            wg, wu = (ring[3 * p + z].rearrange("p (k n) -> p k n", k=KT) for z in range(2))
            if positive(e):
                pe.wait_ge(ev("he_ready"), e)
            pe.wait_ge(ev(f"w_in{3 * p}"), 16 * q + 16)
            group(banks[0], [(HG[:, p, k, :], wg[:, k, :]) for k in range(KT)]).then_inc(ev(f"w_used{3 * p}"), 1)
            pe.wait_ge(ev(f"w_in{3 * p + 1}"), 16 * q + 16)
            group(banks[1], [(HG[:, p, k, :], wu[:, k, :]) for k in range(KT)]).then_inc(ev("gu_full"), 1)
            pe.wait_ge(ev("gu_full"), e + 1)
            pe.sem_inc(ev(f"w_used{3 * p + 1}"), 1)

        def hidden_flip(e, p):
            pe.wait_ge(ev("he_ready"), e + 1)
            for k in range(NJ):
                last = pe.transpose(banks[4][:, k * P:k * P + TS], HE[:, p, k * P:k * P + P], ident)
            last.then_inc(ev("het_full"), 1)

        def expert(e, q, dq, p):
            hidden(e, q, p)
            if type(e) is not int or e < NE - 1:
                gathered(e + 1, q + p, 1 - p)
            if positive(e):
                down(e - 1, dq, 1 - p)
            hidden_flip(e, p)

        gathered(0, 0, 0)
        each_expert(pe, expert)
        down(NE - 1, NE // 2 - 1, 1)
        nov = pe.value_load(ints[0:1, I_NOV:I_NOV + 1], min_val=0, max_val=NOV)

        def further(s, i, p):
            gathered(s + NE, i + NE // 2, p)
            hidden(s + NE, i + NE // 2, p)
            hidden_flip(s + NE, p)
            down(s + NE, i + NE // 2, p)
        each_further(pe, nov, further)


def buckets():
    n = np.maximum(TABLE_END - np.arange(SLEN), 0)
    exact = NBUCK // 2
    nf = np.maximum(n, 1).astype(np.float32)
    large = exact + (np.log(nf / np.float32(exact)) / np.float32(math.log(MAXD / exact)) * (NBUCK - exact)).astype(np.int32)
    b = np.where(n < exact, n, np.minimum(large, NBUCK - 1))
    return (np.arange(NBUCK)[:, None] == b[None, :]).astype(np.float32)


def constants():
    c = np.zeros((P, K_ALL), np.float32)
    p, f = np.arange(P)[:, None], np.arange(P)[None, :]
    c[:, K_ID:K_ID + P] = p == f
    c[:, K_PEN:K_PEN + P] = np.where(f <= p, 0.0, NEG)
    c[:, K_TRI:K_TRI + P] = p <= f
    c[:, K_ONE:K_ONE + P] = 1.0
    row, col = p % NS, np.arange(NS)[None, :]
    c[:, K_PENS:K_PENS + NS] = np.where((row // ST == col // ST) & (col <= row), 0.0, NEG)
    c[0:ST, K_E8:K_E8 + P] = np.arange(ST)[:, None] == f % ST
    c[:, K_BLK:K_BLK + NB] = row // ST == np.arange(NB)[None, :]
    c[:, K_SLOT:K_SLOT + NE] = np.arange(NE)[None, :] * TS - 1.0
    c[:, K_TOK:K_TOK + NT] = p + P * np.arange(NT)[None, :]
    c[:, K_STEP:K_STEP + NOV] = np.arange(NOV)[None, :]
    c[:, K_N + R_LT:K_N + R_THR] = (np.arange(NE)[:, None] > np.arange(NE)[None, :]).reshape(1, -1)
    c[:, K_N + R_THR:K_N + R_HI] = TS * (1 + np.arange(MORE))
    c[:, K_N + R_HI:K_N + R_LO] = TS * np.arange(NHI + 1)
    c[:, K_N + R_LO:] = np.arange(TS) - TS
    return c


INPUTS = ["x_prompt", "x_sample", "cache_k", "cache_v", "cache_kidx", "state_conv", "page_table", "c_prompt", "c_sample",
          "w_ada", "b_ada", "w_in", "b_in", "conv_k", "conv_b", "lnA_g", "lnA_b", "lnC_g", "lnC_b", "w_s", "b_s",
          "w_pa", "w_pb", "w_pc", "w_o", "ln1_g", "ln1_b", "ln2_g", "ln2_b", "rel_table", "w_router", "router_bias",
          "w_e_gate", "w_e_up", "w_e_down"]
OUTPUTS = [("y_prompt", (1, SEQ, D)), ("y_sample", (NB, ST, D)),
           ("new_k_prompt", (1, 1, SEQ, NKV, HD)), ("new_v_prompt", (1, 1, SEQ, NKV, HD)), ("new_kidx_prompt", (1, 1, SEQ, HD)),
           ("new_conv_prompt", (1, 1, CW - 1, DA)),
           ("new_k_sample", (1, NB, ST, NKV, HD)), ("new_v_sample", (1, NB, ST, NKV, HD)), ("new_kidx_sample", (1, NB, ST, HD)),
           ("new_conv_sample", (1, NB, CW - 1, DA)), ("new_vchunk_sample", (1, NB, ST, 512))]


def kernel(**inputs):
    import concourse.bacc as bacc
    from concourse.bass_utils import run_bass_kernel_spmd

    nc = bacc.Bacc("TRN2", target_bir_lowering=False, num_devices=1)
    arrays, I, O = {}, {}, {}
    for name in INPUTS:
        a = np.ascontiguousarray(inputs[name])
        if name == "router_bias":
            a = a.reshape(1, -1)
        arrays["in_" + name] = a
        I[name] = nc.dram_tensor("in_" + name, a.shape, mybir.dt.from_np(a.dtype), kind="ExternalInput").ap()
    for name, a in (("constants", constants()), ("buckets", buckets())):
        arrays[name] = a
        I[name] = nc.dram_tensor(name, a.shape, F32, kind="ExternalInput").ap()
    for name, shape in OUTPUTS:
        O[name] = nc.dram_tensor(name, shape, F32, kind="ExternalOutput").ap()
    build(nc, I, O, I["constants"], I["buckets"])
    r = run_bass_kernel_spmd(nc, [arrays], core_ids=[0])
    return tuple(r.results[0][name] for name, _ in OUTPUTS)
```
